# Optimizing a Trainium2 kernel written in Bass

```python
import math
import jax, jax.numpy as jnp
from jax import lax
import numpy as np

D_MODEL = 1024
BATCH = 1
SEQ = 512
DEPTH = 2

NSA_HEADS = 8
NSA_KV_GROUPS = 2
NSA_HPG = NSA_HEADS // NSA_KV_GROUPS
NSA_HEAD_DIM = 64
N_BRANCH = 3
CMP_BLOCK = 32
CMP_STRIDE = 16
CMP_HIDDEN = 256
SLC_BLOCK = 64
SLC_TOP_N = 16
WINDOW = 512
NSA_Q_BLOCK = 64
ROPE_THETA = 500000.0
ROPE_DIM = NSA_HEAD_DIM // 4

GDN_HEADS = 4
GDN_HEAD_DIM = 128
GDN_CONV = 4
GDN_CHUNK = 64

NSA_WIDTH = NSA_HEADS * NSA_HEAD_DIM
GDN_WIDTH = GDN_HEADS * GDN_HEAD_DIM
MIX_WIDTH = NSA_WIDTH + GDN_WIDTH
NSA_KV_WIDTH = N_BRANCH * 2 * NSA_KV_GROUPS * NSA_HEAD_DIM
NSA_GATE_WIDTH = NSA_HEADS * N_BRANCH
IN_SPLITS = (NSA_WIDTH, NSA_KV_WIDTH, NSA_GATE_WIDTH, 3 * GDN_WIDTH, GDN_HEADS, GDN_HEADS, GDN_WIDTH)
IN_WIDTH = sum(IN_SPLITS)

D_FF = 2816
FFN_CONV = 3
NORM_EPS = 1e-6

kernel_name = "hybrid_nsa_gdn_convffn_trunk"

def rms_norm(x, gain):
    xf = x.astype(jnp.float32)
    y = xf * lax.rsqrt(jnp.mean(xf * xf, axis=-1, keepdims=True) + NORM_EPS)
    return (y * gain.astype(jnp.float32)).astype(x.dtype)

def l2_norm(x):
    xf = x.astype(jnp.float32)
    return xf * lax.rsqrt(jnp.sum(xf * xf, axis=-1, keepdims=True) + NORM_EPS)

def split_columns(t, sizes):
    bounds = np.cumsum(sizes)[:-1].tolist()
    return jnp.split(t, bounds, axis=-1)

def rope_tables(positions):
    inv = ROPE_THETA ** (-jnp.arange(0, ROPE_DIM, 2, dtype=jnp.float32) / ROPE_DIM)
    ang = positions.astype(jnp.float32)[..., None] * inv
    return jnp.cos(ang), jnp.sin(ang)

def apply_partial_rope(x, cos, sin):
    half = ROPE_DIM // 2
    x1 = x[..., :half].astype(jnp.float32)
    x2 = x[..., half:ROPE_DIM].astype(jnp.float32)
    c = cos[:, :, None, :]
    s = sin[:, :, None, :]
    rot = jnp.concatenate([x1 * c - x2 * s, x2 * c + x1 * s], axis=-1).astype(x.dtype)
    return jnp.concatenate([rot, x[..., ROPE_DIM:]], axis=-1)

def masked_softmax(scores, mask):
    s = jnp.where(mask, scores.astype(jnp.float32), -jnp.inf)
    m = jnp.max(s, axis=-1, keepdims=True)
    m = jnp.where(jnp.isfinite(m), m, 0.0)
    p = jnp.exp(s - m)
    return p / jnp.maximum(jnp.sum(p, axis=-1, keepdims=True), 1e-30)

def causal_dwconv(x, w):
    width, T = w.shape[0], x.shape[1]
    xp = jnp.pad(x, ((0, 0), (width - 1, 0), (0, 0)))
    out = xp[:, 0:T] * w[0]
    for j in range(1, width):
        out = out + xp[:, j:j + T] * w[j]
    return out

def compress_blocks(x, pe, w1, w2):
    B, G, T, DH = x.shape
    n_cmp = (T - CMP_BLOCK) // CMP_STRIDE + 1
    idx = jnp.arange(n_cmp)[:, None] * CMP_STRIDE + jnp.arange(CMP_BLOCK)[None, :]
    blocks = (x[:, :, idx] + pe).reshape(B, G, n_cmp, CMP_BLOCK * DH)
    return jax.nn.silu(blocks @ w1) @ w2

def nsa_mixer(q, kv, gate_logits, cos, sin, q_gain, k_gain, cmp_pe, cmp_w1, cmp_w2, out_gain):
    B, T, _ = q.shape
    dt = q.dtype
    G, HPG, DH = NSA_KV_GROUPS, NSA_HPG, NSA_HEAD_DIM
    q = q.reshape(B, T, NSA_HEADS, DH)
    q = apply_partial_rope(rms_norm(q, q_gain), cos, sin) * (DH ** -0.5)
    q = q.reshape(B, T, G, HPG, DH).transpose(0, 2, 3, 1, 4)
    gates = jax.nn.sigmoid(gate_logits).reshape(B, T, G, HPG, N_BRANCH).transpose(0, 2, 3, 1, 4)
    kv = kv.reshape(B, T, N_BRANCH, 2, G, DH)

    def heads_first(t):
        return t.transpose(0, 2, 1, 3)

    k_cmp = rms_norm(compress_blocks(heads_first(apply_partial_rope(kv[:, :, 0, 0], cos, sin)),
                                     cmp_pe[0], cmp_w1[0], cmp_w2[0]), k_gain[0])
    v_cmp = compress_blocks(heads_first(kv[:, :, 0, 1]), cmp_pe[1], cmp_w1[1], cmp_w2[1])
    k_slc = heads_first(apply_partial_rope(rms_norm(kv[:, :, 1, 0], k_gain[1]), cos, sin))
    v_slc = heads_first(kv[:, :, 1, 1])
    k_win = heads_first(apply_partial_rope(rms_norm(kv[:, :, 2, 0], k_gain[2]), cos, sin))
    v_win = heads_first(kv[:, :, 2, 1])

    n_cmp = k_cmp.shape[2]
    n_slc = T // SLC_BLOCK
    n_top = min(SLC_TOP_N, n_slc)
    cmp_start = jnp.arange(n_cmp) * CMP_STRIDE
    cmp_end = cmp_start + CMP_BLOCK - 1
    slc_start = jnp.arange(n_slc) * SLC_BLOCK
    overlap = ((cmp_start[:, None] < slc_start[None, :] + SLC_BLOCK)
               & (cmp_start[:, None] + CMP_BLOCK > slc_start[None, :])).astype(jnp.float32)
    k_slc_blocks = k_slc.reshape(B, G, n_slc, SLC_BLOCK, DH)
    v_slc_blocks = v_slc.reshape(B, G, n_slc, SLC_BLOCK, DH)
    k_win_pad = jnp.pad(k_win, ((0, 0), (0, 0), (WINDOW, 0), (0, 0)))
    v_win_pad = jnp.pad(v_win, ((0, 0), (0, 0), (WINDOW, 0), (0, 0)))
    b_ix = jnp.arange(B)[:, None, None, None]
    g_ix = jnp.arange(G)[None, :, None, None]
    blk_offsets = jnp.arange(SLC_BLOCK)
    win_offsets = jnp.arange(NSA_Q_BLOCK + WINDOW)

    def block_fn(qb):
        t0 = qb * NSA_Q_BLOCK
        t_idx = t0 + jnp.arange(NSA_Q_BLOCK)
        q_b = lax.dynamic_slice_in_dim(q, t0, NSA_Q_BLOCK, axis=3)
        g_b = lax.dynamic_slice_in_dim(gates, t0, NSA_Q_BLOCK, axis=3)
        p_c = masked_softmax(jnp.einsum('bghqd,bgnd->bghqn', q_b, k_cmp), cmp_end[None, :] <= t_idx[:, None])
        o_c = jnp.einsum('bghqn,bgnd->bghqd', p_c.astype(dt), v_cmp)
        imp = jnp.einsum('bghqn,ns->bgqs', p_c, overlap)
        cur = (t_idx // SLC_BLOCK)[:, None]
        j = jnp.arange(n_slc)[None, :]
        forced = (j == 0) | (j == cur) | (j == cur - 1)
        imp = jnp.where(forced, jnp.inf, jnp.where(j > cur, -jnp.inf, imp))
        _, sel = lax.top_k(imp, n_top)
        k_s = k_slc_blocks[b_ix, g_ix, sel].reshape(B, G, NSA_Q_BLOCK, n_top * SLC_BLOCK, DH)
        v_s = v_slc_blocks[b_ix, g_ix, sel].reshape(B, G, NSA_Q_BLOCK, n_top * SLC_BLOCK, DH)
        pos_s = (sel[..., None] * SLC_BLOCK + blk_offsets).reshape(B, G, NSA_Q_BLOCK, n_top * SLC_BLOCK)
        mask_s = (pos_s <= t_idx[None, None, :, None])[:, :, None]
        p_s = masked_softmax(jnp.einsum('bghqd,bgqkd->bghqk', q_b, k_s), mask_s)
        o_s = jnp.einsum('bghqk,bgqkd->bghqd', p_s.astype(dt), v_s)
        k_w = lax.dynamic_slice_in_dim(k_win_pad, t0, NSA_Q_BLOCK + WINDOW, axis=2)
        v_w = lax.dynamic_slice_in_dim(v_win_pad, t0, NSA_Q_BLOCK + WINDOW, axis=2)
        pos_w = t0 - WINDOW + win_offsets
        rel = t_idx[:, None] - pos_w[None, :]
        mask_w = (rel >= 0) & (rel < WINDOW) & (pos_w[None, :] >= 0)
        p_w = masked_softmax(jnp.einsum('bghqd,bgkd->bghqk', q_b, k_w), mask_w)
        o_w = jnp.einsum('bghqk,bgkd->bghqd', p_w.astype(dt), v_w)
        return g_b[..., 0:1] * o_c + g_b[..., 1:2] * o_s + g_b[..., 2:3] * o_w

    out = lax.map(block_fn, jnp.arange(T // NSA_Q_BLOCK))
    out = out.transpose(1, 0, 4, 2, 3, 5).reshape(B, T, NSA_HEADS, DH)
    return rms_norm(out, out_gain).reshape(B, T, NSA_WIDTH)

def gated_delta_rule_chunked(q, k, v, g, beta):
    B, T, H, DK = q.shape
    DV = v.shape[-1]
    C = GDN_CHUNK
    N = T // C
    f32 = jnp.float32

    def chunks(t):
        return t.astype(f32).reshape(B, N, C, H, -1).transpose(1, 0, 3, 2, 4)

    qc = chunks(q) * (DK ** -0.5)
    kc = chunks(k)
    vc = chunks(v)
    gc = chunks(g[..., None])[..., 0]
    bc = chunks(beta[..., None])[..., 0]
    gcum = jnp.cumsum(gc, axis=-1)
    causal = jnp.tril(jnp.ones((C, C), bool))
    strict = jnp.tril(jnp.ones((C, C), bool), -1)
    decay = jnp.exp(jnp.where(causal, gcum[..., :, None] - gcum[..., None, :], -jnp.inf))
    kb = kc * bc[..., None]
    vb = vc * bc[..., None]
    a_kk = jnp.where(strict, jnp.einsum('nbhid,nbhjd->nbhij', kb, kc) * decay, 0.0)
    eye = jnp.eye(C, dtype=f32)
    t_inv = lax.linalg.triangular_solve(a_kk + eye, jnp.broadcast_to(eye, a_kk.shape),
                                        left_side=True, lower=True, unit_diagonal=True)
    u = jnp.einsum('nbhij,nbhjd->nbhid', t_inv, vb)
    w = jnp.einsum('nbhij,nbhjd->nbhid', t_inv, kb * jnp.exp(gcum)[..., None])
    a_qk = jnp.einsum('nbhid,nbhjd->nbhij', qc, kc) * decay

    def step(S, xs):
        q_i, k_i, u_i, w_i, a_i, g_i = xs
        v_new = u_i - jnp.einsum('bhcd,bhde->bhce', w_i, S)
        o_i = (jnp.einsum('bhcd,bhde->bhce', q_i * jnp.exp(g_i)[..., None], S)
               + jnp.einsum('bhij,bhje->bhie', a_i, v_new))
        g_last = g_i[..., -1]
        S = (S * jnp.exp(g_last)[..., None, None]
             + jnp.einsum('bhcd,bhce->bhde', k_i * jnp.exp(g_last[..., None] - g_i)[..., None], v_new))
        return S, o_i

    S0 = jnp.zeros((B, H, DK, DV), f32)
    _, o = lax.scan(step, S0, (qc, kc, u, w, a_qk, gcum))
    return o.transpose(1, 0, 3, 2, 4).reshape(B, T, H, DV)

def gdn_mixer(qkv, a_in, b_in, z, conv_w, a_log, dt_bias, out_gain):
    B, T, _ = qkv.shape
    dt = qkv.dtype
    qkv = jax.nn.silu(causal_dwconv(qkv, conv_w))
    q, k, v = jnp.split(qkv, 3, axis=-1)
    q = l2_norm(q.reshape(B, T, GDN_HEADS, GDN_HEAD_DIM))
    k = l2_norm(k.reshape(B, T, GDN_HEADS, GDN_HEAD_DIM))
    v = v.reshape(B, T, GDN_HEADS, GDN_HEAD_DIM)
    beta = jax.nn.sigmoid(b_in.astype(jnp.float32))
    g = -jnp.exp(a_log.astype(jnp.float32)) * jax.nn.softplus(a_in.astype(jnp.float32) + dt_bias.astype(jnp.float32))
    o = gated_delta_rule_chunked(q, k, v, g, beta)
    o = rms_norm(o, out_gain) * jax.nn.silu(z.astype(jnp.float32).reshape(B, T, GDN_HEADS, GDN_HEAD_DIM))
    return o.astype(dt).reshape(B, T, GDN_WIDTH)

def conv_glu_ffn(h, w_up, conv_w, conv_b, w_down):
    u = causal_dwconv(h @ w_up, conv_w) + conv_b
    gate, up = jnp.split(u, 2, axis=-1)
    return (jax.nn.silu(gate) * up) @ w_down

def setup_inputs(seed: int = 0) -> dict:
    key = jax.random.key(seed)
    ks = jax.random.split(key, 24)
    f32 = jnp.float32

    def nrm(k, shape, scale):
        return scale * jax.random.normal(k, shape, f32)

    def gain(k, shape):
        return 1.0 + 0.02 * jax.random.normal(k, shape, f32)

    res = (2 * DEPTH) ** -0.5
    dt_init = jnp.exp(jax.random.uniform(ks[12], (DEPTH, GDN_HEADS), f32, math.log(1e-3), math.log(1e-1)))
    positions = (jax.random.randint(ks[1], (BATCH, 1), 0, 1024, jnp.int32)
                 + jnp.arange(SEQ, dtype=jnp.int32)[None, :])
    return {
        "x": nrm(ks[0], (BATCH, SEQ, D_MODEL), 1.0),
        "positions": positions,
        "attn_norm": gain(ks[2], (DEPTH, D_MODEL)),
        "w_in": nrm(ks[3], (DEPTH, D_MODEL, IN_WIDTH), D_MODEL ** -0.5),
        "nsa_q_norm": gain(ks[4], (DEPTH, NSA_HEAD_DIM)),
        "nsa_k_norm": gain(ks[5], (DEPTH, N_BRANCH, NSA_HEAD_DIM)),
        "cmp_pe": nrm(ks[6], (DEPTH, 2, CMP_BLOCK, NSA_HEAD_DIM), 0.1),
        "cmp_w1": nrm(ks[7], (DEPTH, 2, CMP_BLOCK * NSA_HEAD_DIM, CMP_HIDDEN), (CMP_BLOCK * NSA_HEAD_DIM) ** -0.5),
        "cmp_w2": nrm(ks[8], (DEPTH, 2, CMP_HIDDEN, NSA_HEAD_DIM), CMP_HIDDEN ** -0.5),
        "nsa_out_norm": gain(ks[9], (DEPTH, NSA_HEADS, NSA_HEAD_DIM)),
        "gdn_conv_w": nrm(ks[10], (DEPTH, GDN_CONV, 3 * GDN_WIDTH), GDN_CONV ** -0.5),
        "gdn_a_log": jnp.log(jax.random.uniform(ks[11], (DEPTH, GDN_HEADS), f32, 1.0, 16.0)),
        "gdn_dt_bias": dt_init + jnp.log(-jnp.expm1(-dt_init)),
        "gdn_out_norm": gain(ks[13], (DEPTH, GDN_HEAD_DIM)),
        "w_out": nrm(ks[14], (DEPTH, MIX_WIDTH, D_MODEL), res * MIX_WIDTH ** -0.5),
        "ffn_norm": gain(ks[15], (DEPTH, D_MODEL)),
        "w_up": nrm(ks[16], (DEPTH, D_MODEL, 2 * D_FF), D_MODEL ** -0.5),
        "ffn_conv_w": nrm(ks[17], (DEPTH, FFN_CONV, 2 * D_FF), FFN_CONV ** -0.5),
        "ffn_conv_b": nrm(ks[18], (DEPTH, 2 * D_FF), 0.01),
        "w_down": nrm(ks[19], (DEPTH, D_FF, D_MODEL), res * D_FF ** -0.5),
    }

def reference(x, positions, attn_norm, w_in, nsa_q_norm, nsa_k_norm, cmp_pe, cmp_w1, cmp_w2, nsa_out_norm,
              gdn_conv_w, gdn_a_log, gdn_dt_bias, gdn_out_norm, w_out, ffn_norm, w_up, ffn_conv_w,
              ffn_conv_b, w_down):
    cos, sin = rope_tables(positions)
    for l in range(DEPTH):
        h = rms_norm(x, attn_norm[l])
        proj = h @ w_in[l]
        nsa_q, nsa_kv, nsa_g, gdn_qkv, gdn_a, gdn_b, gdn_z = split_columns(proj, IN_SPLITS)
        o_nsa = nsa_mixer(nsa_q, nsa_kv, nsa_g, cos, sin, nsa_q_norm[l], nsa_k_norm[l],
                          cmp_pe[l], cmp_w1[l], cmp_w2[l], nsa_out_norm[l])
        o_gdn = gdn_mixer(gdn_qkv, gdn_a, gdn_b, gdn_z, gdn_conv_w[l], gdn_a_log[l],
                          gdn_dt_bias[l], gdn_out_norm[l])
        x = x + jnp.concatenate([o_nsa, o_gdn], axis=-1) @ w_out[l]
        h = rms_norm(x, ffn_norm[l])
        x = x + conv_glu_ffn(h, w_up[l], ffn_conv_w[l], ffn_conv_b[l], w_down[l])
    return x


_drawn_inputs = setup_inputs


def setup_inputs(seed=0):
    import zlib

    import numpy as np

    out = dict(_drawn_inputs(seed))
    spreads = {}
    factors = {'attn_norm': 3.416,
     'nsa_q_norm': 8.0,
     'nsa_k_norm': 8.0,
     'nsa_out_norm': 17.863,
     'gdn_out_norm': 8.0,
     'ffn_norm': 5.012,
     'ffn_conv_b': 8.0}
    for name, (base, spread) in spreads.items():
        noise = np.random.default_rng([zlib.crc32(name.encode()), seed]).standard_normal(out[name].shape)
        drawn = base * np.exp(spread * noise) if base else spread * noise
        out[name] = __import__('jax').numpy.asarray(drawn.astype(out[name].dtype))
    for name, factor in factors.items():
        out[name] = (out[name] * factor).astype(out[name].dtype)
    return out
```

```python
from contextlib import ExitStack

import concourse.bass as bass
from concourse import mybir

F32 = mybir.dt.float32
F32R = mybir.dt.float32r
BF16 = mybir.dt.bfloat16
I32 = mybir.dt.int32
ALU = mybir.AluOpType
ACT = mybir.ActivationFunctionType
AX = mybir.AxisListType

P = 128
D = 1024
T = 512
TT_ = T // P
KC = D // P
NH, DH, NG = 8, 64, 2
NQ = NH * DH
NKV = 3 * 2 * NG * DH
GH, GD, CH = 4, 128, 64
GW = GH * GD
BLK, STRIDE, HID = 32, 16, 256
FF = 2816
FK = FF // P
EPS = 1e-6
THETA, ROPE = 500000.0, 16
NEG = -1e30
PI = 3.1415925
C_Q, C_KV, C_G, C_QKV, C_AB, C_Z = 0, 512, 1280, 1304, 2840, 2848
PJ_W = NQ + NKV + NH * 3 + 2 * GH
PJ_G, PJ_A, PJ_B = 1280, 1304, 1308

PIECE = 2048
U_GQ, U_GK, U_GV, U_TAIL, U_KV, U_Q, U_Z, U_CK, U_CV, U_O0, U_UP, U_DN = 0, 1, 2, 3, 4, 5, 6, 7, 8, 9, 11, 22
N_UP, N_UNITS = 11, 28
N_PIECES = 2 * N_UNITS - 1
N_ITEMS = TT_ * 2 * NH

SIGNALS = dict(
    even_used=28, odd_used=27, hi_done=N_PIECES, split=N_PIECES, dense_done=3 * 20 + 2,
    squares=2, rstd=2, normed=8, hT_psum=24, h_hi=24, h_ready=24,
    proj_evac=28, gconv=12, gsilu=12, par_psum=1, par_ready=1,
    qk_squares=1, qk_rstd=1, q_ready=1, qkT_psum=6, qkT_ready=6, blkT_psum=2, blk_f32=2, blk_hi=2, blk_ready=2,
    hid_ready=4, cmp2_psum=2, kc_ss=1, kc_rstd=1, kc_ready=1, kcT_psum=1, kcT_ready=1, vc_ready=1,
    cs_psum=4, cs_shift=4, cs_exp=4, cp_ready=4, cpT_psum=4, cpT_ready=4, co_psum=4, o_init=4,
    s_psum=N_ITEMS, negmax=N_ITEMS, p_ready=N_ITEMS, pT_psum=N_ITEMS, pT_ready=N_ITEMS, pv_done=N_ITEMS, o_added=8,
    no_ss=1, no_rstd=1, o_final=1,
    ga_in=1, ga_exp=1, ga_out=1, gcum_psum=1, gcum_exp=1,
    raw_psum=12, raw_ev=4, ss_ready=4, rr_ready=4, forms=4, formsT_psum=16, tt_ready=4, kk_psum=4, dt_exp=4, a_ready=4,
    lt_ready=12, y_psum=12, y_ready=10, p_psum=10, x_ready=12, uw_psum=4, uw_ready=4,
    s_ready=9, sg_ready=8, ws_psum=8, vn_ready=8, su_psum=8, oc_psum=8, og_ready=8, oss=4, orr=4, o_written=4,
    x_added=16, ffn_copied=44, ffn_conv=44, silu_ready=22, g_ready=22,
    g_hi_done=22, g_split=22, g_used=11, down_done=7,
)

LOOK_BACK = ("split", "even_used", "odd_used", "x_added", "ffn_conv")


def pieces():
    return [(u, a) for u in range(N_UNITS) for a in range(2) if (u, a) != (N_UNITS - 1, 1)]


def loads_of(unit):
    return 2 if unit == U_TAIL or U_UP <= unit < U_DN else 1


def trunk(nc, depth, x, positions, attn_norm, w_in, nsa_q_norm, nsa_k_norm, cmp_pe, cmp_w1, cmp_w2, nsa_out_norm,
          gdn_conv_w, gdn_a_log, gdn_dt_bias, gdn_out_norm, w_out, ffn_norm, w_up, ffn_conv_w, ffn_conv_b, w_down, out):
    with ExitStack() as ctx:
        base = (nc.sbuf_base + 31) // 32 * 32
        top = [0]

        def at_word(name, shape, dt, word):
            return nc.alloc_sbuf_tensor_at(name, [P if shape[0] is None else shape[0]] + list(shape[1:]), dt,
                                           offset=base + 4 * word)

        def words(shape, dt=F32):
            n = 1
            for s in shape[1:]:
                n *= s
            return n if dt != BF16 else (n + 1) // 2

        def fixed(name, shape, dt=F32):
            t = at_word(name, shape, dt, top[0])
            top[0] += (words(shape, dt) + 7) // 8 * 8
            return t

        def zone(start, limit):
            pos = [start]

            def place(name, shape, dt=F32):
                t = at_word(name, shape, dt, pos[0])
                pos[0] += (words(shape, dt) + 7) // 8 * 8
                assert pos[0] <= limit, (name, pos[0], limit)
                return t
            return place

        x_res = fixed("x_res", [P, TT_, D])
        raw = fixed("raw", [P, 2, PIECE])
        w_hi = fixed("w_hi", [P, 2, PIECE], F32R)
        w_lo = fixed("w_lo", [P, 2, PIECE], F32R)
        xo = fixed("xo", [P, TT_, D])
        ident = fixed("ident", [P, P])
        ident_bf = fixed("ident_bf", [P, P], BF16)
        causal_bf = fixed("causal_bf", [P, P], BF16)
        ident64 = fixed("ident64", [P, CH])
        upto = fixed("upto", [P, CH])
        sum_upto = fixed("sum_upto", [P, P])
        after = fixed("after", [P, P])
        chunk_rows = fixed("chunk_rows", [P, 2, P])
        level_mask = fixed("level_mask", [P, 6, CH])
        cmp_add = fixed("cmp_add", [P, TT_, 32])
        cmp_mul = fixed("cmp_mul", [P, TT_, 32])
        rope_c = fixed("rope_c", [P, TT_, 16])
        rope_s = fixed("rope_s", [P, TT_, 16])
        minus_half = fixed("minus_half", [P, 64])
        par = fixed("par", [P, 3, P])
        par_bc = fixed("par_bc", [P, 904])
        cmp_w2_sb = fixed("cmp_w2_sb", [P, 2, 2, DH])
        ssum = fixed("ssum", [P, 4])
        rstd = fixed("rstd", [P, 4])
        small = fixed("small", [P, 1024])
        CONV0 = top[0]
        conv_in = fixed("conv_in", [P, 4, 4 + T])
        Z0 = top[0]
        h_hi = at_word("h_hi", [P, KC, T], F32R, Z0)
        h_lo = at_word("h_lo", [P, KC, T], F32R, Z0 + KC * T)
        Z1 = Z0 + 2 * KC * T
        par_rows = at_word("par_rows", [P, 3, P], F32, Z1)
        qkvT = at_word("qkvT", [P, 12, T], F32, Z1)
        pj = at_word("pj", [P, TT_, PJ_W], F32, Z1 + 12 * T)
        g_mlp = at_word("g_mlp", [P, FK, T], F32, Z1)
        Z2 = Z1 + 12 * T + TT_ * PJ_W
        END = (nc.sbuf_usable_end - base) // 4
        late = zone(Z2, END)
        conv_out = late("conv_out", [P, 4, T])
        g_hi = late("g_hi", [P, 2, T], F32R)
        g_lo = late("g_lo", [P, 2, T], F32R)
        low, high = zone(Z0, Z1), zone(Z2 + 4 * T, END)
        qT = low("qT", [P, 4, T])
        kT = low("kT", [P, 2, T])
        blk = low("blk", [P, 16, 64])
        hid = low("hid", [P, 2, 2, 64])
        kcT = low("kcT", [P, NG, 32])
        kc_rows = low("kc_rows", [64, DH])
        kc_sq = low("kc_sq", [64, DH])
        kc_two = low("kc_two", [32, P])
        vc_rows = low("vc_rows", [64, DH])
        vc_diag = low("vc_diag", [P, 4 * DH])
        c_prob = low("c_prob", [P, 2, NH * 32])
        c_probT = low("c_probT", [P, 2, 2 * P])
        o_tmp = low("o_tmp", [P, 2, NQ])
        neg_max = low("neg_max", [P, N_ITEMS])
        row_sum = low("row_sum", [P, N_ITEMS])
        sq_tmp = at_word("sq_tmp", [P, 2, 768], F32, Z2)
        blk_hi = high("blk_hi", [P, 16, 64], F32R)
        blk_lo = high("blk_lo", [P, 16, 64], F32R)
        prob = high("prob", [P, 2, T])
        probT = at_word("probT", [P, 2, T], F32, Z2)
        low, high = zone(Z0, Z1), zone(Z2, END)
        forms_sb = low("forms_sb", [P, 4, GH, GD])
        formsT = low("formsT", [P, 3, GH, P])
        raw_qk = low("raw_qk", [P, 2, GH, GD])
        sq_qk = low("sq_qk", [P, 2, GH, GD])
        kbg = low("kbg", [P, 2, GH, GD])
        vb = low("vb", [P, 2, GH, GD])
        g_upto = low("g_upto", [P, GH, CH])
        decayT = low("decayT", [P, GH, CH])
        u_sb = at_word("u_sb", [P, 2, GH, GD], F32, Z0 + 4 * GW + 3 * GW)
        k_dec = high("k_dec", [P, 2, GH, GD])
        wq = high("wq", [P, 2, GH, 4 * CH])
        akkT = high("akkT", [P, 2 * GH, CH])
        aqkT = high("aqkT", [P, 2 * GH, CH])
        ltT = high("ltT", [P, 2 * GH, CH])
        xi = high("xi", [P, 2 * GH, CH])
        xiT = high("xiT", [P, 2 * GH, CH])
        yy = high("yy", [P, 2 * GH, CH])
        state = high("state", [P, GH, GD])
        scan = zone(CONV0, Z0)
        v_new = scan("v_new", [P, GH, GD])
        og = scan("og", [P, GH, GD])
        og_sq = scan("og_sq", [P, GH, GD])
        state_g = scan("state_g", [P, GH, GD])

        def sm(lo, n, rows=P):
            return small[0:rows, lo:lo + n]
        qk_ss, qk_rs = sm(0, 48), sm(48, 48)
        gy, gn, gE, bE, aE = sm(96, 16), sm(112, 16), sm(128, 96), sm(224, 16), sm(240, 4)
        gdec, beta, gate = sm(256, 16), sm(272, 16), sm(288, 96)
        ex = sm(384, 64)
        g_ss, g_rr, g_sc = sm(448, 8), sm(456, 8), sm(464, 20)
        o_ss, o_rr = sm(488, 4), sm(496, 4)
        c_max, c_sum, c_coef = sm(512, 8), sm(520, 8), sm(528, 8)
        coef = sm(536, 8)
        no_ss, no_rr = sm(544, 32), sm(576, 32)
        kc_ss, kc_rr = sm(608, 1, 64), sm(616, 1, 64)
        q_gain = sm(640, 64)
        ang, turns, wrap = sm(704, 32), sm(736, 32), sm(768, 32)
        inv_freq = sm(800, 8)
        pos_f = sm(808, 4)
        cosang = sm(816, 32)
        pos_i = at_word("pos_i", [P, 4], I32, CONV0 - 8)

        ps = [ctx.enter_context(nc.psum_tensor(f"bank{b}", [P, 512], F32)) for b in range(8)]

        sems = {n: ctx.enter_context(nc.semaphore(n)) for n in SIGNALS}
        const_ready = ctx.enter_context(nc.semaphore("const_ready"))
        rope_ready = ctx.enter_context(nc.semaphore("rope_ready"))
        rope_steps = ctx.enter_context(nc.semaphore("rope_steps"))
        x_loaded = ctx.enter_context(nc.semaphore("x_loaded"))
        pos_loaded = ctx.enter_context(nc.semaphore("pos_loaded"))
        par_loaded = ctx.enter_context(nc.semaphore("par_loaded"))
        bc_loaded = ctx.enter_context(nc.semaphore("bc_loaded"))
        raw_loaded = [ctx.enter_context(nc.semaphore(f"raw_loaded{i}")) for i in range(2)]
        pool_steps, sp_steps, pe_steps = (ctx.enter_context(nc.semaphore(n)) for n in ("pool_steps", "sp_steps", "pe_steps"))
        out_stored = ctx.enter_context(nc.semaphore("out_stored"))

        def sig(l, name, k):
            return sems[name], l * SIGNALS[name] + k + (1 if name in LOOK_BACK else 0)

        def task_done(l, unit, j):
            before = 0
            for u in range(unit):
                before += 1 if u in (U_CK, U_CV) else 3
            if j == (1 if unit in (U_CK, U_CV) else 3):
                return sig(l, "odd_used", unit + 1)
            return sig(l, "dense_done", before + j + 1)

        loads_layer = [sum(loads_of(u) for u, a in pieces() if a == s) for s in range(2)]

        def piece_loaded(l, p):
            u, a = pieces()[p]
            n = sum(loads_of(v) for v, b in pieces() if b == a and v <= u)
            return raw_loaded[a], (l * loads_layer[a] + n) * 16

        def slot_free(l, p):
            u, a = pieces()[p]
            return sig(l, "odd_used" if a else "even_used", u)

        def kt_used(l, k):
            if k % 2 == 0:
                return sig(l, "g_used", k // 2 + 1)
            p = 2 * U_DN + k // 2
            return sig(l, "odd_used" if p % 2 else "even_used", p // 2 + 1)

        def over(ap, axis, n):
            a = ap.unsqueeze(axis)
            shape = list(a.shape)
            shape[axis] = n
            return a.broadcast_to(shape)

        def h4(ap):
            return ap.rearrange("p (h n) -> p h n", h=GH)

        gain_attn, gain_ffn = par[:, 0, 0:8], par[:, 0, 8:16]
        gdn_taps = par[:, 0, 16:64].rearrange("p (j c) -> p j c", j=4)
        ffn_bias = par[:, 0, 64:108]
        ffn_taps01 = par[:, 1, 0:88].rearrange("p (j c) -> p j c", j=2)
        ffn_tap2 = par[:, 2, 0:44]
        pe_kv = par[:, 2, 44:76].rearrange("p (v m) -> p v m", v=2)
        bc_q, bc_k = par_bc[:, 0:64], par_bc[:, 64:256].rearrange("p (b d) -> p b d", b=3)
        bc_no, bc_go = par_bc[:, 256:768], par_bc[:, 768:896]
        bc_al, bc_dt = par_bc[:, 896:900], par_bc[:, 900:904]

        block = ctx.enter_context(nc.Block())

        @block.sync
        def _(sp):
            for t in range(TT_):
                sp.dma_start(x_res[:, t, :], x[0, t * P:(t + 1) * P, :]).then_inc(x_loaded, 16)
            with nc.allow_non_contiguous_dma(reason="512 positions"):
                sp.dma_start(pos_i[:, :], positions[0].rearrange("(t p) -> p t", p=P)).then_inc(pos_loaded, 16)
            with sp.Fori(0, depth) as l:

                def load(p):
                    u, a = pieces()[p]
                    if p >= 2:
                        sp.wait_ge(*sig(l, "split", p - 1))
                    else:
                        sp.wait_ge(*sig(l, "split", 0))
                    sp.sem_inc(sp_steps, 1)
                    dst = raw[:, a, :]
                    if u in (U_GQ, U_GK, U_GV, U_KV, U_Q, U_Z):
                        col = {U_GQ: C_QKV, U_GK: C_QKV + GW, U_GV: C_QKV + 2 * GW, U_KV: C_KV, U_Q: C_Q, U_Z: C_Z}[u]
                        src = w_in[l].rearrange("(k p) n -> p k n", p=P)
                        parts = [(dst.rearrange("p (k n) -> p k n", k=4), src[:, 4 * a:4 * a + 4, col:col + 512])]
                    elif u == U_TAIL:
                        d = dst[:, 0:4 * 288].rearrange("p (k n) -> p k n", k=4)
                        src = w_in[l].rearrange("(k p) n -> p k n", p=P)[:, 4 * a:4 * a + 4, :]
                        parts = [(d[:, :, 0:280], src[:, :, 1024:1304]), (d[:, :, 280:288], src[:, :, C_AB:C_AB + 8])]
                    elif u in (U_CK, U_CV):
                        src = cmp_w1[l, u - U_CK].rearrange("(m p) n -> p m n", p=P)
                        parts = [(dst.rearrange("p (m n) -> p m n", m=8), src[:, 8 * a:8 * a + 8, :])]
                    elif u < U_UP:
                        c = (u - U_O0) * 512
                        src = w_out[l].rearrange("(k p) n -> p k n", p=P)
                        parts = [(dst.rearrange("p (k n) -> p k n", k=4), src[:, 4 * a:4 * a + 4, c:c + 512])]
                    elif u < U_DN:
                        c = (u - U_UP) * 256
                        src = w_up[l].rearrange("(k p) n -> p k n", p=P)[:, 4 * a:4 * a + 4, :]
                        d = dst.rearrange("p (k s n) -> p k s n", k=4, s=2)
                        parts = [(d[:, :, s, :], src[:, :, s * FF + c:s * FF + c + 256]) for s in range(2)]
                    else:
                        k = 4 * (u - U_DN) + 2 * a
                        src = w_down[l].rearrange("(k p) n -> p k n", p=P)
                        parts = [(dst.rearrange("p (k n) -> p k n", k=2), src[:, k:k + 2, :])]
                    assert len(parts) == loads_of(u)
                    for d, s in parts:
                        sp.dma_start(d, s).then_inc(raw_loaded[a], 16)

                load(0)
                load(1)
                sp.wait_ge(*sig(l, "x_added", 0))
                sp.sem_inc(sp_steps, 1)
                rows = [(0, 0, 8, attn_norm[l].rearrange("(r c) -> r c", c=P)),
                        (0, 8, 8, ffn_norm[l].rearrange("(r c) -> r c", c=P)),
                        (0, 16, 48, gdn_conv_w[l].rearrange("j (r c) -> (j r) c", c=P)),
                        (0, 64, 44, ffn_conv_b[l].rearrange("(r c) -> r c", c=P)),
                        (1, 0, 88, ffn_conv_w[l, 0:2].rearrange("j (r c) -> (j r) c", c=P)),
                        (2, 0, 44, ffn_conv_w[l, 2].rearrange("(r c) -> r c", c=P)),
                        (2, 44, 32, cmp_pe[l].rearrange("v (m s) d -> (v m) (s d)", s=2))]
                for b, r0, n, src in rows:
                    sp.dma_start(par_rows[r0:r0 + n, b, :], src).then_inc(par_loaded, 16)
                vecs = [(0, 64, nsa_q_norm[l]), (64, 192, nsa_k_norm[l].rearrange("b d -> (b d)")),
                        (256, 512, nsa_out_norm[l].rearrange("h d -> (h d)")), (768, 128, gdn_out_norm[l]),
                        (896, 4, gdn_a_log[l]), (900, 4, gdn_dt_bias[l])]
                for c, n, src in vecs:
                    sp.dma_start(par_bc[:, c:c + n], src.partition_broadcast(P)).then_inc(bc_loaded, 16)
                sp.dma_start(cmp_w2_sb[:, :, :, :], cmp_w2[l].rearrange("v (s p) d -> p v s d", p=P)).then_inc(bc_loaded, 16)
                for p in range(2, N_PIECES):
                    load(p)
            for t in range(TT_):
                sp.wait_ge(*sig(depth - 1, "x_added", 8 + 2 * t + 2))
                sp.dma_start(out[0, t * P:(t + 1) * P, :], x_res[:, t, :]).then_inc(out_stored, 16)
            sp.wait_ge(out_stored, 16 * TT_)

        N_PAR, N_BC = 7 * 16, 7 * 16

        @block.gpsimd
        def _(pool):
            for name in LOOK_BACK:
                pool.sem_inc(sems[name], 1)
            for t, v in ((ident, 0.0), (ident64, 0.0), (upto, 1.0), (sum_upto, 0.0), (after, 0.0), (chunk_rows, 0.0),
                         (level_mask, 0.0), (cmp_add, 0.0), (cmp_mul, 1.0), (minus_half, -0.5), (causal_bf, 0.0)):
                pool.memset(t[:], v)
            for i in range(ROPE // 2):
                pool.memset(inv_freq[:, i:i + 1], THETA ** (-2.0 * i / ROPE))
            pool.drain()
            pool.affine_select(out=ident[:, :], in_=ident[:, :], compare_op=ALU.not_equal, fill=1.0, base=0,
                               pattern=[[-1, P]], channel_multiplier=1)
            pool.affine_select(out=causal_bf[:, :], in_=causal_bf[:, :], compare_op=ALU.is_ge, fill=NEG, base=0,
                               pattern=[[-1, P]], channel_multiplier=1)
            for m, v in ((cmp_add, NEG), (cmp_mul, 0.0)):
                pool.affine_select(out=m[:, :, :], in_=m[:, :, :], compare_op=ALU.is_ge, fill=v, base=-(BLK - 1),
                                   pattern=[[P, TT_], [-STRIDE, 32]], channel_multiplier=1)
            for c in range(2):
                r = slice(CH * c, CH * c + CH)
                pool.drain()
                pool.affine_select(out=ident64[r, :], in_=ident64[r, :], compare_op=ALU.not_equal, fill=1.0, base=0,
                                   pattern=[[-1, CH]], channel_multiplier=1)
                pool.affine_select(out=upto[r, :], in_=upto[r, :], compare_op=ALU.is_ge, fill=0.0, base=0,
                                   pattern=[[1, CH]], channel_multiplier=-1)
                pool.memset(sum_upto[r, r], 1.0)
                pool.memset(after[r, r], 1.0)
                pool.memset(chunk_rows[r, c, :], 1.0)
                for k in range(6):
                    s = 1 << k
                    upper = level_mask[r, k, :].rearrange("p (b u s) -> p b u s", u=2, s=s)[:, :, 1, :]
                    pool.memset(upper, 1.0)
            for c in range(2):
                r = slice(CH * c, CH * c + CH)
                pool.drain()
                pool.affine_select(out=sum_upto[r, r], in_=sum_upto[r, r], compare_op=ALU.is_ge, fill=0.0, base=0,
                                   pattern=[[1, CH]], channel_multiplier=-1)
                pool.affine_select(out=after[r, r], in_=after[r, r], compare_op=ALU.is_ge, fill=0.0, base=-1,
                                   pattern=[[-1, CH]], channel_multiplier=1)
                for k in range(6):
                    s = 1 << k
                    upper = level_mask[r, k, :].rearrange("p (b u s) -> p b u s", u=2, s=s)[:, :, 1, :]
                    pool.affine_select(out=upper, in_=upper, compare_op=ALU.is_ge, fill=0.0, base=0,
                                       pattern=[[-2 * s, CH // (2 * s)], [0, s]], channel_multiplier=1)
            for c in range(2):
                r = slice(CH * c, CH * c + CH)
                pool.drain()
                for k in range(6):
                    s = 1 << k
                    upper = level_mask[r, k, :].rearrange("p (b u s) -> p b u s", u=2, s=s)[:, :, 1, :]
                    pool.affine_select(out=upper, in_=upper, compare_op=ALU.is_ge, fill=0.0, base=s - 1,
                                       pattern=[[2 * s, CH // (2 * s)], [0, s]], channel_multiplier=-1)
            pool.drain()
            pool.tensor_copy(ident_bf[:, :], ident[:, :])
            pool.drain().then_inc(const_ready, 1)

            def inverse_root(dst, src, n, rows, scale, done):
                pool.sem_inc(pool_steps, 1)
                pool.tensor_scalar(src, src, scale, EPS, ALU.mult, ALU.add)
                pool.drain()
                pool.tensor_tensor(dst, src, minus_half[0:rows, 0:n], ALU.pow).then_inc(sems[done], 1)

            with pool.Fori(0, depth) as l:
                pool.wait_ge(*sig(l, "squares", 1))
                inverse_root(rstd[:, :], ssum[:, :], 4, P, 1.0 / D, "rstd")
                pool.wait_ge(*sig(l, "qk_squares", 1))
                inverse_root(qk_rs, qk_ss, 48, P, 1.0 / DH, "qk_rstd")
                pool.wait_ge(*sig(l, "kc_ss", 1))
                inverse_root(kc_rr, kc_ss, 1, 64, 1.0 / DH, "kc_rstd")
                pool.wait_ge(*sig(l, "no_ss", 1))
                inverse_root(no_rr, no_ss, 32, P, 1.0 / DH, "no_rstd")
                for b in range(2):
                    for r in (2 * b, 2 * b + 1):
                        pool.wait_ge(*sig(l, "ss_ready", r + 1))
                        inverse_root(g_rr, g_ss, 8, P, 1.0, "rr_ready")
                    for n in range(4 * b, 4 * b + 4):
                        r, c = n // 2, n % 2
                        pool.wait_ge(*sig(l, "s_ready", n + 1))
                        whole = ex[:, 32 + 16 * c + 4 * r:32 + 16 * c + 4 * r + 4]
                        if n == 0:
                            pool.wait_ge(*sig(l, "gcum_exp", 1))
                        pool.tensor_tensor(state_g[:, :, :], state[:, :, :], over(whole, 2, GD),
                                           ALU.mult).then_inc(sems["sg_ready"], 1)
                        if n % 2 == 1:
                            pool.wait_ge(*sig(l, "oss", r + 1))
                            inverse_root(o_rr, o_ss, 4, P, 1.0 / GD, "orr")
                pool.wait_ge(*sig(l, "squares", 2))
                inverse_root(rstd[:, :], ssum[:, :], 4, P, 1.0 / D, "rstd")

        @block.scalar
        def _(act):
            act.wait_ge(rope_steps, 1)
            act.activation(ang, ang, ACT.Sin)
            act.activation(cosang, cosang, ACT.Sin)
            act.drain().then_inc(rope_ready, 1)
            with act.Fori(0, depth) as l:

                def split_hi(p):
                    if p >= N_PIECES:
                        return
                    act.wait_ge(*piece_loaded(l, p))
                    act.wait_ge(*slot_free(l, p))
                    n = 4 * 288 if p // 2 == U_TAIL else PIECE
                    act.activation(w_hi[:, p % 2, 0:n], raw[:, p % 2, 0:n], ACT.Copy).then_inc(sems["hi_done"], 1)

                def row_squares():
                    for t in range(TT_):
                        act.activation(xo[:, t, :], x_res[:, t, :], ACT.Square, accum_out=ssum[:, t:t + 1])
                    act.drain().then_inc(sems["squares"], 1)

                def h_round(which, gain):
                    for kc in range(KC):
                        act.wait_ge(*sig(l, "hT_psum", 8 * which + kc + 1))
                        if gain is None:
                            act.activation(h_hi[:, kc, :], ps[kc % 4][:, :], ACT.Copy).then_inc(sems["h_hi"], 1)
                        else:
                            act.activation(h_hi[:, kc, :], ps[kc % 4][:, :], ACT.Copy,
                                           scale=gain[:, kc:kc + 1]).then_inc(sems["h_hi"], 1)

                act.wait_ge(x_loaded, 16 * TT_)
                act.wait_ge(*sig(l, "x_added", 0))
                row_squares()
                split_hi(0)
                split_hi(1)
                act.wait_ge(*sig(l, "par_psum", 1))
                for b, n in ((0, 108), (1, 88), (2, 76)):
                    act.activation(par[:, b, 0:n], ps[4][:, b * P:b * P + n], ACT.Copy)
                act.drain().then_inc(sems["par_ready"], 1)
                h_round(0, gain_attn)

                evacs = 0
                for u in range(U_Z + 1):
                    split_hi(2 * u + 2)
                    for j in range(4):
                        bank = ps[4 * (u % 2) + j]
                        act.wait_ge(*task_done(l, u, j))
                        if u <= U_GV:
                            if u > 0:
                                act.wait_ge(*sig(l, "gconv", 4 * (u - 1) + j + 1))
                            elif j == 0:
                                act.wait_ge(*sig(l, "ffn_conv", 0))
                            dst, fn = conv_in[:, j, 4:4 + T], ACT.Copy
                            src = bank[:, :]
                        elif u == U_TAIL:
                            dst, src, fn = pj[:, j, 1024:1312], bank[:, 0:288], ACT.Copy
                        elif u == U_KV:
                            dst, src, fn = pj[:, j, 512:1024], bank[:, :], ACT.Copy
                        elif u == U_Q:
                            dst = pj[:, j, 0:512].rearrange("p (n g d) -> p g n d", g=NG, d=DH)
                            src, fn = bank[:, :].rearrange("p (g n d) -> p g n d", g=NG, d=DH), ACT.Copy
                        else:
                            dst, src, fn = xo[:, j, 512:1024], bank[:, :], ACT.Silu
                        act.activation(dst, src, fn).then_inc(sems["proj_evac"], 1)
                        evacs += 1
                    split_hi(2 * u + 3)
                    if u <= U_GV:
                        for j in range(4):
                            act.wait_ge(*sig(l, "gconv", 4 * u + j + 1))
                            act.activation(qkvT[:, 4 * u + j, :], conv_out[:, j, :], ACT.Silu).then_inc(sems["gsilu"], 1)

                for i in range(6):
                    act.wait_ge(*sig(l, "qkT_psum", i + 1))
                    dst = qT[:, i, :] if i < 4 else kT[:, i - 4, :]
                    act.activation(dst, ps[i][:, :], ACT.Copy).then_inc(sems["qkT_ready"], 1)
                for kv in range(2):
                    act.wait_ge(*sig(l, "blk_f32", kv + 1))
                    act.activation(blk_hi[:, :, :], blk[:, :, :], ACT.Copy).then_inc(sems["blk_hi"], 1)
                    split_hi(2 * (U_CK + kv) + 2)
                    for s in range(2):
                        act.wait_ge(*task_done(l, U_CK + kv, s))
                        act.activation(hid[:, kv, s, :], ps[2 * kv + s][:, 0:64], ACT.Silu).then_inc(sems["hid_ready"], 1)
                    split_hi(2 * (U_CK + kv) + 3)
                act.wait_ge(*sig(l, "kcT_psum", 1))
                for g in range(NG):
                    rows = slice(DH * g, DH * g + DH)
                    act.activation(kcT[rows, g, :], ps[6][rows, 0:32], ACT.Copy)
                act.drain().then_inc(sems["kcT_ready"], 1)
                act.wait_ge(*sig(l, "ga_in", 1))
                act.activation(gn, gn, ACT.Exp)
                act.activation(bE.rearrange("p (t h) -> p t h", t=TT_), pj[:, :, PJ_B:PJ_B + 4], ACT.Exp, scale=-1.0)
                act.activation(gE.rearrange("p (t h) -> p t h", t=TT_), pj[:, :, PJ_G:PJ_G + 24], ACT.Exp, scale=-1.0)
                act.activation(aE, bc_al, ACT.Exp)
                act.drain()
                act.activation(gn, gn, ACT.Ln, bias=1.0).then_inc(sems["ga_exp"], 1)
                act.wait_ge(*sig(l, "gcum_psum", 1))
                act.activation(ex, ps[7][:, 0:64], ACT.Exp).then_inc(sems["gcum_exp"], 1)
                for t in range(TT_):
                    act.wait_ge(*sig(l, "cs_shift", t + 1))
                    act.activation(c_prob[:, t % 2, :], c_prob[:, t % 2, :], ACT.Exp).then_inc(sems["cs_exp"], 1)
                    act.wait_ge(*sig(l, "cpT_psum", t + 1))
                    act.activation(c_probT[:, t % 2, :], ps[2 + t % 2][:, 0:2 * P], ACT.Copy).then_inc(sems["cpT_ready"], 1)
                for i in range(N_ITEMS):
                    n = (i // 16 + 1) * P
                    act.wait_ge(*sig(l, "negmax", i + 1))
                    if i >= 2:
                        act.wait_ge(*sig(l, "pT_psum", i - 1))
                    act.activation(prob[:, i % 2, 0:n], ps[i % 2][:, 0:n], ACT.Exp, bias=neg_max[:, i:i + 1],
                                   accum_out=row_sum[:, i:i + 1])
                    act.drain().then_inc(sems["p_ready"], 1)

                act.wait_ge(*sig(l, "o_final", 1))
                for b in range(2):
                    for r in (2 * b, 2 * b + 1):
                        if b == 1 and r == 2:
                            act.wait_ge(*sig(l, "vn_ready", 4))
                        for f in range(2):
                            act.wait_ge(*sig(l, "raw_psum", 3 * r + f + 1))
                            if f == 0 and r % 2 == 1:
                                act.wait_ge(*sig(l, "forms", r))
                            bank = ps[3 * (r % 2) + f]
                            act.activation(raw_qk[:, f, :, :], h4(bank[:, :]), ACT.Copy)
                            act.activation(sq_qk[:, f, :, :], h4(bank[:, :]), ACT.Square)
                        act.drain().then_inc(sems["raw_ev"], 1)
                        tbank = [0, 1, 2, 6] if r % 2 == 0 else [3, 4, 5, 7]
                        for f in range(4):
                            act.wait_ge(*sig(l, "formsT_psum", 4 * r + f + 1))
                            if f < 3:
                                act.activation(formsT[:, f, :, :], h4(ps[tbank[f]][:, :]), ACT.Copy)
                            else:
                                act.activation(wq[:, r % 2, :, CH:3 * CH],
                                               ps[tbank[f]][:, :].rearrange("p (h n) -> p h n", h=GH), ACT.Copy)
                        act.drain().then_inc(sems["tt_ready"], 1)
                        act.wait_ge(*sig(l, "kk_psum", r + 1))
                        act.activation(decayT[:, :, :], h4(ps[tbank[1]][:, 0:GH * CH]), ACT.Exp).then_inc(sems["dt_exp"], 1)
                    for k in range(1, 6):
                        act.wait_ge(*sig(l, "y_psum", 6 * b + k + 1))
                        act.activation(yy[:, :, :], ps[0][:, :].rearrange("p (k n) -> p k n", k=2 * GH), ACT.Copy).then_inc(sems["y_ready"], 1)
                    for r in (2 * b, 2 * b + 1):
                        act.wait_ge(*sig(l, "uw_psum", 2 * b + 2))
                        act.activation(u_sb[:, r % 2, :, :], h4(ps[3 + r % 2][:, :]), ACT.Copy)
                        for c in range(2):
                            w_view = ps[5 + c][:, 256 * (r % 2):256 * (r % 2) + 256].rearrange("p (h n) -> p h n", h=GH)
                            act.activation(wq[:, r % 2, :, 3 * c * CH:3 * c * CH + CH], w_view, ACT.Copy)
                        act.drain().then_inc(sems["uw_ready"], 1)
                    for n in range(4 * b, 4 * b + 4):
                        r, c = n // 2, n % 2
                        act.wait_ge(*sig(l, "oc_psum", n + 1))
                        if c == 0 and r > 0:
                            act.wait_ge(*sig(l, "o_written", r))
                        src = h4(ps[7 if c == 0 else 0][CH * (1 - c):CH * (1 - c) + CH, :])
                        act.activation(og[CH * c:CH * c + CH, :, :], src, ACT.Copy)
                        act.activation(og_sq[CH * c:CH * c + CH, :, :], src, ACT.Square)
                        act.drain().then_inc(sems["og_ready"], 1)

                h_round(1, None)
                for u in (U_O0, U_O0 + 1):
                    split_hi(2 * u + 2)
                    split_hi(2 * u + 3)
                act.wait_ge(*sig(l, "x_added", 8))
                row_squares()
                h_round(2, gain_ffn)
                for i in range(N_UP):
                    u = U_UP + i
                    split_hi(2 * u + 2)
                    for j in range(4):
                        act.wait_ge(*task_done(l, u, j))
                        if i > 0:
                            act.wait_ge(*sig(l, "ffn_conv", 4 * (i - 1) + j + 1))
                        act.activation(conv_in[:, j, 4:4 + T], ps[4 * (u % 2) + j][:, :],
                                       ACT.Copy).then_inc(sems["ffn_copied"], 1)
                    split_hi(2 * u + 3)
                    for j in range(2):
                        act.wait_ge(*sig(l, "ffn_conv", 4 * i + j + 1))
                        act.activation(conv_out[:, j, :], conv_out[:, j, :], ACT.Silu).then_inc(sems["silu_ready"], 1)
                for k in range(FK):
                    act.wait_ge(*sig(l, "g_ready", k + 1))
                    if k >= 2:
                        act.wait_ge(*kt_used(l, k - 2))
                    act.activation(g_hi[:, k % 2, :], g_mlp[:, k, :], ACT.Copy).then_inc(sems["g_hi_done"], 1)
                    if k % 2 == 0 and k > 0:
                        split_hi(2 * U_DN + k // 2 + 1)

        @block.vector
        def _(dve):
            def tt(o, a, b, op):
                return dve.tensor_tensor(o, a, b, op)

            dve.wait_ge(const_ready, 1)
            dve.wait_ge(pos_loaded, 16)
            dve.tensor_copy(pos_f, pos_i[:, :])
            dve.drain()
            a3 = ang.rearrange("p (t i) -> p t i", t=TT_)
            tt(a3, over(pos_f, 2, 8), over(inv_freq, 1, TT_), ALU.mult)
            dve.drain()
            two_pi = 6.283185307179586
            c1 = 6.28125
            c2 = 0.0019350051879882812
            c3 = two_pi - c1 - c2
            magic = 12582912.0
            dve.tensor_scalar(turns, ang, 1.0 / two_pi, magic, ALU.mult, ALU.add)
            dve.drain()
            dve.tensor_scalar(turns, turns, magic, None, ALU.subtract)
            for c in (c1, c2, c3):
                dve.drain()
                dve.scalar_tensor_tensor(out=ang, in0=turns, scalar=-c, in1=ang, op0=ALU.mult, op1=ALU.add)
            dve.drain()
            dve.tensor_scalar(cosang, ang, two_pi / 4, None, ALU.add)
            dve.drain()
            dve.tensor_scalar(wrap, cosang, PI, -two_pi, ALU.is_gt, ALU.mult)
            dve.drain()
            tt(cosang, cosang, wrap, ALU.add)
            dve.drain()
            dve.tensor_scalar(cosang, cosang, PI, -PI, ALU.min, ALU.max)
            dve.tensor_scalar(ang, ang, PI, -PI, ALU.min, ALU.max)
            dve.drain().then_inc(rope_steps, 1)
            dve.wait_ge(rope_ready, 1)
            s3, k3 = ang.rearrange("p (t i) -> p t i", t=TT_), cosang.rearrange("p (t i) -> p t i", t=TT_)
            dve.tensor_scalar(rope_s[:, :, 0:8], s3, -1.0, None, ALU.mult)
            dve.tensor_copy(rope_s[:, :, 8:16], s3)
            dve.tensor_copy(rope_c[:, :, 0:8], k3)
            dve.tensor_copy(rope_c[:, :, 8:16], k3)
            dve.drain()

            with dve.Fori(0, depth) as l:

                def split_lo(p):
                    if p >= N_PIECES:
                        return
                    n = 4 * 288 if p // 2 == U_TAIL else PIECE
                    dve.wait_ge(*sig(l, "hi_done", p + 1))
                    tt(w_lo[:, p % 2, 0:n], raw[:, p % 2, 0:n], w_hi[:, p % 2, 0:n], ALU.subtract).then_inc(sems["split"], 1)

                def normalize(which):
                    dve.wait_ge(*sig(l, "rstd", which + 1))
                    for t in range(TT_):
                        dve.tensor_scalar(xo[:, t, :], x_res[:, t, :], rstd[:, t:t + 1], None,
                                          ALU.mult).then_inc(sems["normed"], 1)

                def h_rest(which, gain):
                    for kc in range(KC):
                        dve.wait_ge(*sig(l, "h_hi", 8 * which + kc + 1))
                        if gain is None:
                            tt(h_lo[:, kc, :], ps[kc % 4][:, :], h_hi[:, kc, :], ALU.subtract).then_inc(sems["h_ready"], 1)
                        else:
                            dve.scalar_tensor_tensor(out=h_lo[:, kc, :], in0=ps[kc % 4][:, :], scalar=gain[:, kc:kc + 1],
                                                     in1=h_hi[:, kc, :], op0=ALU.mult,
                                                     op1=ALU.subtract).then_inc(sems["h_ready"], 1)

                normalize(0)
                dve.memset(conv_in[:, :, 0:4], 0.0)
                split_lo(0)
                split_lo(1)
                dve.wait_ge(*sig(l, "par_ready", 1))
                h_rest(0, gain_attn)
                for u in range(U_GV + 1):
                    split_lo(2 * u + 2)
                    for j in range(4):
                        dve.wait_ge(*sig(l, "proj_evac", 4 * u + j + 1))
                        if u > 0:
                            dve.wait_ge(*sig(l, "gsilu", 4 * (u - 1) + j + 1))
                        col = 4 * u + j
                        dve.tensor_scalar(conv_out[:, j, :], conv_in[:, j, 4:4 + T], gdn_taps[:, 3, col:col + 1], None,
                                          ALU.mult)
                        for s in (1, 2, 3):
                            dve.drain()
                            last = dve.scalar_tensor_tensor(
                                out=conv_out[:, j, :], in0=conv_in[:, j, 4 - s:4 - s + T],
                                scalar=gdn_taps[:, 3 - s, col:col + 1], in1=conv_out[:, j, :], op0=ALU.mult, op1=ALU.add)
                        last.then_inc(sems["gconv"], 1)
                    split_lo(2 * u + 3)
                for u in range(U_TAIL, U_Z + 1):
                    split_lo(2 * u + 2)
                    split_lo(2 * u + 3)
                dve.wait_ge(bc_loaded, (l * 7 + 7) * 16)
                dve.tensor_scalar(q_gain, bc_q, float(DH) ** -0.5, None, ALU.mult)
                dve.wait_ge(*sig(l, "proj_evac", 24))

                def heads(ap, n):
                    return ap.rearrange("p (h d) -> p h d", h=n)

                for t in range(TT_):
                    tmp = sq_tmp[:, t % 2, :]
                    kn = pj[:, t, 768:1280].rearrange("p (b v n) -> p b v n", b=2, v=2)[:, :, 0, :]
                    tt(tmp[:, 0:512], pj[:, t, 0:512], pj[:, t, 0:512], ALU.mult)
                    tt(tmp[:, 512:768].rearrange("p (b n) -> p b n", b=2), kn, kn, ALU.mult)
                    dve.drain()
                    dve.tensor_reduce(qk_ss[:, 12 * t:12 * t + 12], heads(tmp, 12), AX.X, ALU.add)
                dve.drain().then_inc(sems["qk_squares"], 1)
                dve.wait_ge(*sig(l, "qk_rstd", 1))
                for t in range(TT_):
                    q = heads(pj[:, t, 0:512], 8)
                    kn = pj[:, t, 768:1280].rearrange("p (b v g d) -> p b v g d", b=2, v=2, g=2)[:, :, 0, :, :]
                    rs = qk_rs[:, 12 * t:12 * t + 12]
                    tt(q, q, over(rs[:, 0:8], 2, DH), ALU.mult)
                    for b in range(2):
                        tt(kn[:, b, :, :], kn[:, b, :, :], over(rs[:, 8 + 2 * b:10 + 2 * b], 2, DH), ALU.mult)
                    dve.drain()
                    tt(q, q, over(q_gain, 1, NH), ALU.mult)
                    for b in range(2):
                        tt(kn[:, b, :, :], kn[:, b, :, :], over(bc_k[:, b + 1, :], 1, NG), ALU.mult)
                    dve.drain()
                    kr = pj[:, t, 512:1280].rearrange("p (b v g d) -> p b v g d", b=3, v=2, g=2)[:, :, 0, :, :]
                    t1, t2 = sq_tmp[:, 0, :], sq_tmp[:, 1, :]
                    parts = [(q, t1[:, 0:128], t2[:, 0:128], NH)]
                    for b in range(3):
                        parts.append((kr[:, b, :, :], t1[:, 128 + 32 * b:160 + 32 * b], t2[:, 128 + 32 * b:160 + 32 * b], NG))
                    for xx, m1, m2, n in parts:
                        m1, m2 = heads(m1, n), heads(m2, n)
                        tt(m1, xx[:, :, 0:16], over(rope_c[:, t, :], 1, n), ALU.mult)
                        tt(m2[:, :, 0:8], xx[:, :, 8:16], over(rope_s[:, t, 0:8], 1, n), ALU.mult)
                        tt(m2[:, :, 8:16], xx[:, :, 0:8], over(rope_s[:, t, 8:16], 1, n), ALU.mult)
                    dve.drain()
                    for xx, m1, m2, n in parts:
                        tt(xx[:, :, 0:16], heads(m1, n), heads(m2, n), ALU.add)
                    dve.drain()
                dve.drain().then_inc(sems["q_ready"], 1)
                y3 = gy.rearrange("p (t h) -> p t h", t=TT_)
                tt(y3, pj[:, :, PJ_A:PJ_A + 4], over(bc_dt, 1, TT_), ALU.add)
                dve.drain()
                dve.tensor_scalar(gn, gy, -1.0, None, ALU.mult)
                dve.drain()
                tt(gn, gn, gy, ALU.min).then_inc(sems["ga_in"], 1)
                for kv in range(2):
                    dve.wait_ge(*sig(l, "blkT_psum", kv + 1))
                    if kv == 0:
                        dve.memset(blk[:, :, :], 0.0)
                        dve.drain()
                    else:
                        dve.wait_ge(*sig(l, "blk_ready", 1))
                    for g in range(NG):
                        for s in range(2):
                            rows = slice(64 * g, 64 * g + 64)
                            src = ps[6 + kv][rows, :].rearrange("p (n m s) -> p s m n", m=8, s=2)
                            for half in range(2):
                                o = blk[64 * s:64 * s + 64, 8 * half:8 * half + 8, 32 * g:32 * g + 31]
                                pe_b = over(pe_kv[64 * s:64 * s + 64, kv, 8 * half:8 * half + 8], 2, 31)
                                tt(o, src[:, s, :, half:half + 31], pe_b, ALU.add)
                    dve.drain().then_inc(sems["blk_f32"], 1)
                    if kv == 1:
                        split_lo(2 * U_CV + 1)
                    dve.wait_ge(*sig(l, "blk_hi", kv + 1))
                    tt(blk_lo[:, :, :], blk[:, :, :], blk_hi[:, :, :], ALU.subtract).then_inc(sems["blk_ready"], 1)
                    split_lo(2 * (U_CK + kv) + 2)
                dve.wait_ge(*sig(l, "cmp2_psum", 1))
                dve.tensor_copy(kc_rows[:, :], ps[4][0:64, 0:DH])
                dve.drain()
                tt(kc_sq[:, :], kc_rows[:, :], kc_rows[:, :], ALU.mult)
                dve.drain()
                dve.tensor_reduce(kc_ss, kc_sq[:, :], AX.X, ALU.add).then_inc(sems["kc_ss"], 1)
                dve.wait_ge(*sig(l, "cmp2_psum", 2))
                dve.tensor_copy(vc_rows[:, :], ps[5][0:64, 0:DH])
                dve.memset(vc_diag[:, :], 0.0)
                dve.memset(kcT[:, :, :], 0.0)
                dve.drain()
                for h in range(4):
                    g = h % NG
                    dve.tensor_copy(vc_diag[32 * h:32 * h + 32, DH * h:DH * h + DH], vc_rows[32 * g:32 * g + 32, :])
                dve.drain().then_inc(sems["vc_ready"], 1)
                dve.wait_ge(*sig(l, "kc_rstd", 1))
                dve.scalar_tensor_tensor(out=kc_rows[:, :], in0=kc_rows[:, :], scalar=kc_rr, in1=bc_k[0:64, 0, :],
                                         op0=ALU.mult, op1=ALU.mult)
                dve.drain()
                for g in range(NG):
                    dve.tensor_copy(kc_two[:, DH * g:DH * g + DH], kc_rows[32 * g:32 * g + 32, :])
                dve.drain().then_inc(sems["kc_ready"], 1)
                split_lo(2 * U_O0 + 1)
                dve.wait_ge(*sig(l, "ga_exp", 1))
                dve.scalar_tensor_tensor(out=gdec, in0=gy, scalar=0.0, in1=gn, op0=ALU.max, op1=ALU.add)
                dve.tensor_scalar(bE, bE, 1.0, None, ALU.add)
                dve.tensor_scalar(gE, gE, 1.0, None, ALU.add)
                dve.drain()
                g3 = gdec.rearrange("p (t h) -> p t h", t=TT_)
                tt(g3, g3, over(aE, 1, TT_), ALU.mult)
                dve.reciprocal(beta, bE)
                dve.reciprocal(gate, gE)
                dve.drain()
                dve.tensor_scalar(gdec, gdec, -1.0, None, ALU.mult).then_inc(sems["ga_out"], 1)
                gate4 = gate.rearrange("p (t h b) -> p t h b", t=TT_, h=NH)
                for t in range(TT_):
                    cp = heads(c_prob[:, t % 2, :], NH)
                    dve.wait_ge(*sig(l, "cs_psum", t + 1))
                    tt(cp, heads(ps[t % 2][:, 0:256], NH), over(cmp_add[:, t, :], 1, NH), ALU.add)
                    dve.drain()
                    dve.tensor_reduce(c_max, cp, AX.X, ALU.max)
                    dve.drain()
                    tt(cp, cp, over(c_max, 2, 32), ALU.subtract).then_inc(sems["cs_shift"], 1)
                    dve.wait_ge(*sig(l, "cs_exp", t + 1))
                    tt(cp, cp, over(cmp_mul[:, t, :], 1, NH), ALU.mult).then_inc(sems["cp_ready"], 1)
                    dve.drain()
                    dve.tensor_reduce(c_sum, cp, AX.X, ALU.add)
                    dve.drain()
                    dve.tensor_scalar(c_sum, c_sum, 1e-30, None, ALU.max)
                    dve.drain()
                    dve.reciprocal(c_coef, c_sum)
                    dve.drain()
                    cc = c_coef.rearrange("p (n g) -> p n g", g=NG)
                    tt(cc, cc, gate4[:, t, :, 0].rearrange("p (g n) -> p n g", g=NG), ALU.mult)
                    dve.drain()
                    dve.wait_ge(*sig(l, "co_psum", t + 1))
                    tt(xo[:, t, 0:512].rearrange("p (g n d) -> p n g d", g=NG, d=DH),
                       ps[4 + t % 2][:, :].rearrange("p (n g d) -> p n g d", g=NG, d=DH), over(cc, 3, DH),
                       ALU.mult).then_inc(sems["o_init"], 1)

                def add_branch(k):
                    t, b = k // 2, k % 2
                    dve.wait_ge(*sig(l, "pv_done", 8 * k + 8))
                    dve.reciprocal(coef, row_sum[:, 8 * k:8 * k + 8])
                    dve.drain()
                    tt(coef, coef, gate4[:, t, :, 1 + b], ALU.mult)
                    dve.drain()
                    tt(heads(o_tmp[:, k % 2, :], NH), heads(ps[4 + k % 2][:, :], NH), over(coef, 2, DH),
                       ALU.mult).then_inc(sems["o_added"], 1)
                    dve.drain()
                    tt(xo[:, t, 0:512], xo[:, t, 0:512], o_tmp[:, k % 2, :], ALU.add)

                for i in range(N_ITEMS + 1):
                    if i < N_ITEMS:
                        n = (i // 16 + 1) * P
                        dve.wait_ge(*sig(l, "s_psum", i + 1))
                        dve.tensor_reduce(neg_max[:, i:i + 1], ps[i % 2][:, 0:n], AX.X, ALU.max,
                                          negate=True).then_inc(sems["negmax"], 1)
                    if i >= 1:
                        j = i - 1
                        n = (j // 16 + 1) * P
                        dve.wait_ge(*sig(l, "pT_psum", j + 1))
                        if j >= 2:
                            dve.wait_ge(*sig(l, "pv_done", j - 1))
                        dve.tensor_copy(probT[:, j % 2, 0:n], ps[2 + j % 2][:, 0:n]).then_inc(sems["pT_ready"], 1)
                        if i >= 10 and (i - 2) % 8 == 0:
                            add_branch((i - 2) // 8 - 1)
                add_branch(7)
                dve.drain()
                for t in range(TT_):
                    tt(o_tmp[:, t % 2, :], xo[:, t, 0:512], xo[:, t, 0:512], ALU.mult)
                    dve.drain()
                    dve.tensor_reduce(no_ss[:, 8 * t:8 * t + 8], heads(o_tmp[:, t % 2, :], NH), AX.X, ALU.add)
                dve.drain().then_inc(sems["no_ss"], 1)
                dve.wait_ge(*sig(l, "no_rstd", 1))
                for t in range(TT_):
                    o = heads(xo[:, t, 0:512], NH)
                    tt(o, o, over(no_rr[:, 8 * t:8 * t + 8], 2, DH), ALU.mult)
                dve.drain()
                for t in range(TT_):
                    tt(xo[:, t, 0:512], xo[:, t, 0:512], bc_no, ALU.mult)
                dve.drain().then_inc(sems["o_final"], 1)

                dve.memset(state[:, :, :], 0.0).then_inc(sems["s_ready"], 1)
                lanes = 2 * GH
                for b in range(2):
                    for r in (2 * b, 2 * b + 1):
                        rb = r % 2
                        tbank = [0, 1, 2, 6] if rb == 0 else [3, 4, 5, 7]
                        dve.wait_ge(*sig(l, "raw_ev", r + 1))
                        dve.tensor_reduce(g_ss, sq_qk[:, :, :, :].rearrange("p f h d -> p (f h) d"), AX.X,
                                          ALU.add).then_inc(sems["ss_ready"], 1)
                        dve.wait_ge(*sig(l, "raw_psum", 3 * r + 3))
                        be = beta[:, 4 * r:4 * r + 4]
                        e_cum, e_rest = ex[:, 4 * r:4 * r + 4], ex[:, 16 + 4 * r:20 + 4 * r]
                        tt(vb[:, rb, :, :], ps[3 * rb + 2][:, :].rearrange("p (h d) -> p h d", h=GH), over(be, 2, GD), ALU.mult)
                        tt(g_upto[:, :, :], over(upto[:, :], 1, GH), over(gdec[:, 4 * r:4 * r + 4], 2, CH), ALU.mult)
                        dve.wait_ge(*sig(l, "rr_ready", r + 1))
                        dve.wait_ge(*sig(l, "gcum_exp", 1))
                        s_q, s_qg, s_kb, s_kbg, s_kd = (g_sc[:, 4 * i:4 * i + 4] for i in range(5))
                        dve.tensor_scalar(s_q, g_rr[:, 0:4], float(GD) ** -0.5, None, ALU.mult)
                        tt(s_kb, g_rr[:, 4:8], be, ALU.mult)
                        tt(s_kd, g_rr[:, 4:8], e_rest, ALU.mult)
                        dve.drain()
                        tt(s_qg, s_q, e_cum, ALU.mult)
                        tt(s_kbg, s_kb, e_cum, ALU.mult)
                        dve.drain()
                        q_, k_ = raw_qk[:, 0, :, :], raw_qk[:, 1, :, :]
                        for o, src, sc in ((forms_sb[:, 0, :, :], k_, g_rr[:, 4:8]), (forms_sb[:, 1, :, :], k_, s_kb),
                                           (forms_sb[:, 2, :, :], q_, s_q), (forms_sb[:, 3, :, :], q_, s_qg),
                                           (kbg[:, rb, :, :], k_, s_kbg), (k_dec[:, rb, :, :], k_, s_kd)):
                            tt(o, src, over(sc, 2, GD), ALU.mult)
                        dve.drain().then_inc(sems["forms"], 1)
                        dve.wait_ge(*sig(l, "dt_exp", r + 1))
                        tt(decayT[:, :, :], decayT[:, :, :], over(upto[:, :], 1, GH), ALU.mult)
                        dve.drain()
                        kk = ps[tbank[0]][:, :].rearrange("p (f h n) -> p f h n", f=2, h=GH)
                        tt(akkT[:, GH * rb:GH * rb + GH, :], kk[:, 0, :, :], decayT[:, :, :], ALU.mult)
                        tt(aqkT[:, GH * rb:GH * rb + GH, :], kk[:, 1, :, :], decayT[:, :, :], ALU.mult)
                        dve.drain().then_inc(sems["a_ready"], 1)

                    def level_rows(k):
                        return over(level_mask[:, k, :], 1, lanes)

                    def bank3(i):
                        return ps[i][:, :].rearrange("p (k n) -> p k n", k=lanes)
                    tt(ltT[:, :, :], akkT[:, :, :], level_rows(0), ALU.mult).then_inc(sems["lt_ready"], 1)
                    dve.drain()
                    tt(xiT[:, :, :], over(ident64[:, :], 1, lanes), ltT[:, :, :], ALU.subtract)
                    dve.wait_ge(*sig(l, "y_psum", 6 * b + 1))
                    tt(xi[:, :, :], over(ident64[:, :], 1, lanes), bank3(0), ALU.subtract)
                    dve.drain().then_inc(sems["x_ready"], 1)
                    for k in range(1, 6):
                        tt(ltT[:, :, :], akkT[:, :, :], level_rows(k), ALU.mult).then_inc(sems["lt_ready"], 1)
                        dve.wait_ge(*sig(l, "p_psum", 5 * b + k))
                        if k < 5:
                            tt(xi[:, :, :], xi[:, :, :], bank3(1), ALU.subtract)
                        tt(xiT[:, :, :], xiT[:, :, :], bank3(2), ALU.subtract)
                        dve.drain().then_inc(sems["x_ready"], 1)

                    def finish_tile(r):
                        dve.wait_ge(*sig(l, "orr", r + 1))
                        tt(og[:, :, :], og[:, :, :], over(o_rr, 2, GD), ALU.mult)
                        dve.drain()
                        tt(og[:, :, :], og[:, :, :], over(bc_go, 1, GH), ALU.mult)
                        dve.drain()
                        z = xo[:, r, 512:1024].rearrange("p (h d) -> p h d", h=GH)
                        tt(z, og[:, :, :], z, ALU.mult).then_inc(sems["o_written"], 1)

                    for n in range(4 * b, 4 * b + 4):
                        r, c = n // 2, n % 2
                        rows = slice(CH * c, CH * c + CH)
                        dve.wait_ge(*sig(l, "ws_psum", n + 1))
                        dve.wait_ge(*sig(l, "uw_ready", r + 1))
                        ws = ps[7 if c == 0 else 0][rows, :].rearrange("p (h d) -> p h d", h=GH)
                        tt(v_new[rows, :, :], u_sb[rows, r % 2, :, :], ws, ALU.subtract).then_inc(sems["vn_ready"], 1)
                        dve.wait_ge(*sig(l, "su_psum", n + 1))
                        dve.wait_ge(*sig(l, "sg_ready", n + 1))
                        tt(state[:, :, :], state_g[:, :, :], ps[1][:, :].rearrange("p (h d) -> p h d", h=GH),
                           ALU.add).then_inc(sems["s_ready"], 1)
                        if c == 1:
                            dve.wait_ge(*sig(l, "og_ready", n + 1))
                            dve.tensor_reduce(o_ss, og_sq[:, :, :], AX.X, ALU.add).then_inc(sems["oss"], 1)
                            finish_tile(r)
                dve.drain()
                dve.memset(conv_in[:, :, 0:4], 0.0)
                h_rest(1, None)
                for u in (U_O0, U_O0 + 1):
                    split_lo(2 * u + 2)
                    split_lo(2 * u + 3)
                    c = (u - U_O0) * 512
                    for j in range(4):
                        dve.wait_ge(*task_done(l, u, j))
                        xs = x_res[:, j, c:c + 512]
                        tt(xs, xs, ps[4 * (u % 2) + j][:, :], ALU.add).then_inc(sems["x_added"], 1)
                normalize(1)
                h_rest(2, gain_ffn)
                for i in range(N_UP):
                    u = U_UP + i
                    split_lo(2 * u + 2)
                    for j in range(4):
                        col = 2 * i + j if j < 2 else FK + 2 * i + j - 2
                        dve.wait_ge(*sig(l, "ffn_copied", 4 * i + j + 1))
                        dve.tensor_scalar(conv_out[:, j, :], conv_in[:, j, 4:4 + T], ffn_tap2[:, col:col + 1],
                                          ffn_bias[:, col:col + 1], ALU.mult, ALU.add)
                        for s in (1, 2):
                            dve.drain()
                            dve.scalar_tensor_tensor(
                                out=conv_out[:, j, :], in0=conv_in[:, j, 4 - s:4 - s + T],
                                scalar=ffn_taps01[:, 2 - s, col:col + 1], in1=conv_out[:, j, :], op0=ALU.mult, op1=ALU.add)
                        dve.drain().then_inc(sems["ffn_conv"], 1)
                    split_lo(2 * u + 3)
                    for j in range(2):
                        dve.wait_ge(*sig(l, "silu_ready", 2 * i + j + 1))
                        tt(g_mlp[:, 2 * i + j, :], conv_out[:, j, :], conv_out[:, 2 + j, :],
                           ALU.mult).then_inc(sems["g_ready"], 1)
                    dve.drain()
                for k in range(FK):
                    dve.wait_ge(*sig(l, "g_hi_done", k + 1))
                    tt(g_lo[:, k % 2, :], g_mlp[:, k, :], g_hi[:, k % 2, :], ALU.subtract).then_inc(sems["g_split"], 1)
                    if k % 2 == 0 and k > 0:
                        split_lo(2 * U_DN + k // 2 + 1)
                for i in range(8):
                    if i < 7:
                        dve.wait_ge(*sig(l, "down_done", i + 1))
                    else:
                        dve.wait_ge(*sig(l, "even_used", N_UNITS))
                    xs = x_res[:, i // 2, (i % 2) * 512:(i % 2) * 512 + 512]
                    tt(xs, xs, ps[i][:, :], ALU.add).then_inc(sems["x_added"], 1)

        @block.tensor
        def _(pe):
            def three(o, a, b, start, stop):
                pe.matmul(o, a[0], b[0], start=start, stop=False)
                pe.matmul(o, a[0], b[1], start=False, stop=False)
                return pe.matmul(o, a[1], b[0], start=False, stop=stop)

            pe.wait_ge(const_ready, 1)
            with pe.Fori(0, depth) as l:

                def turn_rows(which, ready):
                    for kc in range(KC):
                        if kc >= 4:
                            pe.wait_ge(*sig(l, "h_ready", 8 * which + kc - 3))
                        for t in range(TT_):
                            if kc == 0:
                                ready(t)
                            last = pe.transpose(ps[kc % 4][:, t * P:(t + 1) * P], xo[:, t, kc * P:(kc + 1) * P], ident[:, :])
                        last.then_inc(sems["hT_psum"], 1)

                def dense(u, which, bank_free):
                    up = U_UP <= u < U_DN
                    channels = u <= U_GV or up
                    width = 288 if u == U_TAIL else 512
                    for a in range(2):
                        pe.wait_ge(*sig(l, "split", 2 * u + a + 1))
                        hi = w_hi[:, a, 0:4 * width].rearrange("p (k n) -> p k n", k=4)
                        lo = w_lo[:, a, 0:4 * width].rearrange("p (k n) -> p k n", k=4)
                        for j in range(4):
                            if a == 0:
                                bank_free(j)
                            bank = ps[4 * (u % 2) + j]
                            for k in range(4):
                                kc = 4 * a + k
                                if j == 0:
                                    pe.wait_ge(*sig(l, "h_ready", 8 * which + kc + 1))
                                h = (h_hi[:, kc, :], h_lo[:, kc, :])
                                st, sp_ = kc == 0, kc == KC - 1
                                if channels:
                                    w = (hi[:, k, P * j:P * j + P], lo[:, k, P * j:P * j + P])
                                    last = three(bank[:, :], w, h, st, sp_)
                                else:
                                    h = (h[0][:, P * j:P * j + P], h[1][:, P * j:P * j + P])
                                    last = three(bank[:, 0:width], h, (hi[:, k, :], lo[:, k, :]), st, sp_)
                            if a == 1 and j < 3:
                                last.then_inc(sems["dense_done"], 1)
                        last.then_inc(sems["odd_used" if a else "even_used"], 1)

                def wait(name, k):
                    pe.wait_ge(*sig(l, name, k))

                pe.wait_ge(par_loaded, (l * 7 + 7) * 16)
                wait("x_added", 0)
                for b, n in ((0, 108), (1, 88), (2, 76)):
                    last = pe.transpose(ps[4][:, b * P:b * P + n], par_rows[0:n, b, :], ident[0:n, 0:n])
                last.then_inc(sems["par_psum"], 1)
                turn_rows(0, lambda t: wait("normed", t + 1))
                wait("par_ready", 1)
                for u in range(U_Z + 1):
                    if u >= 2:
                        dense(u, 0, lambda j: wait("proj_evac", 4 * (u - 2) + j + 1))
                    elif u == 0:
                        dense(u, 0, lambda j: wait("h_ready", 4 + j + 1))
                    else:
                        dense(u, 0, lambda j: None)

                wait("proj_evac", 28)
                wait("q_ready", 1)
                for p in range(4):
                    for t in range(TT_):
                        last = pe.transpose(ps[p][:, t * P:(t + 1) * P], pj[:, t, P * p:P * p + P], ident[:, :])
                    last.then_inc(sems["qkT_psum"], 1)
                for i, col in enumerate((768, 1024, 512, 640)):
                    for t in range(TT_):
                        last = pe.transpose(ps[4 + i][:, t * P:(t + 1) * P], pj[:, t, col:col + P], ident[:, :])
                    last.then_inc(sems["qkT_psum" if i < 2 else "blkT_psum"], 1)
                for kv in range(2):
                    u = U_CK + kv
                    wait("blk_ready", kv + 1)
                    wait("qkT_ready", 2 * kv + 2)
                    for a in range(2):
                        wait("split", 2 * u + a + 1)
                        hi = w_hi[:, a, :].rearrange("p (m n) -> p m n", m=8)
                        lo = w_lo[:, a, :].rearrange("p (m n) -> p m n", m=8)
                        for s in range(2):
                            for m in range(8):
                                c = slice(P * s, P * s + P)
                                last = three(ps[2 * kv + s][:, 0:64], (hi[:, m, c], lo[:, m, c]),
                                             (blk_hi[:, 8 * a + m, :], blk_lo[:, 8 * a + m, :]),
                                             a == 0 and m == 0, a == 1 and m == 7)
                            if a == 1 and s == 0:
                                last.then_inc(sems["dense_done"], 1)
                        last.then_inc(sems["odd_used" if a else "even_used"], 1)
                pe.wait_ge(bc_loaded, (l * 7 + 7) * 16)
                wait("qkT_ready", 6)
                for kv in range(2):
                    for s in range(2):
                        wait("hid_ready", 2 * kv + s + 1)
                        last = pe.matmul(ps[4 + kv][0:64, 0:DH], hid[:, kv, s, :], cmp_w2_sb[:, kv, s, :],
                                         start=s == 0, stop=s == 1)
                    last.then_inc(sems["cmp2_psum"], 1)
                wait("blk_f32", 2)
                wait("kc_ready", 1)
                pe.sem_inc(pe_steps, 1)
                pe.transpose(ps[6][:, 0:32], kc_two[:, :], ident[0:32, 0:32]).then_inc(sems["kcT_psum"], 1)
                wait("ga_out", 1)
                for i, m in enumerate((sum_upto[:, :], after[:, :], chunk_rows[:, 0, :], chunk_rows[:, 1, :])):
                    last = pe.matmul(ps[7][:, 16 * i:16 * i + 16], m, gdec, start=True, stop=True)
                last.then_inc(sems["gcum_psum"], 1)

                def half(h):
                    return slice(64 * (h // 4), 64 * (h // 4) + 64)

                wait("kcT_ready", 1)
                wait("vc_ready", 1)
                wait("hid_ready", 4)

                def c_scores(t):
                    if t >= 2:
                        wait("cs_shift", t - 1)
                    for n in range(NH // NG):
                        last = pe.matmul(ps[t % 2][:, 64 * n:64 * n + 64], qT[:, n, t * P:(t + 1) * P],
                                         kcT[:, :, :].rearrange("p g n -> p (g n)"), start=True, stop=True)
                    last.then_inc(sems["cs_psum"], 1)

                c_scores(0)
                c_scores(1)
                for t in range(TT_):
                    wait("cp_ready", t + 1)
                    if t >= 2:
                        wait("cpT_ready", t - 1)
                    for g in range(NG):
                        last = pe.transpose(ps[2 + t % 2][:, P * g:P * g + P], c_prob[:, t % 2, P * g:P * g + P], ident[:, :])
                    last.then_inc(sems["cpT_psum"], 1)
                    if t + 2 < TT_:
                        c_scores(t + 2)
                    wait("cpT_ready", t + 1)
                    if t >= 2:
                        wait("o_init", t - 1)
                    for g in range(NG):
                        last = pe.matmul(ps[4 + t % 2][:, 256 * g:256 * g + 256], c_probT[:, t % 2, P * g:P * g + P],
                                         vc_diag[:, :], start=True, stop=True)
                    last.then_inc(sems["co_psum"], 1)

                wait("cs_shift", 4)

                def scores(i):
                    t, b, h = i // 16, i // 8 % 2, i % 8
                    if i >= 2:
                        wait("p_ready", i - 1)
                    n = (t + 1) * P
                    pe.matmul(ps[i % 2][:, 0:n], qT[half(h), h % 4, t * P:(t + 1) * P], kT[half(h), b, 0:n],
                              start=True, stop=False)
                    pe.matmul(ps[i % 2][:, t * P:n], ident_bf[:, :], causal_bf[:, :],
                              start=False, stop=True).then_inc(sems["s_psum"], 1)

                def turn(i):
                    t = i // 16
                    wait("p_ready", i + 1)
                    if i >= 2:
                        wait("pT_ready", i - 1)
                    for j in range(t + 1):
                        last = pe.transpose(ps[2 + i % 2][:, j * P:(j + 1) * P], prob[:, i % 2, j * P:(j + 1) * P], ident[:, :])
                    last.then_inc(sems["pT_psum"], 1)

                def weigh(i):
                    t, b, h = i // 16, i // 8 % 2, i % 8
                    k = i // 8
                    wait("pT_ready", i + 1)
                    if i % 8 == 0:
                        if k >= 2:
                            wait("o_added", k - 1)
                        else:
                            wait("o_init", 3 + k)
                    col = 512 + 256 * (b + 1) + 128 + DH * (h // 4)
                    for j in range(t + 1):
                        last = pe.matmul(ps[4 + k % 2][:, DH * h:DH * h + DH], probT[:, i % 2, j * P:(j + 1) * P],
                                         pj[:, j, col:col + DH], start=j == 0, stop=j == t)
                    last.then_inc(sems["pv_done"], 1)

                scores(0)
                scores(1)
                for i in range(N_ITEMS):
                    turn(i)
                    if i + 2 < N_ITEMS:
                        scores(i + 2)
                    if i >= 1:
                        weigh(i - 1)
                weigh(N_ITEMS - 1)

                wait("gsilu", 12)
                wait("o_final", 1)
                for b in range(2):
                    for r in (2 * b, 2 * b + 1):
                        if b == 1:
                            wait("og_ready", 4)
                            wait("s_ready", 5)
                        for f in range(3):
                            for h in range(GH):
                                last = pe.transpose(ps[3 * (r % 2) + f][:, P * h:P * h + P],
                                                    qkvT[:, GH * f + h, r * P:(r + 1) * P], ident[:, :])
                            last.then_inc(sems["raw_psum"], 1)
                    for r in (2 * b, 2 * b + 1):
                        rb = r % 2
                        tbank = [0, 1, 2, 6] if rb == 0 else [3, 4, 5, 7]
                        wait("forms", r + 1)
                        for f in range(4):
                            for h in range(GH):
                                last = pe.transpose(ps[tbank[f]][:, P * h:P * h + P], forms_sb[:, f, h, :], ident[:, :])
                            last.then_inc(sems["formsT_psum"], 1)
                        wait("tt_ready", r + 1)
                        pe.sem_inc(pe_steps, 1)
                        for f, other in ((0, 1), (1, 2)):
                            for h in range(GH):
                                for c in range(2):
                                    rows = slice(CH * c, CH * c + CH)
                                    pe.matmul(ps[tbank[0]][rows, 256 * f + CH * h:256 * f + CH * h + CH],
                                              formsT[:, 0, h, rows], formsT[:, other, h, rows], start=True, stop=True)
                        pe.matmul(ps[tbank[1]][:, 0:GH * CH], after[:, :], g_upto[:, :, :].rearrange("p h n -> p (h n)"),
                                  start=True, stop=True).then_inc(sems["kk_psum"], 1)
                        wait("a_ready", r + 1)

                    def lanes_mm(bank, lhs, rhs):
                        pe.sem_inc(pe_steps, 1)
                        for k in range(2 * GH):
                            for c in range(2):
                                rows = slice(CH * c, CH * c + CH)
                                r_ = rhs[rows, k, :] if rhs is not None else ident64[rows, :]
                                last = pe.matmul(ps[bank][rows, CH * k:CH * k + CH], lhs[rows, k, :], r_,
                                                 start=True, stop=True)
                        return last

                    wait("lt_ready", 6 * b + 1)
                    lanes_mm(0, ltT, None).then_inc(sems["y_psum"], 1)
                    for k in range(1, 6):
                        wait("lt_ready", 6 * b + k + 1)
                        wait("x_ready", 6 * b + k)
                        lanes_mm(0, ltT, xi).then_inc(sems["y_psum"], 1)
                        wait("y_ready", 5 * b + k)
                        if k < 5:
                            lanes_mm(1, xiT, yy)
                        lanes_mm(2, yy, xiT).then_inc(sems["p_psum"], 1)
                    wait("x_ready", 6 * b + 6)
                    pe.sem_inc(pe_steps, 1)
                    for r in (2 * b, 2 * b + 1):
                        rb = r % 2
                        for h in range(GH):
                            for c in range(2):
                                rows = slice(CH * c, CH * c + CH)
                                inv = xiT[rows, GH * rb + h, :]
                                pe.matmul(ps[3 + rb][rows, P * h:P * h + P], inv, vb[rows, rb, h, :], start=True, stop=True)
                                last = pe.matmul(ps[5 + c][:, 256 * rb + CH * h:256 * rb + CH * h + CH], kbg[rows, rb, h, :], inv,
                                                 start=True, stop=True)
                        last.then_inc(sems["uw_psum"], 1)
                    for n in range(4 * b, 4 * b + 4):
                        r, c = n // 2, n % 2
                        rb = r % 2
                        rows, other = slice(CH * c, CH * c + CH), slice(CH * (1 - c), CH * (1 - c) + CH)
                        bank = ps[7 if c == 0 else 0]
                        wait("uw_ready", r + 1)
                        wait("s_ready", n + 1)
                        if n % 4 >= 2:
                            wait("og_ready", n - 1)
                        for h in range(GH):
                            last = pe.matmul(bank[:, P * h:P * h + P], wq[:, rb, h, P * c:P * c + P], state[:, h, :],
                                             start=h == 0, stop=False, skip_group_check=True)
                        last.then_inc(sems["ws_psum"], 1)
                        wait("vn_ready", n + 1)
                        for h in range(GH):
                            last = pe.matmul(ps[1][:, P * h:P * h + P], k_dec[rows, rb, h, :], v_new[rows, h, :],
                                             start=True, stop=True)
                        last.then_inc(sems["su_psum"], 1)
                        for h in range(GH):
                            last = pe.matmul(bank[other, P * h:P * h + P], aqkT[rows, GH * rb + h, :], v_new[rows, h, :],
                                             start=False, stop=h == GH - 1, skip_group_check=True)
                        last.then_inc(sems["oc_psum"], 1)

                wait("o_written", 4)
                turn_rows(1, lambda t: None)
                for u in (U_O0, U_O0 + 1):
                    dense(u, 1, lambda j: None)
                turn_rows(2, lambda t: wait("normed", 4 + t + 1))
                for i in range(N_UP):
                    u = U_UP + i
                    dense(u, 2, (lambda j: wait("ffn_copied", 4 * (i - 2) + j + 1)) if i >= 2 else (lambda j: None))
                for k in range(FK):
                    p = 2 * U_DN + k // 2
                    a = p % 2
                    if k % 2 == 0:
                        wait("split", p + 1)
                    wait("g_split", k + 1)
                    cols = slice((k % 2) * 1024, (k % 2) * 1024 + 1024)
                    hi, lo = w_hi[:, a, cols], w_lo[:, a, cols]
                    for i in range(8):
                        if k == 0 and i % 2 == 0:
                            wait("ffn_copied", 44)
                        j, c = i // 2, slice((i % 2) * 512, (i % 2) * 512 + 512)
                        g = (g_hi[:, k % 2, P * j:P * j + P], g_lo[:, k % 2, P * j:P * j + P])
                        last = three(ps[i][:, :], g, (hi[:, c], lo[:, c]), k == 0, k == FK - 1)
                        if k == FK - 1 and i < 7:
                            last.then_inc(sems["down_done"], 1)
                    last.then_inc(sems["g_used" if k % 2 == 0 else "odd_used" if a else "even_used"], 1)


def kernel(**inputs):
    import numpy as np
    import concourse.bacc as bacc
    from concourse.bass_utils import run_bass_kernel_spmd

    names = ["x", "positions", "attn_norm", "w_in", "nsa_q_norm", "nsa_k_norm", "cmp_pe", "cmp_w1", "cmp_w2",
             "nsa_out_norm", "gdn_conv_w", "gdn_a_log", "gdn_dt_bias", "gdn_out_norm", "w_out", "ffn_norm", "w_up",
             "ffn_conv_w", "ffn_conv_b", "w_down"]
    nc = bacc.Bacc("TRN2", target_bir_lowering=False, num_devices=1)
    arrays = {n: np.ascontiguousarray(inputs[n]) for n in names}
    aps = [nc.dram_tensor(f"in_{n}", arrays[n].shape, mybir.dt.from_np(arrays[n].dtype), kind="ExternalInput").ap()
           for n in names]
    out = nc.dram_tensor("out", arrays["x"].shape, F32, kind="ExternalOutput").ap()
    trunk(nc, arrays["w_in"].shape[0], *aps, out)
    r = run_bass_kernel_spmd(nc, [{f"in_{n}": arrays[n] for n in names}], core_ids=[0])
    return r.results[0]["out"]
```

```python
from contextlib import ExitStack

import concourse.bass as bass
from concourse import mybir

F32 = mybir.dt.float32
F32R = mybir.dt.float32r
BF16 = mybir.dt.bfloat16
I32 = mybir.dt.int32
ALU = mybir.AluOpType
ACT = mybir.ActivationFunctionType
AX = mybir.AxisListType

P = 128
D = 1024
T = 512
TT_ = T // P
KC = D // P
NH, DH, NG = 8, 64, 2
NQ = NH * DH
NKV = 3 * 2 * NG * DH
GH, GD, CH = 4, 128, 64
GW = GH * GD
BLK, STRIDE, HID = 32, 16, 256
FF = 2816
FK = FF // P
EPS = 1e-6
THETA, ROPE = 500000.0, 16
NEG = -1e30
PI = 3.1415925
C_Q, C_KV, C_G, C_QKV, C_AB, C_Z = 0, 512, 1280, 1304, 2840, 2848
PJ_W = NQ + NKV + NH * 3 + 2 * GH
PJ_G, PJ_A, PJ_B = 1280, 1304, 1308

PIECE = 2048
U_GQ, U_GK, U_GV, U_TAIL, U_KV, U_Q, U_Z, U_CK, U_CV, U_O0, U_UP, U_DN = 0, 1, 2, 3, 4, 5, 6, 7, 8, 9, 11, 22
N_UP, N_UNITS = 11, 28
N_PIECES = 2 * N_UNITS - 1
N_ITEMS = TT_ * 2 * NH

SIGNALS = dict(
    even_used=28, odd_used=27, hi_done=N_PIECES, split=N_PIECES, dense_done=3 * 20,
    squares=2, rstd=2, normed=8, hT_psum=24, h_hi=24, h_ready=24,
    proj_evac=28, gconv=12, gsilu=12, par_psum=1, par_ready=1,
    qk_squares=1, qk_rstd=1, q_ready=1, qkT_psum=6, qkT_ready=6, blkT_psum=2, blk_f32=2, blk_hi=2, blk_ready=2,
    hid_silu=2, hid_psum=1, hid_ready=1, cmp2_psum=1, kc_ss=1, kc_rstd=1, kc_ready=1, kcT_psum=1, kcT_ready=1, vc_ready=1,
    cs_psum=4, cs_shift=4, cs_exp=4, cp_ready=4, cpT_psum=4, cpT_ready=4, co_psum=4, o_init=4,
    s_psum=N_ITEMS, negmax=N_ITEMS, p_ready=N_ITEMS, pT_psum=N_ITEMS, pT_ready=N_ITEMS, pv_done=N_ITEMS, o_added=8,
    no_ss=TT_, no_rstd=TT_, o_final=1,
    ga_in=1, ga_exp=1, ga_out=1, gcum_psum=1, gcum_exp=1,
    raw_psum=12, raw_ev=4, rr_ready=4, vb_ready=4, decay_psum=4, dt_exp=4, forms=4, formsT_psum=16, formsT_ready=16,
    kk_psum=4, a_ready=4,
    lt_ready=12, y_psum=12, y_ready=10, p_psum=10, x_ready=12, uw_psum=4, uw_ready=4,
    s_ready=9, sg_ready=8, ws_psum=8, vn_ready=8, su_psum=8, oc_psum=8, og_ready=8, oss=4, orr=4, o_written=4,
    x_added=16, ffn_copied=44, ffn_conv=44, silu_ready=22, g_ready=22,
    g_hi_done=22, g_split=22, g_used=11, down_done=7,
)

LOOK_BACK = ("split", "even_used", "odd_used", "x_added", "ffn_conv")


def pieces():
    return [(u, a) for u in range(N_UNITS) for a in range(2) if (u, a) != (N_UNITS - 1, 1)]


def loads_of(unit):
    return 2 if unit == U_TAIL or U_UP <= unit < U_DN else 1


def trunk(nc, depth, x, positions, attn_norm, w_in, nsa_q_norm, nsa_k_norm, cmp_pe, cmp_w1, cmp_w2, nsa_out_norm,
          gdn_conv_w, gdn_a_log, gdn_dt_bias, gdn_out_norm, w_out, ffn_norm, w_up, ffn_conv_w, ffn_conv_b, w_down, out):
    with ExitStack() as ctx:
        base = (nc.sbuf_base + 31) // 32 * 32
        top = [0]

        def at_word(name, shape, dt, word):
            return nc.alloc_sbuf_tensor_at(name, [P if shape[0] is None else shape[0]] + list(shape[1:]), dt,
                                           offset=base + 4 * word)

        def words(shape, dt=F32):
            n = 1
            for s in shape[1:]:
                n *= s
            return n if dt != BF16 else (n + 1) // 2

        def fixed(name, shape, dt=F32):
            t = at_word(name, shape, dt, top[0])
            top[0] += (words(shape, dt) + 7) // 8 * 8
            return t

        def zone(start, limit):
            pos = [start]

            def place(name, shape, dt=F32):
                t = at_word(name, shape, dt, pos[0])
                pos[0] += (words(shape, dt) + 7) // 8 * 8
                assert pos[0] <= limit, (name, pos[0], limit)
                return t
            return place

        x_res = fixed("x_res", [P, TT_, D])
        raw = fixed("raw", [P, 2, PIECE])
        w_hi = fixed("w_hi", [P, 2, PIECE], F32R)
        w_lo = fixed("w_lo", [P, 2, PIECE], F32R)
        xo = fixed("xo", [P, TT_, D])
        ident = fixed("ident", [P, P])
        ident_bf = fixed("ident_bf", [P, P], BF16)
        causal_bf = fixed("causal_bf", [P, P], BF16)
        ident64 = fixed("ident64", [P, CH])
        upto = fixed("upto", [P, CH])
        sum_upto = fixed("sum_upto", [P, P])
        after = fixed("after", [P, P])
        chunk_rows = fixed("chunk_rows", [P, 2, P])
        level_mask = fixed("level_mask", [P, 6, CH])
        cmp_add = fixed("cmp_add", [P, TT_, 32])
        cmp_mul = fixed("cmp_mul", [P, TT_, 32])
        rope_c = fixed("rope_c", [P, TT_, 16])
        rope_s = fixed("rope_s", [P, TT_, 16])
        minus_half = fixed("minus_half", [P, 64])
        par = fixed("par", [P, 3, P])
        par_bc = fixed("par_bc", [P, 904])
        cmp_w2_sb = fixed("cmp_w2_sb", [P, 2, 2, DH])
        ssum = fixed("ssum", [P, 4])
        rstd = fixed("rstd", [P, 4])
        small = fixed("small", [P, 1024])
        CONV0 = top[0]
        conv_in = fixed("conv_in", [P, 4, 4 + T])
        Z0 = top[0]
        h_hi = at_word("h_hi", [P, KC, T], F32R, Z0)
        h_lo = at_word("h_lo", [P, KC, T], F32R, Z0 + KC * T)
        Z1 = Z0 + 2 * KC * T
        par_rows = at_word("par_rows", [P, 3, P], F32, Z1)
        qkvT = at_word("qkvT", [P, 12, T], F32, Z1)
        pj = at_word("pj", [P, TT_, PJ_W], F32, Z1 + 12 * T)
        g_mlp = at_word("g_mlp", [P, FK, T], F32, Z1)
        Z2 = Z1 + 12 * T + TT_ * PJ_W
        END = (nc.sbuf_usable_end - base) // 4
        late = zone(Z2, END)
        conv_out = late("conv_out", [P, 4, T])
        g_hi = late("g_hi", [P, 2, T], F32R)
        g_lo = late("g_lo", [P, 2, T], F32R)
        low, high, front = zone(Z0, Z1), zone(Z2, END), zone(CONV0, Z0)
        sq_tmp = at_word("sq_tmp", [P, 2, 768], F32, Z2)
        qT = low("qT", [P, 4, T])
        kT = low("kT", [P, 2, T])
        blk = low("blk", [P, 16, 64])
        o_tmp = at_word("o_tmp", [P, 2, NQ], F32, Z0 + 6 * T)
        hid_rows = low("hid_rows", [64, 2, HID])
        hid = low("hid", [P, 2, 2, 64])
        kcT = low("kcT", [P, NG, 32])
        kc_rows = low("kc_rows", [64, DH])
        kc_sq = low("kc_sq", [64, DH])
        kc_two = low("kc_two", [32, P])
        vc_rows = low("vc_rows", [64, DH])
        vc_diag = low("vc_diag", [P, 4 * DH])
        neg_max = low("neg_max", [P, N_ITEMS])
        row_sum = low("row_sum", [P, N_ITEMS])
        c_prob = at_word("c_prob", [P, 2, NH * 32], F32, CONV0)
        c_probT = at_word("c_probT", [P, 2, 2 * P], F32, CONV0 + 512)
        blk_hi = at_word("blk_hi", [P, 16, 64], F32R, CONV0)
        blk_lo = at_word("blk_lo", [P, 16, 64], F32R, CONV0 + 1024)
        prob = front("prob", [P, 2, T])
        probT = front("probT", [P, 2, T])
        formsT = low("formsT", [P, 3, GH, P])
        forms_sb = high("forms_sb", [P, 4, GH, GD])
        inverse = zone(Z2, Z2 + 4 * GW)
        ltT = inverse("ltT", [P, 2 * GH, CH])
        xi = inverse("xi", [P, 2 * GH, CH])
        xiT = inverse("xiT", [P, 2 * GH, CH])
        yy = inverse("yy", [P, 2 * GH, CH])
        raw_qk = high("raw_qk", [P, 2, GH, GD])
        u_sb = at_word("u_sb", [P, 2, GH, GD], F32, Z2 + 4 * GW)
        g_upto = high("g_upto", [P, GH, CH])
        decayT = high("decayT", [P, GH, CH])
        wq = high("wq", [P, 2, GH, 4 * CH])
        akkT = low("akkT", [P, 2 * GH, CH])
        aqkT = high("aqkT", [P, 2 * GH, CH])

        def of_tile(part, r):
            return qkvT[:, GH * part:GH * part + GH, r * P:(r + 1) * P]

        v_new, og, og_sq, state_g = (pj[:, i, 0:GW].rearrange("p (h d) -> p h d", h=GH) for i in range(4))
        state = pj[:, :, 512:512 + GD]

        def sm(lo, n, rows=P):
            return small[0:rows, lo:lo + n]
        qk_ss, qk_rs = sm(0, 48), sm(48, 48)
        gy, gn, gE, bE, aE = sm(96, 16), sm(112, 16), sm(128, 96), sm(224, 16), sm(240, 4)
        gdec, beta, gate = sm(256, 16), sm(272, 16), sm(288, 96)
        ex = sm(384, 64)
        g_ss, g_rr, g_sc = sm(448, 8), sm(456, 8), sm(464, 20)
        o_ss, o_rr = sm(488, 4), sm(496, 4)
        c_max, c_sum, c_coef = sm(512, 8), sm(520, 8), sm(528, 8)
        coef = sm(536, 8)
        no_ss, no_rr = sm(544, 32), sm(576, 32)
        kc_ss, kc_rr = sm(608, 1, 64), sm(616, 1, 64)
        q_gain = sm(640, 64)
        ang, turns, wrap = sm(704, 32), sm(736, 32), sm(768, 32)
        inv_freq = sm(800, 8)
        pos_f = sm(808, 4)
        cosang = sm(816, 32)
        pos_i = at_word("pos_i", [P, 4], I32, CONV0 - 8)

        ps = [ctx.enter_context(nc.psum_tensor(f"bank{b}", [P, 512], F32)) for b in range(8)]

        sems = {n: ctx.enter_context(nc.semaphore(n)) for n in SIGNALS}
        const_ready = ctx.enter_context(nc.semaphore("const_ready"))
        rope_ready = ctx.enter_context(nc.semaphore("rope_ready"))
        rope_steps = ctx.enter_context(nc.semaphore("rope_steps"))
        x_loaded = ctx.enter_context(nc.semaphore("x_loaded"))
        pos_loaded = ctx.enter_context(nc.semaphore("pos_loaded"))
        par_loaded = ctx.enter_context(nc.semaphore("par_loaded"))
        bc_loaded = ctx.enter_context(nc.semaphore("bc_loaded"))
        raw_loaded = [ctx.enter_context(nc.semaphore(f"raw_loaded{i}")) for i in range(2)]
        pool_steps, sp_steps, pe_steps = (ctx.enter_context(nc.semaphore(n)) for n in ("pool_steps", "sp_steps", "pe_steps"))
        out_stored = ctx.enter_context(nc.semaphore("out_stored"))

        def sig(l, name, k):
            return sems[name], l * SIGNALS[name] + k + (1 if name in LOOK_BACK else 0)

        def task_done(l, unit, j):
            before = 0
            for u in range(unit):
                before += 0 if u in (U_CK, U_CV) else 3
            if j == (0 if unit in (U_CK, U_CV) else 3):
                return sig(l, "odd_used", unit + 1)
            return sig(l, "dense_done", before + j + 1)

        loads_layer = [sum(loads_of(u) for u, a in pieces() if a == s) for s in range(2)]

        def piece_loaded(l, p):
            u, a = pieces()[p]
            n = sum(loads_of(v) for v, b in pieces() if b == a and v <= u)
            return raw_loaded[a], (l * loads_layer[a] + n) * 16

        def slot_free(l, p):
            u, a = pieces()[p]
            return sig(l, "odd_used" if a else "even_used", u)

        def kt_used(l, k):
            if k % 2 == 0:
                return sig(l, "g_used", k // 2 + 1)
            p = 2 * U_DN + k // 2
            return sig(l, "odd_used" if p % 2 else "even_used", p // 2 + 1)

        def over(ap, axis, n):
            a = ap.unsqueeze(axis)
            shape = list(a.shape)
            shape[axis] = n
            return a.broadcast_to(shape)

        def h4(ap):
            return ap.rearrange("p (h n) -> p h n", h=GH)

        gain_attn, gain_ffn = par[:, 0, 0:8], par[:, 0, 8:16]
        gdn_taps = par[:, 0, 16:64].rearrange("p (j c) -> p j c", j=4)
        ffn_bias = par[:, 0, 64:108]
        ffn_taps01 = par[:, 1, 0:88].rearrange("p (j c) -> p j c", j=2)
        ffn_tap2 = par[:, 2, 0:44]
        pe_kv = par[:, 2, 44:76].rearrange("p (v m) -> p v m", v=2)
        bc_q, bc_k = par_bc[:, 0:64], par_bc[:, 64:256].rearrange("p (b d) -> p b d", b=3)
        bc_no, bc_go = par_bc[:, 256:768], par_bc[:, 768:896]
        bc_al, bc_dt = par_bc[:, 896:900], par_bc[:, 900:904]

        block = ctx.enter_context(nc.Block())

        @block.sync
        def _(sp):
            for t in range(TT_):
                sp.dma_start(x_res[:, t, :], x[0, t * P:(t + 1) * P, :]).then_inc(x_loaded, 16)
            with nc.allow_non_contiguous_dma(reason="512 positions"):
                sp.dma_start(pos_i[:, :], positions[0].rearrange("(t p) -> p t", p=P)).then_inc(pos_loaded, 16)
            with sp.Fori(0, depth) as l:

                def load(p):
                    u, a = pieces()[p]
                    if p >= 2:
                        sp.wait_ge(*sig(l, "split", p - 1))
                    else:
                        sp.wait_ge(*sig(l, "split", 0))
                    sp.sem_inc(sp_steps, 1)
                    dst = raw[:, a, :]
                    if u in (U_GQ, U_GK, U_GV, U_KV, U_Q, U_Z):
                        col = {U_GQ: C_QKV, U_GK: C_QKV + GW, U_GV: C_QKV + 2 * GW, U_KV: C_KV, U_Q: C_Q, U_Z: C_Z}[u]
                        src = w_in[l].rearrange("(k p) n -> p k n", p=P)
                        parts = [(dst.rearrange("p (k n) -> p k n", k=4), src[:, 4 * a:4 * a + 4, col:col + 512])]
                    elif u == U_TAIL:
                        d = dst[:, 0:4 * 288].rearrange("p (k n) -> p k n", k=4)
                        src = w_in[l].rearrange("(k p) n -> p k n", p=P)[:, 4 * a:4 * a + 4, :]
                        parts = [(d[:, :, 0:280], src[:, :, 1024:1304]), (d[:, :, 280:288], src[:, :, C_AB:C_AB + 8])]
                    elif u in (U_CK, U_CV):
                        src = cmp_w1[l, u - U_CK].rearrange("(m p) n -> p m n", p=P)
                        parts = [(dst.rearrange("p (m n) -> p m n", m=8), src[:, 8 * a:8 * a + 8, :])]
                    elif u < U_UP:
                        c = (u - U_O0) * 512
                        src = w_out[l].rearrange("(k p) n -> p k n", p=P)
                        parts = [(dst.rearrange("p (k n) -> p k n", k=4), src[:, 4 * a:4 * a + 4, c:c + 512])]
                    elif u < U_DN:
                        c = (u - U_UP) * 256
                        src = w_up[l].rearrange("(k p) n -> p k n", p=P)[:, 4 * a:4 * a + 4, :]
                        d = dst.rearrange("p (k s n) -> p k s n", k=4, s=2)
                        parts = [(d[:, :, s, :], src[:, :, s * FF + c:s * FF + c + 256]) for s in range(2)]
                    else:
                        k = 4 * (u - U_DN) + 2 * a
                        src = w_down[l].rearrange("(k p) n -> p k n", p=P)
                        parts = [(dst.rearrange("p (k n) -> p k n", k=2), src[:, k:k + 2, :])]
                    assert len(parts) == loads_of(u)
                    for d, s in parts:
                        sp.dma_start(d, s).then_inc(raw_loaded[a], 16)

                load(0)
                load(1)
                sp.wait_ge(*sig(l, "x_added", 0))
                sp.sem_inc(sp_steps, 1)
                rows = [(0, 0, 8, attn_norm[l].rearrange("(r c) -> r c", c=P)),
                        (0, 8, 8, ffn_norm[l].rearrange("(r c) -> r c", c=P)),
                        (0, 16, 48, gdn_conv_w[l].rearrange("j (r c) -> (j r) c", c=P)),
                        (0, 64, 44, ffn_conv_b[l].rearrange("(r c) -> r c", c=P)),
                        (1, 0, 88, ffn_conv_w[l, 0:2].rearrange("j (r c) -> (j r) c", c=P)),
                        (2, 0, 44, ffn_conv_w[l, 2].rearrange("(r c) -> r c", c=P)),
                        (2, 44, 32, cmp_pe[l].rearrange("v (m s) d -> (v m) (s d)", s=2))]
                for b, r0, n, src in rows:
                    sp.dma_start(par_rows[r0:r0 + n, b, :], src).then_inc(par_loaded, 16)
                vecs = [(0, 64, nsa_q_norm[l]), (64, 192, nsa_k_norm[l].rearrange("b d -> (b d)")),
                        (256, 512, nsa_out_norm[l].rearrange("h d -> (h d)")), (768, 128, gdn_out_norm[l]),
                        (896, 4, gdn_a_log[l]), (900, 4, gdn_dt_bias[l])]
                for c, n, src in vecs:
                    sp.dma_start(par_bc[:, c:c + n], src.partition_broadcast(P)).then_inc(bc_loaded, 16)
                sp.dma_start(cmp_w2_sb[:, :, :, :], cmp_w2[l].rearrange("v (s p) d -> p v s d", p=P)).then_inc(bc_loaded, 16)
                for p in range(2, N_PIECES):
                    load(p)
            for t in range(TT_):
                sp.wait_ge(*sig(depth - 1, "x_added", 8 + 2 * t + 2))
                sp.dma_start(out[0, t * P:(t + 1) * P, :], x_res[:, t, :]).then_inc(out_stored, 16)
            sp.wait_ge(out_stored, 16 * TT_)

        N_PAR, N_BC = 7 * 16, 7 * 16

        @block.gpsimd
        def _(pool):
            for name in LOOK_BACK:
                pool.sem_inc(sems[name], 1)
            for t, v in ((ident, 0.0), (ident64, 0.0), (upto, 1.0), (sum_upto, 0.0), (after, 0.0), (chunk_rows, 0.0),
                         (level_mask, 0.0), (cmp_add, 0.0), (cmp_mul, 1.0), (minus_half, -0.5), (causal_bf, 0.0)):
                pool.memset(t[:], v)
            for i in range(ROPE // 2):
                pool.memset(inv_freq[:, i:i + 1], THETA ** (-2.0 * i / ROPE))
            pool.drain()
            pool.affine_select(out=ident[:, :], in_=ident[:, :], compare_op=ALU.not_equal, fill=1.0, base=0,
                               pattern=[[-1, P]], channel_multiplier=1)
            pool.affine_select(out=causal_bf[:, :], in_=causal_bf[:, :], compare_op=ALU.is_ge, fill=NEG, base=0,
                               pattern=[[-1, P]], channel_multiplier=1)
            for m, v in ((cmp_add, NEG), (cmp_mul, 0.0)):
                pool.affine_select(out=m[:, :, :], in_=m[:, :, :], compare_op=ALU.is_ge, fill=v, base=-(BLK - 1),
                                   pattern=[[P, TT_], [-STRIDE, 32]], channel_multiplier=1)
            for c in range(2):
                r = slice(CH * c, CH * c + CH)
                pool.drain()
                pool.affine_select(out=ident64[r, :], in_=ident64[r, :], compare_op=ALU.not_equal, fill=1.0, base=0,
                                   pattern=[[-1, CH]], channel_multiplier=1)
                pool.affine_select(out=upto[r, :], in_=upto[r, :], compare_op=ALU.is_ge, fill=0.0, base=0,
                                   pattern=[[1, CH]], channel_multiplier=-1)
                pool.memset(sum_upto[r, r], 1.0)
                pool.memset(after[r, r], 1.0)
                pool.memset(chunk_rows[r, c, :], 1.0)
                for k in range(6):
                    s = 1 << k
                    upper = level_mask[r, k, :].rearrange("p (b u s) -> p b u s", u=2, s=s)[:, :, 1, :]
                    pool.memset(upper, 1.0)
            for c in range(2):
                r = slice(CH * c, CH * c + CH)
                pool.drain()
                pool.affine_select(out=sum_upto[r, r], in_=sum_upto[r, r], compare_op=ALU.is_ge, fill=0.0, base=0,
                                   pattern=[[1, CH]], channel_multiplier=-1)
                pool.affine_select(out=after[r, r], in_=after[r, r], compare_op=ALU.is_ge, fill=0.0, base=-1,
                                   pattern=[[-1, CH]], channel_multiplier=1)
                for k in range(6):
                    s = 1 << k
                    upper = level_mask[r, k, :].rearrange("p (b u s) -> p b u s", u=2, s=s)[:, :, 1, :]
                    pool.affine_select(out=upper, in_=upper, compare_op=ALU.is_ge, fill=0.0, base=0,
                                       pattern=[[-2 * s, CH // (2 * s)], [0, s]], channel_multiplier=1)
            for c in range(2):
                r = slice(CH * c, CH * c + CH)
                pool.drain()
                for k in range(6):
                    s = 1 << k
                    upper = level_mask[r, k, :].rearrange("p (b u s) -> p b u s", u=2, s=s)[:, :, 1, :]
                    pool.affine_select(out=upper, in_=upper, compare_op=ALU.is_ge, fill=0.0, base=s - 1,
                                       pattern=[[2 * s, CH // (2 * s)], [0, s]], channel_multiplier=-1)
            pool.drain()
            pool.tensor_copy(ident_bf[:, :], ident[:, :])
            pool.drain().then_inc(const_ready, 1)

            def inverse_root(dst, src, n, rows, scale, done):
                pool.sem_inc(pool_steps, 1)
                pool.tensor_scalar(src, src, scale, EPS, ALU.mult, ALU.add)
                pool.drain()
                pool.tensor_tensor(dst, src, minus_half[0:rows, 0:n], ALU.pow).then_inc(sems[done], 1)

            with pool.Fori(0, depth) as l:
                pool.wait_ge(*sig(l, "squares", 1))
                inverse_root(rstd[:, :], ssum[:, :], 4, P, 1.0 / D, "rstd")
                pool.wait_ge(*sig(l, "qk_squares", 1))
                inverse_root(qk_rs, qk_ss, 48, P, 1.0 / DH, "qk_rstd")

                def deltanet():
                    def output_root(r):
                        pool.wait_ge(*sig(l, "oss", r + 1))
                        inverse_root(o_rr, o_ss, 4, P, 1.0 / GD, "orr")

                    for b in range(2):
                        for r in (2 * b, 2 * b + 1):
                            pool.wait_ge(*sig(l, "raw_ev", r + 1))
                            inverse_root(g_rr, g_ss, 8, P, 1.0, "rr_ready")
                            if r == 2:
                                output_root(1)
                            for _ in range(4):
                                yield
                        for _ in range(13):
                            yield
                        for n in range(4 * b, 4 * b + 4):
                            r, c = n // 2, n % 2
                            pool.wait_ge(*sig(l, "s_ready", n + 1))
                            whole = ex[:, 32 + 16 * c + 4 * r:32 + 16 * c + 4 * r + 4]
                            if n == 0:
                                pool.wait_ge(*sig(l, "gcum_exp", 1))
                            pool.tensor_tensor(state_g, state, over(whole, 2, GD), ALU.mult).then_inc(sems["sg_ready"], 1)
                            if n % 4 == 2:
                                output_root(r - 1)
                            yield
                            yield
                    output_root(3)
                    yield
                    yield

                steps = deltanet()
                for segment in range(7):
                    if segment == 5:
                        pool.wait_ge(*sig(l, "kc_ss", 1))
                        inverse_root(kc_rr, kc_ss, 1, 64, 1.0 / DH, "kc_rstd")
                    next(steps, None)
                for t in range(TT_):
                    next(steps, None)
                for i in range(N_ITEMS):
                    if i >= 16 and i % 16 == 3:
                        pool.wait_ge(*sig(l, "no_ss", i // 16))
                        t = i // 16 - 1
                        inverse_root(no_rr[:, 8 * t:8 * t + 8], no_ss[:, 8 * t:8 * t + 8], 8, P, 1.0 / DH, "no_rstd")
                    next(steps, None)
                pool.wait_ge(*sig(l, "no_ss", TT_))
                inverse_root(no_rr[:, 24:32], no_ss[:, 24:32], 8, P, 1.0 / DH, "no_rstd")
                pool.wait_ge(*sig(l, "squares", 2))
                inverse_root(rstd[:, :], ssum[:, :], 4, P, 1.0 / D, "rstd")

        @block.scalar
        def _(act):
            act.wait_ge(rope_steps, 1)
            act.activation(ang, ang, ACT.Sin)
            act.activation(cosang, cosang, ACT.Sin)
            act.drain().then_inc(rope_ready, 1)
            with act.Fori(0, depth) as l:

                def split_hi(p):
                    if p >= N_PIECES:
                        return
                    act.wait_ge(*piece_loaded(l, p))
                    act.wait_ge(*slot_free(l, p))
                    n = 4 * 288 if p // 2 == U_TAIL else PIECE
                    act.activation(w_hi[:, p % 2, 0:n], raw[:, p % 2, 0:n], ACT.Copy).then_inc(sems["hi_done"], 1)

                def row_squares():
                    for t in range(TT_):
                        act.activation(xo[:, t, :], x_res[:, t, :], ACT.Square, accum_out=ssum[:, t:t + 1])
                    act.drain().then_inc(sems["squares"], 1)

                def h_round(which, gain):
                    for kc in range(KC):
                        act.wait_ge(*sig(l, "hT_psum", 8 * which + kc + 1))
                        if gain is None:
                            act.activation(h_hi[:, kc, :], ps[kc % 4][:, :], ACT.Copy).then_inc(sems["h_hi"], 1)
                        else:
                            act.activation(h_hi[:, kc, :], ps[kc % 4][:, :], ACT.Copy,
                                           scale=gain[:, kc:kc + 1]).then_inc(sems["h_hi"], 1)

                act.wait_ge(x_loaded, 16 * TT_)
                act.wait_ge(*sig(l, "x_added", 0))
                row_squares()
                split_hi(0)
                split_hi(1)
                act.wait_ge(*sig(l, "par_psum", 1))
                for b, n in ((0, 108), (1, 88), (2, 76)):
                    act.activation(par[:, b, 0:n], ps[4][:, b * P:b * P + n], ACT.Copy)
                act.drain().then_inc(sems["par_ready"], 1)
                h_round(0, gain_attn)

                for u in range(U_Z + 1):
                    split_hi(2 * u + 2)
                    if u == U_Q:
                        act.wait_ge(*sig(l, "ga_in", 1))
                        act.activation(gn, gn, ACT.Exp)
                        act.activation(bE.rearrange("p (t h) -> p t h", t=TT_), pj[:, :, PJ_B:PJ_B + 4], ACT.Exp, scale=-1.0)
                        act.activation(gE.rearrange("p (t h) -> p t h", t=TT_), pj[:, :, PJ_G:PJ_G + 24], ACT.Exp, scale=-1.0)
                        act.activation(aE, bc_al, ACT.Exp)
                        act.drain()
                        act.activation(gn, gn, ACT.Ln, bias=1.0).then_inc(sems["ga_exp"], 1)
                    for j in range(4):
                        bank = ps[4 * (u % 2) + j]
                        act.wait_ge(*task_done(l, u, j))
                        if u <= U_GV:
                            if u > 0:
                                act.wait_ge(*sig(l, "gconv", 4 * (u - 1) + j + 1))
                            elif j == 0:
                                act.wait_ge(*sig(l, "ffn_conv", 0))
                            dst, fn = conv_in[:, j, 4:4 + T], ACT.Copy
                            src = bank[:, :]
                        elif u == U_TAIL:
                            dst, src, fn = pj[:, j, 1024:1312], bank[:, 0:288], ACT.Copy
                        elif u == U_KV:
                            dst, src, fn = pj[:, j, 512:1024], bank[:, :], ACT.Copy
                        elif u == U_Q:
                            dst = pj[:, j, 0:512].rearrange("p (n g d) -> p g n d", g=NG, d=DH)
                            src, fn = bank[:, :].rearrange("p (g n d) -> p g n d", g=NG, d=DH), ACT.Copy
                        else:
                            dst, src, fn = xo[:, j, 512:1024], bank[:, :], ACT.Silu
                        act.activation(dst, src, fn).then_inc(sems["proj_evac"], 1)
                    split_hi(2 * u + 3)
                    if u <= U_GV:
                        for j in range(4):
                            act.wait_ge(*sig(l, "gconv", 4 * u + j + 1))
                            act.activation(qkvT[:, 4 * u + j, :], conv_out[:, j, :], ACT.Silu).then_inc(sems["gsilu"], 1)

                act.wait_ge(*sig(l, "gcum_psum", 1))
                act.activation(ex, ps[4][:, 0:64], ACT.Exp).then_inc(sems["gcum_exp"], 1)

                def deltanet():
                    for b in range(2):
                        for r in (2 * b, 2 * b + 1):
                            for f in range(2):
                                act.wait_ge(*sig(l, "raw_psum", 3 * r + f + 1))
                                act.activation(raw_qk[:, f, :, :], h4(ps[5 + f][:, :]), ACT.Copy)
                                for h in range(GH):
                                    act.activation(of_tile(f, r)[:, h, :], ps[5 + f][:, GD * h:GD * h + GD], ACT.Square,
                                                   accum_out=g_ss[:, GH * f + h:GH * f + h + 1])
                            act.drain().then_inc(sems["raw_ev"], 1)
                            yield
                            act.wait_ge(*sig(l, "decay_psum", r + 1))
                            act.activation(decayT[:, :, :], h4(ps[7][:, 0:GH * CH]), ACT.Exp).then_inc(sems["dt_exp"], 1)
                            yield
                            for f in range(3):
                                act.wait_ge(*sig(l, "formsT_psum", 4 * r + f + 1))
                                act.activation(formsT[:, f, :, :], h4(ps[5 + f][:, :]),
                                               ACT.Copy).then_inc(sems["formsT_ready"], 1)
                            yield
                            act.wait_ge(*sig(l, "formsT_psum", 4 * r + 4))
                            act.activation(wq[:, r % 2, :, CH:3 * CH], h4(ps[5][:, :]),
                                           ACT.Copy).then_inc(sems["formsT_ready"], 1)
                            yield
                        yield
                        for k in range(1, 6):
                            act.wait_ge(*sig(l, "y_psum", 6 * b + k + 1))
                            act.activation(yy[:, :, :], ps[5][:, :].rearrange("p (k n) -> p k n", k=2 * GH),
                                           ACT.Copy).then_inc(sems["y_ready"], 1)
                            yield
                            yield
                        act.wait_ge(*sig(l, "uw_psum", 2 * b + 1))
                        act.activation(u_sb[:, 0, :, :], h4(ps[5][:, :]), ACT.Copy)
                        for c in range(2):
                            w_view = ps[6 + c][:, :].rearrange("p (r h n) -> p r h n", r=2, h=GH)
                            act.activation(wq[:, :, :, 3 * c * CH:3 * c * CH + CH], w_view, ACT.Copy)
                        act.drain().then_inc(sems["uw_ready"], 1)
                        yield
                        act.wait_ge(*sig(l, "uw_psum", 2 * b + 2))
                        act.activation(u_sb[:, 1, :, :], h4(ps[5][:, :]), ACT.Copy).then_inc(sems["uw_ready"], 1)
                        yield
                        for n in range(4 * b, 4 * b + 4):
                            r, c = n // 2, n % 2
                            yield
                            act.wait_ge(*sig(l, "oc_psum", n + 1))
                            if c == 0 and r > 0:
                                act.wait_ge(*sig(l, "o_written", r))
                            src = h4(ps[6 + c][CH * (1 - c):CH * (1 - c) + CH, :])
                            act.activation(og[CH * c:CH * c + CH, :, :], src, ACT.Copy)
                            act.activation(og_sq[CH * c:CH * c + CH, :, :], src, ACT.Square)
                            act.drain().then_inc(sems["og_ready"], 1)
                            yield
                    yield
                    yield

                steps = deltanet()

                def keep_turned(i):
                    act.wait_ge(*sig(l, "qkT_psum", i + 1))
                    dst = qT[:, i, :] if i < 4 else kT[:, i - 4, :]
                    act.activation(dst, ps[i % 5][:, :], ACT.Copy).then_inc(sems["qkT_ready"], 1)

                for i in range(5):
                    keep_turned(i)
                next(steps, None)
                keep_turned(5)
                act.wait_ge(*sig(l, "blk_f32", 1))
                act.activation(blk_hi[:, :, :], blk[:, :, :], ACT.Copy).then_inc(sems["blk_hi"], 1)
                next(steps, None)
                for kv in range(2):
                    act.wait_ge(*task_done(l, U_CK + kv, 0))
                    act.activation(hid_rows[:, kv, :], ps[3 + kv][0:64, 0:HID], ACT.Silu).then_inc(sems["hid_silu"], 1)
                    if kv == 0:
                        act.wait_ge(*sig(l, "blk_f32", 2))
                        act.activation(blk_hi[:, :, :], blk[:, :, :], ACT.Copy).then_inc(sems["blk_hi"], 1)
                    split_hi(2 * (U_CK + kv) + 2)
                    split_hi(2 * (U_CK + kv) + 3)
                    next(steps, None)
                act.wait_ge(*sig(l, "hid_psum", 1))
                act.activation(hid[:, :, :, :], ps[0][:, 0:256].rearrange("p (v s n) -> p v s n", v=2, s=2),
                               ACT.Copy).then_inc(sems["hid_ready"], 1)
                next(steps, None)
                next(steps, None)
                act.wait_ge(*sig(l, "kcT_psum", 1))
                for g in range(NG):
                    rows = slice(DH * g, DH * g + DH)
                    act.activation(kcT[rows, g, :], ps[2][rows, 0:32], ACT.Copy)
                act.drain().then_inc(sems["kcT_ready"], 1)
                next(steps, None)
                for t in range(TT_):
                    act.wait_ge(*sig(l, "cs_shift", t + 1))
                    act.activation(c_prob[:, t % 2, :], c_prob[:, t % 2, :], ACT.Exp).then_inc(sems["cs_exp"], 1)
                    act.wait_ge(*sig(l, "cpT_psum", t + 1))
                    act.activation(c_probT[:, t % 2, :], ps[2 + t % 2][:, 0:2 * P], ACT.Copy).then_inc(sems["cpT_ready"], 1)
                    next(steps, None)
                act.wait_ge(*sig(l, "co_psum", TT_))
                def exponentials(i):
                    n = (i // 16 + 1) * P
                    act.wait_ge(*sig(l, "negmax", i + 1))
                    if i >= 2:
                        act.wait_ge(*sig(l, "pT_psum", i - 1))
                    act.activation(prob[:, i % 2, 0:n], ps[i % 2][:, 0:n], ACT.Exp, bias=neg_max[:, i:i + 1],
                                   accum_out=row_sum[:, i:i + 1])
                    act.drain().then_inc(sems["p_ready"], 1)

                exponentials(0)
                for i in range(N_ITEMS):
                    if i + 1 < N_ITEMS:
                        exponentials(i + 1)
                    next(steps, None)

                h_round(1, None)
                for u in (U_O0, U_O0 + 1):
                    split_hi(2 * u + 2)
                    split_hi(2 * u + 3)
                act.wait_ge(*sig(l, "x_added", 8))
                row_squares()
                h_round(2, gain_ffn)
                for i in range(N_UP):
                    u = U_UP + i
                    split_hi(2 * u + 2)
                    for j in range(4):
                        act.wait_ge(*task_done(l, u, j))
                        if i > 0:
                            act.wait_ge(*sig(l, "ffn_conv", 4 * (i - 1) + j + 1))
                        act.activation(conv_in[:, j, 4:4 + T], ps[4 * (u % 2) + j][:, :],
                                       ACT.Copy).then_inc(sems["ffn_copied"], 1)
                    split_hi(2 * u + 3)
                    for j in range(2):
                        act.wait_ge(*sig(l, "ffn_conv", 4 * i + j + 1))
                        act.activation(conv_out[:, j, :], conv_out[:, j, :], ACT.Silu).then_inc(sems["silu_ready"], 1)
                for k in range(FK):
                    act.wait_ge(*sig(l, "g_ready", k + 1))
                    if k >= 2:
                        act.wait_ge(*kt_used(l, k - 2))
                    act.activation(g_hi[:, k % 2, :], g_mlp[:, k, :], ACT.Copy).then_inc(sems["g_hi_done"], 1)
                    if k % 2 == 0 and k > 0:
                        split_hi(2 * U_DN + k // 2 + 1)

        @block.vector
        def _(dve):
            def tt(o, a, b, op):
                return dve.tensor_tensor(o, a, b, op)

            dve.wait_ge(const_ready, 1)
            dve.wait_ge(pos_loaded, 16)
            dve.tensor_copy(pos_f, pos_i[:, :])
            dve.drain()
            a3 = ang.rearrange("p (t i) -> p t i", t=TT_)
            tt(a3, over(pos_f, 2, 8), over(inv_freq, 1, TT_), ALU.mult)
            dve.drain()
            two_pi = 6.283185307179586
            c1 = 6.28125
            c2 = 0.0019350051879882812
            c3 = two_pi - c1 - c2
            magic = 12582912.0
            dve.tensor_scalar(turns, ang, 1.0 / two_pi, magic, ALU.mult, ALU.add)
            dve.drain()
            dve.tensor_scalar(turns, turns, magic, None, ALU.subtract)
            for c in (c1, c2, c3):
                dve.drain()
                dve.scalar_tensor_tensor(out=ang, in0=turns, scalar=-c, in1=ang, op0=ALU.mult, op1=ALU.add)
            dve.drain()
            dve.tensor_scalar(cosang, ang, two_pi / 4, None, ALU.add)
            dve.drain()
            dve.tensor_scalar(wrap, cosang, PI, -two_pi, ALU.is_gt, ALU.mult)
            dve.drain()
            tt(cosang, cosang, wrap, ALU.add)
            dve.drain()
            dve.tensor_scalar(cosang, cosang, PI, -PI, ALU.min, ALU.max)
            dve.tensor_scalar(ang, ang, PI, -PI, ALU.min, ALU.max)
            dve.drain().then_inc(rope_steps, 1)
            dve.wait_ge(rope_ready, 1)
            s3, k3 = ang.rearrange("p (t i) -> p t i", t=TT_), cosang.rearrange("p (t i) -> p t i", t=TT_)
            dve.tensor_scalar(rope_s[:, :, 0:8], s3, -1.0, None, ALU.mult)
            dve.tensor_copy(rope_s[:, :, 8:16], s3)
            dve.tensor_copy(rope_c[:, :, 0:8], k3)
            dve.tensor_copy(rope_c[:, :, 8:16], k3)
            dve.drain()

            with dve.Fori(0, depth) as l:

                def split_lo(p):
                    if p >= N_PIECES:
                        return
                    n = 4 * 288 if p // 2 == U_TAIL else PIECE
                    dve.wait_ge(*sig(l, "hi_done", p + 1))
                    tt(w_lo[:, p % 2, 0:n], raw[:, p % 2, 0:n], w_hi[:, p % 2, 0:n], ALU.subtract).then_inc(sems["split"], 1)

                def normalize(which):
                    dve.wait_ge(*sig(l, "rstd", which + 1))
                    for t in range(TT_):
                        dve.tensor_scalar(xo[:, t, :], x_res[:, t, :], rstd[:, t:t + 1], None,
                                          ALU.mult).then_inc(sems["normed"], 1)

                def h_rest(which, gain):
                    for kc in range(KC):
                        dve.wait_ge(*sig(l, "h_hi", 8 * which + kc + 1))
                        if gain is None:
                            tt(h_lo[:, kc, :], ps[kc % 4][:, :], h_hi[:, kc, :], ALU.subtract).then_inc(sems["h_ready"], 1)
                        else:
                            dve.scalar_tensor_tensor(out=h_lo[:, kc, :], in0=ps[kc % 4][:, :], scalar=gain[:, kc:kc + 1],
                                                     in1=h_hi[:, kc, :], op0=ALU.mult,
                                                     op1=ALU.subtract).then_inc(sems["h_ready"], 1)

                normalize(0)
                dve.memset(conv_in[:, :, 0:4], 0.0)
                split_lo(0)
                split_lo(1)
                dve.wait_ge(*sig(l, "par_ready", 1))
                h_rest(0, gain_attn)
                for u in range(U_GV + 1):
                    split_lo(2 * u + 2)
                    for j in range(4):
                        dve.wait_ge(*sig(l, "proj_evac", 4 * u + j + 1))
                        if u > 0:
                            dve.wait_ge(*sig(l, "gsilu", 4 * (u - 1) + j + 1))
                        col = 4 * u + j
                        dve.tensor_scalar(conv_out[:, j, :], conv_in[:, j, 4:4 + T], gdn_taps[:, 3, col:col + 1], None,
                                          ALU.mult)
                        for s in (1, 2, 3):
                            dve.drain()
                            last = dve.scalar_tensor_tensor(
                                out=conv_out[:, j, :], in0=conv_in[:, j, 4 - s:4 - s + T],
                                scalar=gdn_taps[:, 3 - s, col:col + 1], in1=conv_out[:, j, :], op0=ALU.mult, op1=ALU.add)
                        last.then_inc(sems["gconv"], 1)
                    split_lo(2 * u + 3)
                for u in range(U_TAIL, U_Q + 1):
                    split_lo(2 * u + 2)
                    split_lo(2 * u + 3)
                    if u == U_KV:
                        dve.wait_ge(bc_loaded, (l * 7 + 7) * 16)
                        dve.wait_ge(*sig(l, "proj_evac", 16))
                        y3 = gy.rearrange("p (t h) -> p t h", t=TT_)
                        tt(y3, pj[:, :, PJ_A:PJ_A + 4], over(bc_dt, 1, TT_), ALU.add)
                        dve.drain()
                        dve.tensor_scalar(gn, gy, -1.0, None, ALU.mult)
                        dve.drain()
                        tt(gn, gn, gy, ALU.min).then_inc(sems["ga_in"], 1)
                dve.wait_ge(*sig(l, "ga_exp", 1))
                dve.scalar_tensor_tensor(out=gdec, in0=gy, scalar=0.0, in1=gn, op0=ALU.max, op1=ALU.add)
                dve.tensor_scalar(bE, bE, 1.0, None, ALU.add)
                dve.tensor_scalar(gE, gE, 1.0, None, ALU.add)
                dve.drain()
                g3 = gdec.rearrange("p (t h) -> p t h", t=TT_)
                tt(g3, g3, over(aE, 1, TT_), ALU.mult)
                dve.reciprocal(beta, bE)
                dve.reciprocal(gate, gE)
                dve.drain()
                dve.tensor_scalar(gdec, gdec, -1.0, None, ALU.mult).then_inc(sems["ga_out"], 1)
                gate4 = gate.rearrange("p (t h b) -> p t h b", t=TT_, h=NH)
                dve.tensor_scalar(q_gain, bc_q, float(DH) ** -0.5, None, ALU.mult)
                dve.wait_ge(*sig(l, "proj_evac", 24))

                def heads(ap, n):
                    return ap.rearrange("p (h d) -> p h d", h=n)

                for t in range(TT_):
                    tmp = sq_tmp[:, t % 2, :]
                    kn = pj[:, t, 768:1280].rearrange("p (b v n) -> p b v n", b=2, v=2)[:, :, 0, :]
                    tt(tmp[:, 0:512], pj[:, t, 0:512], pj[:, t, 0:512], ALU.mult)
                    tt(tmp[:, 512:768].rearrange("p (b n) -> p b n", b=2), kn, kn, ALU.mult)
                    dve.drain()
                    dve.tensor_reduce(qk_ss[:, 12 * t:12 * t + 12], heads(tmp, 12), AX.X, ALU.add)
                dve.drain().then_inc(sems["qk_squares"], 1)
                dve.wait_ge(*sig(l, "qk_rstd", 1))
                for t in range(TT_):
                    q = heads(pj[:, t, 0:512], 8)
                    kn = pj[:, t, 768:1280].rearrange("p (b v g d) -> p b v g d", b=2, v=2, g=2)[:, :, 0, :, :]
                    rs = qk_rs[:, 12 * t:12 * t + 12]
                    tt(q, q, over(rs[:, 0:8], 2, DH), ALU.mult)
                    for b in range(2):
                        tt(kn[:, b, :, :], kn[:, b, :, :], over(rs[:, 8 + 2 * b:10 + 2 * b], 2, DH), ALU.mult)
                    dve.drain()
                    tt(q, q, over(q_gain, 1, NH), ALU.mult)
                    for b in range(2):
                        tt(kn[:, b, :, :], kn[:, b, :, :], over(bc_k[:, b + 1, :], 1, NG), ALU.mult)
                    dve.drain()
                    kr = pj[:, t, 512:1280].rearrange("p (b v g d) -> p b v g d", b=3, v=2, g=2)[:, :, 0, :, :]
                    t1, t2 = sq_tmp[:, 0, :], sq_tmp[:, 1, :]
                    parts = [(q, t1[:, 0:128], t2[:, 0:128], NH)]
                    for b in range(3):
                        parts.append((kr[:, b, :, :], t1[:, 128 + 32 * b:160 + 32 * b], t2[:, 128 + 32 * b:160 + 32 * b], NG))
                    for xx, m1, m2, n in parts:
                        m1, m2 = heads(m1, n), heads(m2, n)
                        tt(m1, xx[:, :, 0:16], over(rope_c[:, t, :], 1, n), ALU.mult)
                        tt(m2[:, :, 0:8], xx[:, :, 8:16], over(rope_s[:, t, 0:8], 1, n), ALU.mult)
                        tt(m2[:, :, 8:16], xx[:, :, 0:8], over(rope_s[:, t, 8:16], 1, n), ALU.mult)
                    dve.drain()
                    for xx, m1, m2, n in parts:
                        tt(xx[:, :, 0:16], heads(m1, n), heads(m2, n), ALU.add)
                    dve.drain()
                dve.drain().then_inc(sems["q_ready"], 1)
                split_lo(2 * U_Z + 2)
                split_lo(2 * U_Z + 3)

                def deltanet():
                    lanes = 2 * GH

                    def level(k):
                        tt(ltT[:, :, :], akkT[:, :, :], over(level_mask[:, k, :], 1, lanes), ALU.mult).then_inc(sems["lt_ready"], 1)

                    def lanes_of(bank):
                        return ps[bank][:, :].rearrange("p (k n) -> p k n", k=lanes)

                    def output_squares(r):
                        dve.wait_ge(*sig(l, "og_ready", 2 * r + 2))
                        dve.tensor_reduce(o_ss, og_sq, AX.X, ALU.add).then_inc(sems["oss"], 1)

                    def finish_tile(r):
                        dve.wait_ge(*sig(l, "orr", r + 1))
                        tt(og, og, over(o_rr, 2, GD), ALU.mult)
                        dve.drain()
                        tt(og, og, over(bc_go, 1, GH), ALU.mult)
                        dve.drain()
                        z = h4(xo[:, r, 512:1024])
                        tt(z, og, z, ALU.mult).then_inc(sems["o_written"], 1)

                    for b in range(2):
                        for r in (2 * b, 2 * b + 1):
                            rb = r % 2
                            be = beta[:, 4 * r:4 * r + 4]
                            dve.wait_ge(*sig(l, "raw_psum", 3 * r + 3))
                            tt(of_tile(2, r), h4(ps[7][:, :]), over(be, 2, GD), ALU.mult)
                            tt(g_upto[:, :, :], over(upto[:, :], 1, GH), over(gdec[:, 4 * r:4 * r + 4], 2, CH), ALU.mult)
                            dve.drain().then_inc(sems["vb_ready"], 1)
                            if r == 2:
                                output_squares(1)
                            yield
                            dve.wait_ge(*sig(l, "rr_ready", r + 1))
                            dve.wait_ge(*sig(l, "gcum_exp", 1))
                            e_cum, e_rest = ex[:, 4 * r:4 * r + 4], ex[:, 16 + 4 * r:20 + 4 * r]
                            s_q, s_qg, s_kb, s_kbg, s_kd = (g_sc[:, 4 * i:4 * i + 4] for i in range(5))
                            dve.tensor_scalar(s_q, g_rr[:, 0:4], float(GD) ** -0.5, None, ALU.mult)
                            tt(s_kb, g_rr[:, 4:8], be, ALU.mult)
                            tt(s_kd, g_rr[:, 4:8], e_rest, ALU.mult)
                            dve.drain()
                            tt(s_qg, s_q, e_cum, ALU.mult)
                            tt(s_kbg, s_kb, e_cum, ALU.mult)
                            dve.drain()
                            q_, k_ = raw_qk[:, 0, :, :], raw_qk[:, 1, :, :]
                            for o, src, sc in ((forms_sb[:, 0, :, :], k_, g_rr[:, 4:8]), (forms_sb[:, 1, :, :], k_, s_kb),
                                               (forms_sb[:, 2, :, :], q_, s_q), (forms_sb[:, 3, :, :], q_, s_qg),
                                               (of_tile(0, r), k_, s_kbg), (of_tile(1, r), k_, s_kd)):
                                tt(o, src, over(sc, 2, GD), ALU.mult)
                            dve.drain().then_inc(sems["forms"], 1)
                            if r == 2:
                                finish_tile(1)
                            yield
                            dve.wait_ge(*sig(l, "dt_exp", r + 1))
                            tt(decayT[:, :, :], decayT[:, :, :], over(upto[:, :], 1, GH), ALU.mult)
                            dve.drain()
                            yield
                            dve.wait_ge(*sig(l, "kk_psum", r + 1))
                            kk = ps[6][:, :].rearrange("p (f h n) -> p f h n", f=2, h=GH)
                            tt(akkT[:, GH * rb:GH * rb + GH, :], kk[:, 0, :, :], decayT[:, :, :], ALU.mult)
                            tt(aqkT[:, GH * rb:GH * rb + GH, :], kk[:, 1, :, :], decayT[:, :, :], ALU.mult)
                            dve.drain().then_inc(sems["a_ready"], 1)
                            if rb == 1:
                                level(0)
                                dve.drain()
                                tt(xiT[:, :, :], over(ident64[:, :], 1, lanes), ltT[:, :, :], ALU.subtract)
                            yield
                        dve.wait_ge(*sig(l, "y_psum", 6 * b + 1))
                        tt(xi[:, :, :], over(ident64[:, :], 1, lanes), lanes_of(5), ALU.subtract)
                        dve.drain().then_inc(sems["x_ready"], 1)
                        level(1)
                        yield
                        for k in range(1, 6):
                            yield
                            dve.wait_ge(*sig(l, "p_psum", 5 * b + k))
                            if k < 5:
                                tt(xi[:, :, :], xi[:, :, :], lanes_of(6), ALU.subtract)
                            tt(xiT[:, :, :], xiT[:, :, :], lanes_of(7), ALU.subtract)
                            dve.drain().then_inc(sems["x_ready"], 1)
                            if k < 5:
                                level(k + 1)
                            yield
                        if b == 0:
                            dve.memset(state, 0.0).then_inc(sems["s_ready"], 1)
                        yield
                        yield
                        for n in range(4 * b, 4 * b + 4):
                            r, c = n // 2, n % 2
                            rows = slice(CH * c, CH * c + CH)
                            dve.wait_ge(*sig(l, "ws_psum", n + 1))
                            tt(v_new[rows, :, :], u_sb[rows, r % 2, :, :], h4(ps[6 + c][rows, :]),
                               ALU.subtract).then_inc(sems["vn_ready"], 1)
                            if n % 4 == 2:
                                output_squares(r - 1)
                            yield
                            dve.wait_ge(*sig(l, "su_psum", n + 1))
                            dve.wait_ge(*sig(l, "sg_ready", n + 1))
                            tt(state, state_g, h4(ps[5][:, :]), ALU.add).then_inc(sems["s_ready"], 1)
                            if n % 4 == 2:
                                finish_tile(r - 1)
                            yield
                    output_squares(3)
                    yield
                    finish_tile(3)
                    yield

                steps = deltanet()
                next(steps, None)

                def blocks(kv):
                    dve.wait_ge(*sig(l, "blkT_psum", kv + 1))
                    if kv == 0:
                        dve.memset(blk[:, :, :], 0.0)
                        dve.drain()
                    else:
                        dve.wait_ge(*sig(l, "blk_hi", 1))
                    for g in range(NG):
                        for s in range(2):
                            rows = slice(64 * g, 64 * g + 64)
                            src = ps[1 + kv][rows, :].rearrange("p (n m s) -> p s m n", m=8, s=2)
                            for half in range(2):
                                o = blk[64 * s:64 * s + 64, 8 * half:8 * half + 8, 32 * g:32 * g + 31]
                                pe_b = over(pe_kv[64 * s:64 * s + 64, kv, 8 * half:8 * half + 8], 2, 31)
                                tt(o, src[:, s, :, half:half + 31], pe_b, ALU.add)
                    dve.drain().then_inc(sems["blk_f32"], 1)
                    dve.wait_ge(*sig(l, "blk_hi", kv + 1))
                    tt(blk_lo[:, :, :], blk[:, :, :], blk_hi[:, :, :], ALU.subtract).then_inc(sems["blk_ready"], 1)

                blocks(0)
                next(steps, None)
                blocks(1)
                split_lo(2 * U_CV)
                split_lo(2 * U_CV + 1)
                next(steps, None)
                split_lo(2 * U_O0)
                split_lo(2 * U_O0 + 1)
                next(steps, None)
                next(steps, None)
                dve.wait_ge(*sig(l, "cmp2_psum", 1))
                dve.tensor_copy(kc_rows[:, :], ps[1][0:64, 0:DH])
                dve.tensor_copy(vc_rows[:, :], ps[1][0:64, DH:2 * DH])
                dve.memset(vc_diag[:, :], 0.0)
                dve.memset(kcT[:, :, :], 0.0)
                dve.drain()
                tt(kc_sq[:, :], kc_rows[:, :], kc_rows[:, :], ALU.mult)
                dve.drain()
                dve.tensor_reduce(kc_ss, kc_sq[:, :], AX.X, ALU.add).then_inc(sems["kc_ss"], 1)
                for h in range(4):
                    g = h % NG
                    dve.tensor_copy(vc_diag[32 * h:32 * h + 32, DH * h:DH * h + DH], vc_rows[32 * g:32 * g + 32, :])
                dve.drain().then_inc(sems["vc_ready"], 1)
                next(steps, None)
                dve.wait_ge(*sig(l, "kc_rstd", 1))
                dve.scalar_tensor_tensor(out=kc_rows[:, :], in0=kc_rows[:, :], scalar=kc_rr, in1=bc_k[0:64, 0, :],
                                         op0=ALU.mult, op1=ALU.mult)
                dve.drain()
                for g in range(NG):
                    dve.tensor_copy(kc_two[:, DH * g:DH * g + DH], kc_rows[32 * g:32 * g + 32, :])
                dve.drain().then_inc(sems["kc_ready"], 1)
                next(steps, None)
                for t in range(TT_):
                    cp = heads(c_prob[:, t % 2, :], NH)
                    dve.wait_ge(*sig(l, "cs_psum", t + 1))
                    tt(cp, heads(ps[t % 2][:, 0:256], NH), over(cmp_add[:, t, :], 1, NH), ALU.add)
                    dve.drain()
                    dve.tensor_reduce(c_max, cp, AX.X, ALU.max)
                    dve.drain()
                    tt(cp, cp, over(c_max, 2, 32), ALU.subtract).then_inc(sems["cs_shift"], 1)
                    dve.wait_ge(*sig(l, "cs_exp", t + 1))
                    tt(cp, cp, over(cmp_mul[:, t, :], 1, NH), ALU.mult).then_inc(sems["cp_ready"], 1)
                    dve.drain()
                    dve.tensor_reduce(c_sum, cp, AX.X, ALU.add)
                    dve.drain()
                    dve.tensor_scalar(c_sum, c_sum, 1e-30, None, ALU.max)
                    dve.drain()
                    dve.reciprocal(c_coef, c_sum)
                    dve.drain()
                    cc = c_coef.rearrange("p (n g) -> p n g", g=NG)
                    tt(cc, cc, gate4[:, t, :, 0].rearrange("p (g n) -> p n g", g=NG), ALU.mult)
                    dve.drain()
                    dve.wait_ge(*sig(l, "co_psum", t + 1))
                    tt(xo[:, t, 0:512].rearrange("p (g n d) -> p n g d", g=NG, d=DH),
                       ps[4][:, :].rearrange("p (n g d) -> p n g d", g=NG, d=DH), over(cc, 3, DH),
                       ALU.mult).then_inc(sems["o_init"], 1)
                    next(steps, None)

                def add_branch(k):
                    t, b = k // 2, k % 2
                    dve.reciprocal(coef, row_sum[:, 8 * k:8 * k + 8])
                    dve.drain()
                    tt(coef, coef, gate4[:, t, :, 1 + b], ALU.mult)
                    dve.drain()
                    dve.wait_ge(*sig(l, "pv_done", 8 * k + 8))
                    tt(heads(o_tmp[:, k % 2, :], NH), heads(ps[4][:, :], NH), over(coef, 2, DH),
                       ALU.mult).then_inc(sems["o_added"], 1)
                    dve.drain()
                    tt(xo[:, t, 0:512], xo[:, t, 0:512], o_tmp[:, k % 2, :], ALU.add)

                def norm_squares(t):
                    dve.drain()
                    tt(o_tmp[:, t % 2, :], xo[:, t, 0:512], xo[:, t, 0:512], ALU.mult)
                    dve.drain()
                    dve.tensor_reduce(no_ss[:, 8 * t:8 * t + 8], heads(o_tmp[:, t % 2, :], NH), AX.X,
                                      ALU.add).then_inc(sems["no_ss"], 1)
                    dve.drain()

                def norm_scale(t):
                    dve.wait_ge(*sig(l, "no_rstd", t + 1))
                    o = heads(xo[:, t, 0:512], NH)
                    tt(o, o, over(no_rr[:, 8 * t:8 * t + 8], 2, DH), ALU.mult)
                    dve.drain()
                    tt(xo[:, t, 0:512], xo[:, t, 0:512], bc_no, ALU.mult)

                def row_max(i):
                    n = (i // 16 + 1) * P
                    dve.wait_ge(*sig(l, "s_psum", i + 1))
                    dve.tensor_reduce(neg_max[:, i:i + 1], ps[i % 2][:, 0:n], AX.X, ALU.max,
                                      negate=True).then_inc(sems["negmax"], 1)

                row_max(0)
                row_max(1)
                for i in range(N_ITEMS):
                    n = (i // 16 + 1) * P
                    dve.wait_ge(*sig(l, "pT_psum", i + 1))
                    if i >= 2:
                        dve.wait_ge(*sig(l, "pv_done", i - 1))
                    dve.tensor_copy(probT[:, i % 2, 0:n], ps[2 + i % 2][:, 0:n]).then_inc(sems["pT_ready"], 1)
                    next(steps, None)
                    if i + 2 < N_ITEMS:
                        row_max(i + 2)
                    if i >= 8 and i % 8 == 0:
                        add_branch(i // 8 - 1)
                    if i >= 16 and i % 16 == 3:
                        norm_squares(i // 16 - 1)
                    if i >= 16 and i % 16 == 5:
                        norm_scale(i // 16 - 1)
                add_branch(7)
                norm_squares(3)
                norm_scale(3)
                dve.drain().then_inc(sems["o_final"], 1)
                dve.drain()
                dve.memset(conv_in[:, :, 0:4], 0.0)
                h_rest(1, None)
                for u in (U_O0, U_O0 + 1):
                    split_lo(2 * u + 2)
                    split_lo(2 * u + 3)
                    c = (u - U_O0) * 512
                    for j in range(4):
                        dve.wait_ge(*task_done(l, u, j))
                        xs = x_res[:, j, c:c + 512]
                        tt(xs, xs, ps[4 * (u % 2) + j][:, :], ALU.add).then_inc(sems["x_added"], 1)
                normalize(1)
                h_rest(2, gain_ffn)
                for i in range(N_UP):
                    u = U_UP + i
                    split_lo(2 * u + 2)
                    for j in range(4):
                        col = 2 * i + j if j < 2 else FK + 2 * i + j - 2
                        dve.wait_ge(*sig(l, "ffn_copied", 4 * i + j + 1))
                        dve.tensor_scalar(conv_out[:, j, :], conv_in[:, j, 4:4 + T], ffn_tap2[:, col:col + 1],
                                          ffn_bias[:, col:col + 1], ALU.mult, ALU.add)
                        for s in (1, 2):
                            dve.drain()
                            dve.scalar_tensor_tensor(
                                out=conv_out[:, j, :], in0=conv_in[:, j, 4 - s:4 - s + T],
                                scalar=ffn_taps01[:, 2 - s, col:col + 1], in1=conv_out[:, j, :], op0=ALU.mult, op1=ALU.add)
                        dve.drain().then_inc(sems["ffn_conv"], 1)
                    split_lo(2 * u + 3)
                    for j in range(2):
                        dve.wait_ge(*sig(l, "silu_ready", 2 * i + j + 1))
                        tt(g_mlp[:, 2 * i + j, :], conv_out[:, j, :], conv_out[:, 2 + j, :],
                           ALU.mult).then_inc(sems["g_ready"], 1)
                    dve.drain()
                for k in range(FK):
                    dve.wait_ge(*sig(l, "g_hi_done", k + 1))
                    tt(g_lo[:, k % 2, :], g_mlp[:, k, :], g_hi[:, k % 2, :], ALU.subtract).then_inc(sems["g_split"], 1)
                    if k % 2 == 0 and k > 0:
                        split_lo(2 * U_DN + k // 2 + 1)
                for i in range(8):
                    if i < 7:
                        dve.wait_ge(*sig(l, "down_done", i + 1))
                    else:
                        dve.wait_ge(*sig(l, "even_used", N_UNITS))
                    xs = x_res[:, i // 2, (i % 2) * 512:(i % 2) * 512 + 512]
                    tt(xs, xs, ps[i][:, :], ALU.add).then_inc(sems["x_added"], 1)

        @block.tensor
        def _(pe):
            def three(o, a, b, start, stop):
                pe.matmul(o, a[0], b[0], start=start, stop=False)
                pe.matmul(o, a[0], b[1], start=False, stop=False)
                return pe.matmul(o, a[1], b[0], start=False, stop=stop)

            pe.wait_ge(const_ready, 1)
            with pe.Fori(0, depth) as l:

                def turn_rows(which, ready):
                    for kc in range(KC):
                        if kc >= 4:
                            pe.wait_ge(*sig(l, "h_ready", 8 * which + kc - 3))
                        for t in range(TT_):
                            if kc == 0:
                                ready(t)
                            last = pe.transpose(ps[kc % 4][:, t * P:(t + 1) * P], xo[:, t, kc * P:(kc + 1) * P], ident[:, :])
                        last.then_inc(sems["hT_psum"], 1)

                def dense(u, which, bank_free):
                    up = U_UP <= u < U_DN
                    channels = u <= U_GV or up
                    width = 288 if u == U_TAIL else 512
                    for a in range(2):
                        pe.wait_ge(*sig(l, "split", 2 * u + a + 1))
                        hi = w_hi[:, a, 0:4 * width].rearrange("p (k n) -> p k n", k=4)
                        lo = w_lo[:, a, 0:4 * width].rearrange("p (k n) -> p k n", k=4)
                        for j in range(4):
                            if a == 0:
                                bank_free(j)
                            bank = ps[4 * (u % 2) + j]
                            for k in range(4):
                                kc = 4 * a + k
                                if j == 0:
                                    pe.wait_ge(*sig(l, "h_ready", 8 * which + kc + 1))
                                h = (h_hi[:, kc, :], h_lo[:, kc, :])
                                st, sp_ = kc == 0, kc == KC - 1
                                if channels:
                                    w = (hi[:, k, P * j:P * j + P], lo[:, k, P * j:P * j + P])
                                    last = three(bank[:, :], w, h, st, sp_)
                                else:
                                    h = (h[0][:, P * j:P * j + P], h[1][:, P * j:P * j + P])
                                    last = three(bank[:, 0:width], h, (hi[:, k, :], lo[:, k, :]), st, sp_)
                            if a == 1 and j < 3:
                                last.then_inc(sems["dense_done"], 1)
                        last.then_inc(sems["odd_used" if a else "even_used"], 1)

                def wait(name, k):
                    pe.wait_ge(*sig(l, name, k))

                pe.wait_ge(par_loaded, (l * 7 + 7) * 16)
                wait("x_added", 0)
                for b, n in ((0, 108), (1, 88), (2, 76)):
                    last = pe.transpose(ps[4][:, b * P:b * P + n], par_rows[0:n, b, :], ident[0:n, 0:n])
                last.then_inc(sems["par_psum"], 1)
                turn_rows(0, lambda t: wait("normed", t + 1))
                wait("par_ready", 1)
                for u in range(U_Z + 1):
                    if u >= 2:
                        dense(u, 0, lambda j: wait("proj_evac", 4 * (u - 2) + j + 1))
                    elif u == 0:
                        dense(u, 0, lambda j: wait("h_ready", 4 + j + 1))
                    else:
                        dense(u, 0, lambda j: None)

                wait("ga_out", 1)
                for i, m in enumerate((sum_upto[:, :], after[:, :], chunk_rows[:, 0, :], chunk_rows[:, 1, :])):
                    last = pe.matmul(ps[4][:, 16 * i:16 * i + 16], m, gdec, start=True, stop=True)
                last.then_inc(sems["gcum_psum"], 1)

                def deltanet():
                    def lanes_mm(bank, lhs, rhs):
                        pe.sem_inc(pe_steps, 1)
                        for k in range(2 * GH):
                            for c in range(2):
                                rows = slice(CH * c, CH * c + CH)
                                r_ = rhs[rows, k, :] if rhs is not None else ident64[rows, :]
                                last = pe.matmul(ps[bank][rows, CH * k:CH * k + CH], lhs[rows, k, :], r_,
                                                 start=True, stop=True)
                        return last

                    wait("gsilu", 12)
                    for b in range(2):
                        for r in (2 * b, 2 * b + 1):
                            rb = r % 2
                            if r == 2:
                                wait("og_ready", 4)
                                wait("s_ready", 5)
                            elif rb == 1:
                                wait("formsT_ready", 4 * r)
                                wait("a_ready", r)
                            for f in range(3):
                                for h in range(GH):
                                    last = pe.transpose(ps[5 + f][:, P * h:P * h + P],
                                                        qkvT[:, GH * f + h, r * P:(r + 1) * P], ident[:, :])
                                last.then_inc(sems["raw_psum"], 1)
                            yield
                            wait("vb_ready", r + 1)
                            pe.matmul(ps[7][:, 0:GH * CH], after[:, :], g_upto[:, :, :].rearrange("p h n -> p (h n)"),
                                      start=True, stop=True).then_inc(sems["decay_psum"], 1)
                            yield
                            wait("forms", r + 1)
                            for f in range(3):
                                if f == 2:
                                    wait("dt_exp", r + 1)
                                for h in range(GH):
                                    last = pe.transpose(ps[5 + f][:, P * h:P * h + P], forms_sb[:, f, h, :], ident[:, :])
                                last.then_inc(sems["formsT_psum"], 1)
                            yield
                            wait("formsT_ready", 4 * r + 1)
                            for h in range(GH):
                                last = pe.transpose(ps[5][:, P * h:P * h + P], forms_sb[:, 3, h, :], ident[:, :])
                            last.then_inc(sems["formsT_psum"], 1)
                            wait("formsT_ready", 4 * r + 3)
                            pe.sem_inc(pe_steps, 1)
                            for f, other in ((0, 1), (1, 2)):
                                for h in range(GH):
                                    for c in range(2):
                                        rows = slice(CH * c, CH * c + CH)
                                        last = pe.matmul(ps[6][rows, 256 * f + CH * h:256 * f + CH * h + CH],
                                                         formsT[:, 0, h, rows], formsT[:, other, h, rows], start=True, stop=True)
                            last.then_inc(sems["kk_psum"], 1)
                            yield
                        wait("lt_ready", 6 * b + 1)
                        wait("formsT_ready", 8 * b + 8)
                        lanes_mm(5, ltT, None).then_inc(sems["y_psum"], 1)
                        yield
                        for k in range(1, 6):
                            wait("lt_ready", 6 * b + k + 1)
                            wait("x_ready", 6 * b + k)
                            lanes_mm(5, ltT, xi).then_inc(sems["y_psum"], 1)
                            yield
                            wait("y_ready", 5 * b + k)
                            if k < 5:
                                lanes_mm(6, xiT, yy)
                            lanes_mm(7, yy, xiT).then_inc(sems["p_psum"], 1)
                            yield
                        wait("x_ready", 6 * b + 6)
                        pe.sem_inc(pe_steps, 1)
                        for rb in range(2):
                            r = 2 * b + rb
                            if rb == 1:
                                wait("uw_ready", 2 * b + 1)
                                pe.sem_inc(pe_steps, 1)
                            for h in range(GH):
                                for c in range(2):
                                    rows = slice(CH * c, CH * c + CH)
                                    last = pe.matmul(ps[5][rows, P * h:P * h + P], xiT[rows, GH * rb + h, :],
                                                     of_tile(2, r)[rows, h, :], start=True, stop=True)
                            if rb == 0:
                                for r2 in range(2):
                                    for h in range(GH):
                                        for c in range(2):
                                            rows = slice(CH * c, CH * c + CH)
                                            col = 256 * r2 + CH * h
                                            last = pe.matmul(ps[6 + c][:, col:col + CH], of_tile(0, 2 * b + r2)[rows, h, :],
                                                             xiT[rows, GH * r2 + h, :], start=True, stop=True)
                            last.then_inc(sems["uw_psum"], 1)
                            yield
                        for n in range(4 * b, 4 * b + 4):
                            r, c = n // 2, n % 2
                            rb = r % 2
                            rows, other = slice(CH * c, CH * c + CH), slice(CH * (1 - c), CH * (1 - c) + CH)
                            bank = ps[6 + c]
                            wait("uw_ready", 2 * b + 2)
                            wait("s_ready", n + 1)
                            if n % 4 >= 2:
                                wait("og_ready", n - 1)
                            for h in range(GH):
                                last = pe.matmul(bank[:, P * h:P * h + P], wq[:, rb, h, P * c:P * c + P], state[:, h, :],
                                                 start=h == 0, stop=False, skip_group_check=True)
                            last.then_inc(sems["ws_psum"], 1)
                            yield
                            wait("vn_ready", n + 1)
                            for h in range(GH):
                                last = pe.matmul(ps[5][:, P * h:P * h + P], of_tile(1, r)[rows, h, :], v_new[rows, h, :],
                                                 start=True, stop=True)
                            last.then_inc(sems["su_psum"], 1)
                            for h in range(GH):
                                last = pe.matmul(bank[other, P * h:P * h + P], aqkT[rows, GH * rb + h, :], v_new[rows, h, :],
                                                 start=False, stop=h == GH - 1, skip_group_check=True)
                            last.then_inc(sems["oc_psum"], 1)
                            yield
                    yield
                    yield

                steps = deltanet()

                wait("proj_evac", 28)
                wait("q_ready", 1)
                for p in range(4):
                    for t in range(TT_):
                        last = pe.transpose(ps[p][:, t * P:(t + 1) * P], pj[:, t, P * p:P * p + P], ident[:, :])
                    last.then_inc(sems["qkT_psum"], 1)
                wait("gcum_exp", 1)
                for i, (bank, col) in enumerate(((4, 768), (0, 1024), (1, 512), (2, 640))):
                    if i > 0:
                        wait("qkT_ready", i)
                    for t in range(TT_):
                        last = pe.transpose(ps[bank][:, t * P:(t + 1) * P], pj[:, t, col:col + P], ident[:, :])
                    last.then_inc(sems["qkT_psum" if i < 2 else "blkT_psum"], 1)
                    if i == 0:
                        next(steps, None)
                next(steps, None)
                for kv in range(2):
                    u = U_CK + kv
                    wait("blk_ready", kv + 1)
                    wait("qkT_ready", 4 + kv)
                    for a in range(2):
                        wait("split", 2 * u + a + 1)
                        pe.sem_inc(pe_steps, 1)
                        hi = w_hi[:, a, :].rearrange("p (m n) -> p m n", m=8)
                        lo = w_lo[:, a, :].rearrange("p (m n) -> p m n", m=8)
                        for m in range(8):
                            last = three(ps[3 + kv][0:64, 0:HID], (blk_hi[:, 8 * a + m, :], blk_lo[:, 8 * a + m, :]),
                                         (hi[:, m, :], lo[:, m, :]), a == 0 and m == 0, a == 1 and m == 7)
                        last.then_inc(sems["odd_used" if a else "even_used"], 1)
                    next(steps, None)
                wait("hid_silu", 2)
                wait("qkT_ready", 6)
                pe.sem_inc(pe_steps, 1)
                for kv in range(2):
                    for s in range(2):
                        c = 64 * (2 * kv + s)
                        last = pe.transpose(ps[0][:, c:c + 64], hid_rows[:, kv, P * s:P * s + P], ident[0:64, 0:64])
                last.then_inc(sems["hid_psum"], 1)
                next(steps, None)
                pe.wait_ge(bc_loaded, (l * 7 + 7) * 16)
                wait("hid_ready", 1)
                wait("blk_f32", 1)
                pe.sem_inc(pe_steps, 1)
                for kv in range(2):
                    for s in range(2):
                        last = pe.matmul(ps[1][0:64, DH * kv:DH * kv + DH], hid[:, kv, s, :], cmp_w2_sb[:, kv, s, :],
                                         start=s == 0, stop=s == 1)
                last.then_inc(sems["cmp2_psum"], 1)
                next(steps, None)
                wait("blk_f32", 2)
                wait("kc_ready", 1)
                pe.sem_inc(pe_steps, 1)
                pe.transpose(ps[2][:, 0:32], kc_two[:, :], ident[0:32, 0:32]).then_inc(sems["kcT_psum"], 1)
                next(steps, None)

                def half(h):
                    return slice(64 * (h // 4), 64 * (h // 4) + 64)

                wait("kcT_ready", 1)
                wait("vc_ready", 1)

                def c_scores(t):
                    if t >= 2:
                        wait("cs_shift", t - 1)
                    for n in range(NH // NG):
                        last = pe.matmul(ps[t % 2][:, 64 * n:64 * n + 64], qT[:, n, t * P:(t + 1) * P],
                                         kcT[:, :, :].rearrange("p g n -> p (g n)"), start=True, stop=True)
                    last.then_inc(sems["cs_psum"], 1)

                c_scores(0)
                c_scores(1)
                for t in range(TT_):
                    wait("cp_ready", t + 1)
                    if t >= 2:
                        wait("cpT_ready", t - 1)
                    for g in range(NG):
                        last = pe.transpose(ps[2 + t % 2][:, P * g:P * g + P], c_prob[:, t % 2, P * g:P * g + P], ident[:, :])
                    last.then_inc(sems["cpT_psum"], 1)
                    if t + 2 < TT_:
                        c_scores(t + 2)
                    wait("cpT_ready", t + 1)
                    if t >= 1:
                        wait("o_init", t)
                    for g in range(NG):
                        last = pe.matmul(ps[4][:, 256 * g:256 * g + 256], c_probT[:, t % 2, P * g:P * g + P],
                                         vc_diag[:, :], start=True, stop=True)
                    last.then_inc(sems["co_psum"], 1)
                    next(steps, None)

                wait("cs_shift", 4)

                def scores(i):
                    t, b, h = i // 16, i // 8 % 2, i % 8
                    if i >= 2:
                        wait("p_ready", i - 1)
                    n = (t + 1) * P
                    pe.matmul(ps[i % 2][:, 0:n], qT[half(h), h % 4, t * P:(t + 1) * P], kT[half(h), b, 0:n],
                              start=True, stop=False)
                    pe.matmul(ps[i % 2][:, t * P:n], ident_bf[:, :], causal_bf[:, :],
                              start=False, stop=True).then_inc(sems["s_psum"], 1)

                def turn(i):
                    t = i // 16
                    wait("p_ready", i + 1)
                    if i >= 2:
                        wait("pT_ready", i - 1)
                    for j in range(t + 1):
                        last = pe.transpose(ps[2 + i % 2][:, j * P:(j + 1) * P], prob[:, i % 2, j * P:(j + 1) * P], ident[:, :])
                    last.then_inc(sems["pT_psum"], 1)

                def weigh(i):
                    t, b, h = i // 16, i // 8 % 2, i % 8
                    k = i // 8
                    wait("pT_ready", i + 1)
                    if i == 0:
                        wait("o_init", 4)
                    elif i % 8 == 0:
                        wait("o_added", k)
                    col = 512 + 256 * (b + 1) + 128 + DH * (h // 4)
                    for j in range(t + 1):
                        last = pe.matmul(ps[4][:, DH * h:DH * h + DH], probT[:, i % 2, j * P:(j + 1) * P],
                                         pj[:, j, col:col + DH], start=j == 0, stop=j == t)
                    last.then_inc(sems["pv_done"], 1)

                scores(0)
                scores(1)
                for i in range(N_ITEMS):
                    turn(i)
                    next(steps, None)
                    if i + 2 < N_ITEMS:
                        scores(i + 2)
                    if i >= 1:
                        weigh(i - 1)
                weigh(N_ITEMS - 1)

                wait("o_written", 4)
                wait("o_final", 1)
                turn_rows(1, lambda t: None)
                for u in (U_O0, U_O0 + 1):
                    dense(u, 1, lambda j: None)
                turn_rows(2, lambda t: wait("normed", 4 + t + 1))
                for i in range(N_UP):
                    u = U_UP + i
                    dense(u, 2, (lambda j: wait("ffn_copied", 4 * (i - 2) + j + 1)) if i >= 2 else (lambda j: None))
                for k in range(FK):
                    p = 2 * U_DN + k // 2
                    a = p % 2
                    if k % 2 == 0:
                        wait("split", p + 1)
                    wait("g_split", k + 1)
                    cols = slice((k % 2) * 1024, (k % 2) * 1024 + 1024)
                    hi, lo = w_hi[:, a, cols], w_lo[:, a, cols]
                    for i in range(8):
                        if k == 0 and i % 2 == 0:
                            wait("ffn_copied", 44)
                        j, c = i // 2, slice((i % 2) * 512, (i % 2) * 512 + 512)
                        g = (g_hi[:, k % 2, P * j:P * j + P], g_lo[:, k % 2, P * j:P * j + P])
                        last = three(ps[i][:, :], g, (hi[:, c], lo[:, c]), k == 0, k == FK - 1)
                        if k == FK - 1 and i < 7:
                            last.then_inc(sems["down_done"], 1)
                    last.then_inc(sems["g_used" if k % 2 == 0 else "odd_used" if a else "even_used"], 1)


def kernel(**inputs):
    import numpy as np
    import concourse.bacc as bacc
    from concourse.bass_utils import run_bass_kernel_spmd

    names = ["x", "positions", "attn_norm", "w_in", "nsa_q_norm", "nsa_k_norm", "cmp_pe", "cmp_w1", "cmp_w2",
             "nsa_out_norm", "gdn_conv_w", "gdn_a_log", "gdn_dt_bias", "gdn_out_norm", "w_out", "ffn_norm", "w_up",
             "ffn_conv_w", "ffn_conv_b", "w_down"]
    nc = bacc.Bacc("TRN2", target_bir_lowering=False, num_devices=1)
    arrays = {n: np.ascontiguousarray(inputs[n]) for n in names}
    aps = [nc.dram_tensor(f"in_{n}", arrays[n].shape, mybir.dt.from_np(arrays[n].dtype), kind="ExternalInput").ap()
           for n in names]
    out = nc.dram_tensor("out", arrays["x"].shape, F32, kind="ExternalOutput").ap()
    trunk(nc, arrays["w_in"].shape[0], *aps, out)
    r = run_bass_kernel_spmd(nc, [{f"in_{n}": arrays[n] for n in names}], core_ids=[0])
    return r.results[0]["out"]
```

```python
from contextlib import ExitStack

import concourse.bass as bass
from concourse import mybir

F32 = mybir.dt.float32
F32R = mybir.dt.float32r
BF16 = mybir.dt.bfloat16
I32 = mybir.dt.int32
ALU = mybir.AluOpType
ACT = mybir.ActivationFunctionType
AX = mybir.AxisListType

P = 128
D = 1024
T = 512
TT_ = T // P
KC = D // P
NH, DH, NG = 8, 64, 2
NQ = NH * DH
NKV = 3 * 2 * NG * DH
GH, GD, CH = 4, 128, 64
GW = GH * GD
BLK, STRIDE, HID = 32, 16, 256
FF = 2816
FK = FF // P
EPS = 1e-6
THETA, ROPE = 500000.0, 16
NEG = -1e30
PI = 3.1415925
C_Q, C_KV, C_G, C_QKV, C_AB, C_Z = 0, 512, 1280, 1304, 2840, 2848
PJ_W = NQ + NKV + NH * 3 + 2 * GH
PJ_G, PJ_A, PJ_B = 1280, 1304, 1308

PIECE = 2048
U_GQ, U_GK, U_GV, U_TAIL, U_KV, U_Q, U_Z, U_CK, U_CV, U_O0, U_UP, U_DN = 0, 1, 2, 3, 4, 5, 6, 7, 8, 9, 11, 22
N_UP, N_UNITS = 11, 28
N_PIECES = 2 * N_UNITS - 1
N_ITEMS = TT_ * 2 * NH

SIGNALS = dict(
    even_used=28, odd_used=27, hi_done=N_PIECES, split=N_PIECES, dense_done=3 * 20,
    squares=8, rstd=8, normed=8, params_free=1, hT_psum=24, h_hi=24, h_ready=24,
    proj_evac=28, gconv=12, gsilu=12, par_psum=1, par_ready=1,
    qk_squares=2, qk_rstd=2, q_ready=1, qkT_psum=6, qkT_ready=6, blkT_psum=2, blk_f32=2, blk_hi=2, blk_ready=2,
    hid_silu=2, hid_psum=1, hid_ready=1, cmp2_psum=1, stack_hi=1, q_stacked=1, k_stacked=1, kc_ss=1, kc_rstd=1, kc_ready=1, kcT_psum=1, kcT_ready=1, vc_ready=1,
    cs_psum=2, cs_shift=2, cs_exp=2, cp_ready=2, cpT_psum=2, cpT_ready=2, co_psum=4, o_init=4,
    s_psum=N_ITEMS, negmax=N_ITEMS, p_ready=N_ITEMS, pT_psum=N_ITEMS, pT_ready=N_ITEMS, pv_done=N_ITEMS, o_added=8,
    no_ss=TT_, no_rstd=TT_, o_final=TT_,
    ga_in=1, ga_exp=1, ga_out=1, gcum_psum=1, gcum_exp=1,
    raw_psum=12, raw_ev=4, rr_ready=4, vb_ready=4, decay_psum=4, dt_exp=4, forms=4, formsT_psum=16, formsT_ready=16,
    kk_psum=4, a_ready=4,
    lt_ready=12, y_psum=12, y_ready=10, xi_psum=8, xiT_psum=10, xi_ready=10, xiT_ready=12, uw_psum=4, uw_ready=4,
    s_ready=9, sg_ready=8, ws_psum=8, vn_ready=8, su_psum=8, oc_psum=8, og_ready=8, oss=4, orr=4, o_written=4,
    x_added=16, ffn_copied=44, ffn_conv=44, silu_ready=22, g_ready=22,
    g_hi_done=22, g_split=22, g_used=11, down_done=7,
)

LOOK_BACK = ("split", "even_used", "odd_used", "x_added", "ffn_conv", "params_free")


UNIT_STEPS = {U_KV: (1, 2, 4, 5, 6, 7), U_Q: (1, 2, 3, 4, 5, 6, 7), U_Z: (0, 1, 2, 3, 4, 5)}


def item_step(i):
    return i % 2 == 1 or i >= 56


TILES = (0, 1, 2, 3)


def item(i):
    return TILES[i // (2 * NH)], i // NH % 2, i % NH


def pieces():
    return [(u, a) for u in range(N_UNITS) for a in range(2) if (u, a) != (N_UNITS - 1, 1)]


def loads_of(unit):
    return 2 if unit == U_TAIL or U_UP <= unit < U_DN else 1


def trunk(nc, depth, x, positions, attn_norm, w_in, nsa_q_norm, nsa_k_norm, cmp_pe, cmp_w1, cmp_w2, nsa_out_norm,
          gdn_conv_w, gdn_a_log, gdn_dt_bias, gdn_out_norm, w_out, ffn_norm, w_up, ffn_conv_w, ffn_conv_b, w_down, out):
    with ExitStack() as ctx:
        base = (nc.sbuf_base + 31) // 32 * 32
        top = [0]

        def at_word(name, shape, dt, word):
            return nc.alloc_sbuf_tensor_at(name, [P if shape[0] is None else shape[0]] + list(shape[1:]), dt,
                                           offset=base + 4 * word)

        def words(shape, dt=F32):
            n = 1
            for s in shape[1:]:
                n *= s
            return n if dt != BF16 else (n + 1) // 2

        def fixed(name, shape, dt=F32):
            t = at_word(name, shape, dt, top[0])
            top[0] += (words(shape, dt) + 7) // 8 * 8
            return t

        def zone(start, limit):
            pos = [start]

            def place(name, shape, dt=F32):
                t = at_word(name, shape, dt, pos[0])
                pos[0] += (words(shape, dt) + 7) // 8 * 8
                assert pos[0] <= limit, (name, pos[0], limit)
                return t
            return place

        x_res = fixed("x_res", [P, TT_, D])
        raw = fixed("raw", [P, 2, PIECE])
        W0 = top[0]
        w_hi = fixed("w_hi", [P, 2, PIECE], F32R)
        w_lo = fixed("w_lo", [P, 2, PIECE], F32R)
        q_stack = at_word("q_stack", [P, NH, T], F32R, W0)
        k_stack = at_word("k_stack", [P, 2, 2, NG, T], F32R, W0 + NH * T)
        xo = fixed("xo", [P, TT_, D])
        ident = fixed("ident", [P, P])
        ident_bf = fixed("ident_bf", [P, P], BF16)
        causal_bf = fixed("causal_bf", [P, P], BF16)
        ident64 = fixed("ident64", [P, CH])
        upto = fixed("upto", [P, CH])
        sum_upto = fixed("sum_upto", [P, P])
        after = fixed("after", [P, P])
        chunk_rows = fixed("chunk_rows", [P, 2, P])
        level_mask = fixed("level_mask", [P, 6, CH])
        cmp_add = fixed("cmp_add", [P, TT_, 32])
        cmp_mul = fixed("cmp_mul", [P, TT_, 32])
        rope_c = fixed("rope_c", [P, TT_, 16])
        rope_s = fixed("rope_s", [P, TT_, 16])
        minus_half = fixed("minus_half", [P, 64])
        par = fixed("par", [P, 3, P])
        par_bc = fixed("par_bc", [P, 904])
        cmp_w2_sb = fixed("cmp_w2_sb", [P, 2, 2, DH])
        ssum = fixed("ssum", [P, 4])
        rstd = fixed("rstd", [P, 4])
        small = fixed("small", [P, 1024])
        CONV0 = top[0]
        conv_in = fixed("conv_in", [P, 4, 4 + T])
        Z0 = top[0]
        h_hi = at_word("h_hi", [P, KC, T], F32R, Z0)
        h_lo = at_word("h_lo", [P, KC, T], F32R, Z0 + KC * T)
        Z1 = Z0 + 2 * KC * T
        qkvT = at_word("qkvT", [P, 12, T], F32, Z1)
        pj = at_word("pj", [P, TT_, PJ_W], F32, Z1 + 12 * T)
        g_mlp = at_word("g_mlp", [P, FK, T], F32, Z1)
        Z2 = Z1 + 12 * T + TT_ * PJ_W
        END = (nc.sbuf_usable_end - base) // 4
        par_rows = at_word("par_rows", [P, 3, P], F32, (END - 3 * P) // 8 * 8)
        late = zone(Z2, END)
        conv_out = late("conv_out", [P, 4, T])
        g_hi = late("g_hi", [P, 2, T], F32R)
        g_lo = late("g_lo", [P, 2, T], F32R)
        low, high, front = zone(Z0, Z1), zone(Z2, END), zone(CONV0, Z0)
        qT = low("qT", [P, 4, T])
        kT = low("kT", [P, 2, T])
        blk = low("blk", [P, 16, 64])
        o_tmp = at_word("o_tmp", [P, 2, NQ], F32, Z0 + 6 * T)
        hid_rows = low("hid_rows", [64, 2, HID])
        hid = low("hid", [P, 2, 2, 64])
        kcT = low("kcT", [P, NG, 32])
        kc_rows = low("kc_rows", [64, DH])
        kc_sq = low("kc_sq", [64, DH])
        kc_two = low("kc_two", [32, P])
        vc_rows = low("vc_rows", [64, DH])
        vc_diag = low("vc_diag", [P, 4 * DH])
        neg_max = low("neg_max", [P, N_ITEMS])
        row_sum = low("row_sum", [P, N_ITEMS])
        prob = low("prob", [P, 2, T])
        probT = low("probT", [P, 2, T])
        A0 = Z1 - 4 * T
        c_prob = at_word("c_prob", [P, TT_, NH * 32], F32, A0)
        c_probT = at_word("c_probT", [P, TT_, 2 * P], F32, A0 + 1024)
        blk_hi = at_word("blk_hi", [P, 16, 64], F32R, A0)
        blk_lo = at_word("blk_lo", [P, 16, 64], F32R, A0 + 1024)
        formsT = front("formsT", [P, 3, GH, P])
        forms_sb = high("forms_sb", [P, 4, GH, GD])
        inverse = zone(Z2, Z2 + 4 * GW)
        lt_even = inverse("lt_even", [P, 2 * GH, CH])
        xi = inverse("xi", [P, 2 * GH, CH])
        xiT = inverse("xiT", [P, 2 * GH, CH])
        yy = inverse("yy", [P, 2 * GH, CH])
        raw_qk = high("raw_qk", [P, 2, GH, GD])
        u_sb = at_word("u_sb", [P, 2, GH, GD], F32, Z2 + 4 * GW)
        g_upto = high("g_upto", [P, GH, CH])
        decayT = high("decayT", [P, GH, CH])
        wq = high("wq", [P, 2, GH, 4 * CH])
        akkT = front("akkT", [P, 2 * GH, CH])
        lt_odd = high("lt_odd", [P, 2 * GH, CH])
        ltT = (lt_even, lt_odd)
        aqkT = high("aqkT", [P, 2 * GH, CH])

        def of_tile(part, r):
            return qkvT[:, GH * part:GH * part + GH, r * P:(r + 1) * P]

        v_new, og, og_sq, state_g = (pj[:, i, 0:GW].rearrange("p (h d) -> p h d", h=GH) for i in range(4))
        state = pj[:, :, 512:512 + GD]

        def sm(lo, n, rows=P):
            return small[0:rows, lo:lo + n]
        qk_ss, qk_rs = sm(0, 48), sm(48, 48)
        gy, gn, gE, bE, aE = sm(96, 16), sm(112, 16), sm(128, 96), sm(224, 16), sm(240, 4)
        gdec, beta, gate = sm(256, 16), sm(272, 16), sm(288, 96)
        ex = sm(384, 64)
        g_ss, g_rr, g_sc = sm(448, 8), sm(456, 8), sm(464, 20)
        o_ss, o_rr = sm(488, 4), sm(496, 4)
        c_max, c_sum, c_coef = sm(848, 32), sm(880, 32), sm(912, 32)
        coef = sm(536, 8)
        no_ss, no_rr = sm(544, 32), sm(576, 32)
        kc_ss, kc_rr = sm(608, 1, 64), sm(616, 1, 64)
        q_gain = sm(640, 64)
        ang, turns, wrap = sm(704, 32), sm(736, 32), sm(768, 32)
        inv_freq = sm(800, 8)
        pos_f = sm(808, 4)
        cosang = sm(816, 32)
        pos_i = at_word("pos_i", [P, 4], I32, CONV0 - 8)

        ps = [ctx.enter_context(nc.psum_tensor(f"bank{b}", [P, 512], F32)) for b in range(8)]

        sems = {n: ctx.enter_context(nc.semaphore(n)) for n in SIGNALS}
        const_ready = ctx.enter_context(nc.semaphore("const_ready"))
        rope_ready = ctx.enter_context(nc.semaphore("rope_ready"))
        rope_steps = ctx.enter_context(nc.semaphore("rope_steps"))
        x_loaded = ctx.enter_context(nc.semaphore("x_loaded"))
        pos_loaded = ctx.enter_context(nc.semaphore("pos_loaded"))
        par_loaded = ctx.enter_context(nc.semaphore("par_loaded"))
        bc_loaded = ctx.enter_context(nc.semaphore("bc_loaded"))
        raw_loaded = [ctx.enter_context(nc.semaphore(f"raw_loaded{i}")) for i in range(2)]
        pool_steps, sp_steps, pe_steps = (ctx.enter_context(nc.semaphore(n)) for n in ("pool_steps", "sp_steps", "pe_steps"))
        out_stored = ctx.enter_context(nc.semaphore("out_stored"))

        def sig(l, name, k):
            return sems[name], l * SIGNALS[name] + k + (SIGNALS[name] if name in LOOK_BACK else 0)

        def task_done(l, unit, j):
            before = 0
            for u in range(unit):
                before += 0 if u in (U_CK, U_CV) else 3
            if j == (0 if unit in (U_CK, U_CV) else 3):
                return sig(l, "odd_used", unit + 1)
            return sig(l, "dense_done", before + j + 1)

        loads_layer = [sum(loads_of(u) for u, a in pieces() if a == s) for s in range(2)]

        def piece_loaded(l, p):
            u, a = pieces()[p]
            n = sum(loads_of(v) for v, b in pieces() if b == a and v <= u)
            return raw_loaded[a], (l * loads_layer[a] + n) * 16

        def slot_free(l, p):
            u, a = pieces()[p]
            return sig(l, "odd_used" if a else "even_used", u)

        def kt_used(l, k):
            if k % 2 == 0:
                return sig(l, "g_used", k // 2 + 1)
            p = 2 * U_DN + k // 2
            return sig(l, "odd_used" if p % 2 else "even_used", p // 2 + 1)

        def over(ap, axis, n):
            a = ap.unsqueeze(axis)
            shape = list(a.shape)
            shape[axis] = n
            return a.broadcast_to(shape)

        def turned_bank(which, kc):
            return ps[kc if which == 0 else (kc + 4) % 8]

        def h4(ap):
            return ap.rearrange("p (h n) -> p h n", h=GH)

        gain_attn, gain_ffn = par[:, 0, 0:8], par[:, 0, 8:16]
        gdn_taps = par[:, 0, 16:64].rearrange("p (j c) -> p j c", j=4)
        ffn_bias = par[:, 0, 64:108]
        ffn_taps01 = par[:, 1, 0:88].rearrange("p (j c) -> p j c", j=2)
        ffn_tap2 = par[:, 2, 0:44]
        pe_kv = par[:, 2, 44:76].rearrange("p (v m) -> p v m", v=2)
        bc_q, bc_k = par_bc[:, 0:64], par_bc[:, 64:256].rearrange("p (b d) -> p b d", b=3)
        bc_no, bc_go = par_bc[:, 256:768], par_bc[:, 768:896]
        bc_al, bc_dt = par_bc[:, 896:900], par_bc[:, 900:904]

        block = ctx.enter_context(nc.Block())

        @block.sync
        def _(sp):
            with nc.allow_non_contiguous_dma(reason="512 positions"):
                sp.dma_start(pos_i[:, :], positions[0].rearrange("(t p) -> p t", p=P)).then_inc(pos_loaded, 16)
            for t in range(TT_):
                sp.dma_start(x_res[:, t, :], x[0, t * P:(t + 1) * P, :]).then_inc(x_loaded, 16)
            with sp.Fori(0, depth) as l:

                def load(p):
                    u, a = pieces()[p]
                    if p >= 2:
                        sp.wait_ge(*sig(l, "split", p - 1))
                    else:
                        sp.wait_ge(*sig(l, "split", 0))
                    sp.sem_inc(sp_steps, 1)
                    dst = raw[:, a, :]
                    if u in (U_GQ, U_GK, U_GV, U_KV, U_Q, U_Z):
                        col = {U_GQ: C_QKV, U_GK: C_QKV + GW, U_GV: C_QKV + 2 * GW, U_KV: C_KV, U_Q: C_Q, U_Z: C_Z}[u]
                        src = w_in[l].rearrange("(k p) n -> p k n", p=P)
                        parts = [(dst.rearrange("p (k n) -> p k n", k=4), src[:, 4 * a:4 * a + 4, col:col + 512])]
                    elif u == U_TAIL:
                        d = dst[:, 0:4 * 288].rearrange("p (k n) -> p k n", k=4)
                        src = w_in[l].rearrange("(k p) n -> p k n", p=P)[:, 4 * a:4 * a + 4, :]
                        parts = [(d[:, :, 0:280], src[:, :, 1024:1304]), (d[:, :, 280:288], src[:, :, C_AB:C_AB + 8])]
                    elif u in (U_CK, U_CV):
                        src = cmp_w1[l, u - U_CK].rearrange("(m p) n -> p m n", p=P)
                        parts = [(dst.rearrange("p (m n) -> p m n", m=8), src[:, 8 * a:8 * a + 8, :])]
                    elif u < U_UP:
                        c = (u - U_O0) * 512
                        src = w_out[l].rearrange("(k p) n -> p k n", p=P)
                        parts = [(dst.rearrange("p (k n) -> p k n", k=4), src[:, 4 * a:4 * a + 4, c:c + 512])]
                    elif u < U_DN:
                        c = (u - U_UP) * 256
                        src = w_up[l].rearrange("(k p) n -> p k n", p=P)[:, 4 * a:4 * a + 4, :]
                        d = dst.rearrange("p (k s n) -> p k s n", k=4, s=2)
                        parts = [(d[:, :, s, :], src[:, :, s * FF + c:s * FF + c + 256]) for s in range(2)]
                    else:
                        k = 4 * (u - U_DN) + 2 * a
                        src = w_down[l].rearrange("(k p) n -> p k n", p=P)
                        parts = [(dst.rearrange("p (k n) -> p k n", k=2), src[:, k:k + 2, :])]
                    assert len(parts) == loads_of(u)
                    for d, s in parts:
                        sp.dma_start(d, s).then_inc(raw_loaded[a], 16)

                sp.wait_ge(*sig(l, "params_free", 0))
                sp.sem_inc(sp_steps, 1)
                rows = [(0, 0, 8, attn_norm[l].rearrange("(r c) -> r c", c=P)),
                        (0, 8, 8, ffn_norm[l].rearrange("(r c) -> r c", c=P)),
                        (0, 16, 48, gdn_conv_w[l].rearrange("j (r c) -> (j r) c", c=P)),
                        (0, 64, 44, ffn_conv_b[l].rearrange("(r c) -> r c", c=P)),
                        (1, 0, 88, ffn_conv_w[l, 0:2].rearrange("j (r c) -> (j r) c", c=P)),
                        (2, 0, 44, ffn_conv_w[l, 2].rearrange("(r c) -> r c", c=P)),
                        (2, 44, 32, cmp_pe[l].rearrange("v (m s) d -> (v m) (s d)", s=2))]
                for b, r0, n, src in rows:
                    sp.dma_start(par_rows[r0:r0 + n, b, :], src).then_inc(par_loaded, 16)
                vecs = [(0, 64, nsa_q_norm[l]), (64, 192, nsa_k_norm[l].rearrange("b d -> (b d)")),
                        (256, 512, nsa_out_norm[l].rearrange("h d -> (h d)")), (768, 128, gdn_out_norm[l]),
                        (896, 4, gdn_a_log[l]), (900, 4, gdn_dt_bias[l])]
                for c, n, src in vecs:
                    sp.dma_start(par_bc[:, c:c + n], src.partition_broadcast(P)).then_inc(bc_loaded, 16)
                sp.dma_start(cmp_w2_sb[:, :, :, :], cmp_w2[l].rearrange("v (s p) d -> p v s d", p=P)).then_inc(bc_loaded, 16)
                for p in range(N_PIECES):
                    load(p)
            for t in range(TT_):
                sp.wait_ge(*sig(depth - 1, "x_added", 8 + 2 * t + 2))
                sp.dma_start(out[0, t * P:(t + 1) * P, :], x_res[:, t, :]).then_inc(out_stored, 16)
            sp.wait_ge(out_stored, 16 * TT_)

        N_PAR, N_BC = 7 * 16, 7 * 16

        @block.gpsimd
        def _(pool):
            for name in LOOK_BACK:
                pool.sem_inc(sems[name], SIGNALS[name])
            for i in range(ROPE // 2):
                pool.memset(inv_freq[:, i:i + 1], THETA ** (-2.0 * i / ROPE))
            pool.drain().then_inc(const_ready, 1)
            for t, v in ((ident, 0.0), (ident64, 0.0), (upto, 1.0), (sum_upto, 0.0), (after, 0.0), (chunk_rows, 0.0),
                         (level_mask, 0.0), (cmp_add, 0.0), (cmp_mul, 1.0), (minus_half, -0.5), (causal_bf, 0.0)):
                pool.memset(t[:], v)
            pool.drain()
            pool.affine_select(out=ident[:, :], in_=ident[:, :], compare_op=ALU.not_equal, fill=1.0, base=0,
                               pattern=[[-1, P]], channel_multiplier=1)
            pool.affine_select(out=causal_bf[:, :], in_=causal_bf[:, :], compare_op=ALU.is_ge, fill=NEG, base=0,
                               pattern=[[-1, P]], channel_multiplier=1)
            for m, v in ((cmp_add, NEG), (cmp_mul, 0.0)):
                pool.affine_select(out=m[:, :, :], in_=m[:, :, :], compare_op=ALU.is_ge, fill=v, base=-(BLK - 1),
                                   pattern=[[P, TT_], [-STRIDE, 32]], channel_multiplier=1)
            r = slice(0, CH)
            upper = [level_mask[r, k, :].rearrange("p (b u s) -> p b u s", u=2, s=1 << k)[:, :, 1, :] for k in range(6)]
            pool.affine_select(out=ident64[r, :], in_=ident64[r, :], compare_op=ALU.not_equal, fill=1.0, base=0,
                               pattern=[[-1, CH]], channel_multiplier=1)
            pool.affine_select(out=upto[r, :], in_=upto[r, :], compare_op=ALU.is_ge, fill=0.0, base=0,
                               pattern=[[1, CH]], channel_multiplier=-1)
            pool.memset(sum_upto[r, r], 1.0)
            pool.memset(after[r, r], 1.0)
            pool.memset(chunk_rows[r, 0, :], 1.0)
            for k in range(6):
                pool.memset(upper[k], 1.0)
            pool.drain()
            pool.memset(chunk_rows[CH:2 * CH, 1, :], 1.0)
            pool.drain()
            pool.affine_select(out=sum_upto[r, r], in_=sum_upto[r, r], compare_op=ALU.is_ge, fill=0.0, base=0,
                               pattern=[[1, CH]], channel_multiplier=-1)
            pool.affine_select(out=after[r, r], in_=after[r, r], compare_op=ALU.is_ge, fill=0.0, base=-1,
                               pattern=[[-1, CH]], channel_multiplier=1)
            for k in range(6):
                s = 1 << k
                pool.affine_select(out=upper[k], in_=upper[k], compare_op=ALU.is_ge, fill=0.0, base=0,
                                   pattern=[[-2 * s, CH // (2 * s)], [0, s]], channel_multiplier=1)
            pool.drain()
            for k in range(6):
                s = 1 << k
                pool.affine_select(out=upper[k], in_=upper[k], compare_op=ALU.is_ge, fill=0.0, base=s - 1,
                                   pattern=[[2 * s, CH // (2 * s)], [0, s]], channel_multiplier=-1)
            pool.drain()
            pool.tensor_copy(ident_bf[:, :], ident[:, :])
            pool.drain().then_inc(const_ready, 1)

            def inverse_root(dst, src, n, rows, scale, done):
                pool.sem_inc(pool_steps, 1)
                pool.tensor_scalar(src, src, scale, EPS, ALU.mult, ALU.add)
                pool.drain()
                pool.tensor_tensor(dst, src, minus_half[0:rows, 0:n], ALU.pow).then_inc(sems[done], 1)

            with pool.Fori(0, depth) as l:
                def row_roots(which):
                    for t in range(TT_):
                        pool.wait_ge(*sig(l, "squares", 4 * which + t + 1))
                        inverse_root(rstd[:, t:t + 1], ssum[:, t:t + 1], 1, P, 1.0 / D, "rstd")

                row_roots(0)

                def deltanet():
                    def output_root(r):
                        pool.wait_ge(*sig(l, "oss", r + 1))
                        inverse_root(o_rr, o_ss, 4, P, 1.0 / GD, "orr")

                    for b in range(2):
                        for r in (2 * b, 2 * b + 1):
                            pool.wait_ge(*sig(l, "raw_ev", r + 1))
                            inverse_root(g_rr, g_ss, 8, P, 1.0, "rr_ready")
                            if r == 2:
                                output_root(1)
                            for _ in range(4):
                                yield
                        for _ in range(13):
                            yield
                        for n in range(4 * b, 4 * b + 4):
                            r, c = n // 2, n % 2
                            pool.wait_ge(*sig(l, "s_ready", n + 1))
                            whole = ex[:, 32 + 16 * c + 4 * r:32 + 16 * c + 4 * r + 4]
                            if n == 0:
                                pool.wait_ge(*sig(l, "gcum_exp", 1))
                            pool.tensor_tensor(state_g, state, over(whole, 2, GD), ALU.mult).then_inc(sems["sg_ready"], 1)
                            if n % 4 == 2:
                                output_root(r - 1)
                            yield
                            yield
                    output_root(3)
                    yield
                    yield

                steps = deltanet()
                for u in (U_KV, U_Q, U_Z):
                    for j in UNIT_STEPS[u]:
                        next(steps)
                        if u == U_Z and j in (0, 1):
                            pool.wait_ge(*sig(l, "qk_squares", j + 1))
                            cols = slice(24 * j, 24 * j + 24)
                            inverse_root(qk_rs[:, cols], qk_ss[:, cols], 24, P, 1.0 / DH, "qk_rstd")
                for segment in range(1, 7):
                    if segment == 5:
                        pool.wait_ge(*sig(l, "kc_ss", 1))
                        inverse_root(kc_rr, kc_ss, 1, 64, 1.0 / DH, "kc_rstd")
                    next(steps)
                for part in range(3):
                    next(steps, None)
                    if part == 0:
                        pool.wait_ge(*sig(l, "stack_hi", 1))
                        pool.sem_inc(pool_steps, 1)
                        for g in range(NG):
                            rows = slice(DH * g, DH * g + DH)
                            for to in range(2):
                                pool.drain()
                                pool.tensor_tensor(k_stack[DH * to:DH * to + DH, 1, :, g, :], kT[rows, :, :],
                                                   k_stack[rows, 0, :, g, :], ALU.subtract)
                        pool.drain().then_inc(sems["k_stacked"], 1)
                for i in range(N_ITEMS):
                    if i >= 16 and i % 16 == 3:
                        pool.wait_ge(*sig(l, "no_ss", i // 16))
                        t = item(i - 16)[0]
                        inverse_root(no_rr[:, 8 * t:8 * t + 8], no_ss[:, 8 * t:8 * t + 8], 8, P, 1.0 / DH, "no_rstd")
                    if item_step(i):
                        next(steps, None)
                pool.wait_ge(*sig(l, "no_ss", TT_))
                last = slice(8 * TILES[-1], 8 * TILES[-1] + 8)
                inverse_root(no_rr[:, last], no_ss[:, last], 8, P, 1.0 / DH, "no_rstd")
                row_roots(1)

        @block.scalar
        def _(act):
            act.wait_ge(rope_steps, 1)
            act.activation(ang, ang, ACT.Sin)
            act.activation(cosang, cosang, ACT.Sin)
            act.drain().then_inc(rope_ready, 1)
            with act.Fori(0, depth) as l:

                def split_hi(p):
                    if p >= N_PIECES:
                        return
                    act.wait_ge(*piece_loaded(l, p))
                    act.wait_ge(*slot_free(l, p))
                    n = 4 * 288 if p // 2 == U_TAIL else PIECE
                    act.activation(w_hi[:, p % 2, 0:n], raw[:, p % 2, 0:n], ACT.Copy).then_inc(sems["hi_done"], 1)

                def row_squares(t):
                    act.activation(xo[:, t, :], x_res[:, t, :], ACT.Square, accum_out=ssum[:, t:t + 1])
                    act.drain().then_inc(sems["squares"], 1)

                def h_round(which, gain):
                    for kc in range(KC):
                        act.wait_ge(*sig(l, "hT_psum", 8 * which + kc + 1))
                        bank = turned_bank(which, kc)
                        if gain is None:
                            act.activation(h_hi[:, kc, :], bank[:, :], ACT.Copy).then_inc(sems["h_hi"], 1)
                        else:
                            act.activation(h_hi[:, kc, :], bank[:, :], ACT.Copy,
                                           scale=gain[:, kc:kc + 1]).then_inc(sems["h_hi"], 1)

                act.wait_ge(x_loaded, 16 * TT_)
                for t in range(TT_):
                    act.wait_ge(*sig(l, "x_added", 2 * t + 2 - 8))
                    row_squares(t)
                act.wait_ge(*sig(l, "par_psum", 1))
                for b, n in ((0, 108), (1, 88), (2, 76)):
                    act.activation(par[:, b, 0:n], ps[0][:, b * P:b * P + n], ACT.Copy)
                act.drain().then_inc(sems["par_ready"], 1)
                split_hi(0)
                split_hi(1)
                h_round(0, gain_attn)

                def evacuate(u, j):
                    bank = ps[j]
                    act.wait_ge(*task_done(l, u, j))
                    if u <= U_GV:
                        if u > 0:
                            act.wait_ge(*sig(l, "gconv", 4 * (u - 1) + j + 1))
                        elif j == 0:
                            act.wait_ge(*sig(l, "ffn_conv", 0))
                        dst, fn = conv_in[:, j, 4:4 + T], ACT.Copy
                        src = bank[:, :]
                    elif u == U_TAIL:
                        dst, src, fn = pj[:, j, 1024:1312], bank[:, 0:288], ACT.Copy
                    elif u == U_KV:
                        dst, src, fn = pj[:, j, 512:1024], bank[:, :], ACT.Copy
                    elif u == U_Q:
                        dst = pj[:, j, 0:512].rearrange("p (n g d) -> p g n d", g=NG, d=DH)
                        src, fn = bank[:, :].rearrange("p (g n d) -> p g n d", g=NG, d=DH), ACT.Copy
                    else:
                        dst, src, fn = xo[:, j, 512:1024], bank[:, :], ACT.Silu
                    act.activation(dst, src, fn).then_inc(sems["proj_evac"], 1)

                for u in range(U_TAIL + 1):
                    split_hi(2 * u + 2)
                    for j in range(4):
                        evacuate(u, j)
                    split_hi(2 * u + 3)
                    if u <= U_GV:
                        for j in range(4):
                            act.wait_ge(*sig(l, "gconv", 4 * u + j + 1))
                            act.activation(qkvT[:, 4 * u + j, :], conv_out[:, j, :], ACT.Silu).then_inc(sems["gsilu"], 1)
                act.wait_ge(*sig(l, "ga_in", 1))
                act.activation(gn, gn, ACT.Exp)
                act.activation(bE.rearrange("p (t h) -> p t h", t=TT_), pj[:, :, PJ_B:PJ_B + 4], ACT.Exp, scale=-1.0)
                act.activation(gE.rearrange("p (t h) -> p t h", t=TT_), pj[:, :, PJ_G:PJ_G + 24], ACT.Exp, scale=-1.0)
                act.activation(aE, bc_al, ACT.Exp)
                act.drain()
                act.activation(gn, gn, ACT.Ln, bias=1.0).then_inc(sems["ga_exp"], 1)
                def deltanet():
                    for b in range(2):
                        for r in (2 * b, 2 * b + 1):
                            for f in range(2):
                                act.wait_ge(*sig(l, "raw_psum", 3 * r + f + 1))
                                act.activation(raw_qk[:, f, :, :], h4(ps[5 + f][:, :]), ACT.Copy)
                                for h in range(GH):
                                    act.activation(of_tile(f, r)[:, h, :], ps[5 + f][:, GD * h:GD * h + GD], ACT.Square,
                                                   accum_out=g_ss[:, GH * f + h:GH * f + h + 1])
                            act.drain().then_inc(sems["raw_ev"], 1)
                            yield
                            act.wait_ge(*sig(l, "decay_psum", r + 1))
                            act.activation(decayT[:, :, :], h4(ps[7][:, 0:GH * CH]), ACT.Exp).then_inc(sems["dt_exp"], 1)
                            yield
                            for f in range(3):
                                act.wait_ge(*sig(l, "formsT_psum", 4 * r + f + 1))
                                act.activation(formsT[:, f, :, :], h4(ps[5 + f][:, :]),
                                               ACT.Copy).then_inc(sems["formsT_ready"], 1)
                            yield
                            act.wait_ge(*sig(l, "formsT_psum", 4 * r + 4))
                            act.activation(wq[:, r % 2, :, CH:3 * CH], h4(ps[5][:, :]),
                                           ACT.Copy).then_inc(sems["formsT_ready"], 1)
                            yield
                        yield
                        for k in range(1, 6):
                            act.wait_ge(*sig(l, "y_psum", 6 * b + k + 1))
                            act.activation(yy[:, :, :], ps[5][:, :].rearrange("p (k n) -> p k n", k=2 * GH),
                                           ACT.Copy).then_inc(sems["y_ready"], 1)
                            yield
                            yield
                        act.wait_ge(*sig(l, "uw_psum", 2 * b + 1))
                        act.activation(u_sb[:, 0, :, :], h4(ps[5][:, :]), ACT.Copy)
                        for c in range(2):
                            w_view = ps[6 + c][:, :].rearrange("p (r h n) -> p r h n", r=2, h=GH)
                            act.activation(wq[:, :, :, 3 * c * CH:3 * c * CH + CH], w_view, ACT.Copy)
                        act.drain().then_inc(sems["uw_ready"], 1)
                        yield
                        act.wait_ge(*sig(l, "uw_psum", 2 * b + 2))
                        act.activation(u_sb[:, 1, :, :], h4(ps[5][:, :]), ACT.Copy).then_inc(sems["uw_ready"], 1)
                        yield
                        for n in range(4 * b, 4 * b + 4):
                            r, c = n // 2, n % 2
                            yield
                            act.wait_ge(*sig(l, "oc_psum", n + 1))
                            if c == 0 and r > 0:
                                act.wait_ge(*sig(l, "o_written", r))
                            src = h4(ps[6 + c][CH * (1 - c):CH * (1 - c) + CH, :])
                            act.activation(og[CH * c:CH * c + CH, :, :], src, ACT.Copy)
                            act.activation(og_sq[CH * c:CH * c + CH, :, :], src, ACT.Square)
                            act.drain().then_inc(sems["og_ready"], 1)
                            yield
                    yield
                    yield

                steps = deltanet()
                for u in (U_KV, U_Q, U_Z):
                    for j in range(8):
                        if j == 3:
                            split_hi(2 * u + 2)
                        if j >= 4:
                            evacuate(u, j - 4)
                        if u == U_KV and j == 2:
                            act.wait_ge(*sig(l, "gcum_psum", 1))
                            act.activation(ex, ps[4][:, 0:64], ACT.Exp).then_inc(sems["gcum_exp"], 1)
                        if j in UNIT_STEPS[u]:
                            next(steps)
                    split_hi(2 * u + 3)

                def keep_turned(i):
                    act.wait_ge(*sig(l, "qkT_psum", i + 1))
                    dst = qT[:, i, :] if i < 4 else kT[:, i - 4, :]
                    act.activation(dst, ps[2 + i % 3][:, :], ACT.Copy).then_inc(sems["qkT_ready"], 1)

                for i in range(6):
                    keep_turned(i)
                act.wait_ge(*sig(l, "blk_f32", 1))
                act.activation(blk_hi[:, :, :], blk[:, :, :], ACT.Copy).then_inc(sems["blk_hi"], 1)
                next(steps)
                for kv in range(2):
                    if kv == 0:
                        split_hi(2 * U_CV)
                    act.wait_ge(*task_done(l, U_CK + kv, 0))
                    act.activation(hid_rows[:, kv, :], ps[3 + kv][0:64, 0:HID], ACT.Silu).then_inc(sems["hid_silu"], 1)
                    if kv == 0:
                        act.wait_ge(*sig(l, "blk_f32", 2))
                        act.activation(blk_hi[:, :, :], blk[:, :, :], ACT.Copy).then_inc(sems["blk_hi"], 1)
                        split_hi(2 * U_CV + 1)
                    next(steps, None)
                act.wait_ge(*sig(l, "hid_psum", 1))
                act.activation(hid[:, :, :, :], ps[0][:, 0:256].rearrange("p (v s n) -> p v s n", v=2, s=2),
                               ACT.Copy).then_inc(sems["hid_ready"], 1)
                next(steps, None)
                next(steps, None)
                act.wait_ge(*sig(l, "kcT_psum", 1))
                for g in range(NG):
                    rows = slice(DH * g, DH * g + DH)
                    act.activation(kcT[rows, g, :], ps[2][rows, 0:32], ACT.Copy)
                act.drain().then_inc(sems["kcT_ready"], 1)
                next(steps, None)
                for g in range(NG):
                    rows = slice(DH * g, DH * g + DH)
                    act.activation(q_stack[rows, 4 * g:4 * g + 4, :], qT[rows, :, :], ACT.Copy)
                    for to in range(2):
                        act.activation(k_stack[DH * to:DH * to + DH, 0, :, g, :], kT[rows, :, :], ACT.Copy)
                act.drain().then_inc(sems["stack_hi"], 1)
                for i in range(2):
                    cp = c_prob[:, 2 * i:2 * i + 2, :]
                    act.wait_ge(*sig(l, "cs_shift", i + 1))
                    act.activation(cp, cp, ACT.Exp).then_inc(sems["cs_exp"], 1)
                next(steps, None)
                for i in range(2):
                    act.wait_ge(*sig(l, "cpT_psum", i + 1))
                    act.activation(c_probT[:, 2 * i:2 * i + 2, :], ps[2 + i][:, :].rearrange("p (t n) -> p t n", t=2),
                                   ACT.Copy).then_inc(sems["cpT_ready"], 1)
                next(steps, None)
                act.wait_ge(*sig(l, "co_psum", TT_))
                next(steps, None)
                def exponentials(i):
                    n = (item(i)[0] + 1) * P
                    act.wait_ge(*sig(l, "negmax", i + 1))
                    if i >= 2:
                        act.wait_ge(*sig(l, "pT_psum", i - 1))
                    act.activation(prob[:, i % 2, 0:n], ps[i % 2][:, 0:n], ACT.Exp, bias=neg_max[:, i:i + 1],
                                   accum_out=row_sum[:, i:i + 1])
                    act.drain().then_inc(sems["p_ready"], 1)

                exponentials(0)
                for i in range(N_ITEMS):
                    if i + 1 < N_ITEMS:
                        exponentials(i + 1)
                    n = (item(i)[0] + 1) * P
                    act.wait_ge(*sig(l, "pT_psum", i + 1))
                    if i >= 2:
                        act.wait_ge(*sig(l, "pv_done", i - 1))
                    act.activation(probT[:, i % 2, 0:n], ps[2 + i % 2][:, 0:n], ACT.Copy).then_inc(sems["pT_ready"], 1)
                    if item_step(i):
                        next(steps, None)
                split_hi(2 * U_O0)
                split_hi(2 * U_O0 + 1)

                h_round(1, None)
                for p in range(2 * U_O0 + 2, 2 * U_UP + 1):
                    split_hi(p)
                for t in range(TT_):
                    act.wait_ge(*sig(l, "x_added", 4 + t + 1))
                    row_squares(t)
                split_hi(2 * U_UP + 1)
                h_round(2, gain_ffn)
                def hidden_hi(k):
                    if k >= 2:
                        act.wait_ge(*kt_used(l, k - 2))
                    act.activation(g_hi[:, k % 2, :], g_mlp[:, k, :], ACT.Copy).then_inc(sems["g_hi_done"], 1)

                for i in range(N_UP):
                    u = U_UP + i
                    split_hi(2 * u + 2)
                    if i == N_UP - 1:
                        for k in range(2):
                            act.wait_ge(*sig(l, "g_ready", k + 1))
                            hidden_hi(k)
                    for j in range(4):
                        act.wait_ge(*task_done(l, u, j))
                        if i > 0:
                            act.wait_ge(*sig(l, "ffn_conv", 4 * (i - 1) + j + 1))
                        act.activation(conv_in[:, j, 4:4 + T], ps[4 * (u % 2) + j][:, :],
                                       ACT.Copy).then_inc(sems["ffn_copied"], 1)
                    split_hi(2 * u + 3)
                    for j in range(2):
                        act.wait_ge(*sig(l, "ffn_conv", 4 * i + j + 1))
                        act.activation(conv_out[:, j, :], conv_out[:, j, :], ACT.Silu).then_inc(sems["silu_ready"], 1)
                for k in range(FK):
                    if k >= 2:
                        act.wait_ge(*sig(l, "g_ready", k + 1))
                        hidden_hi(k)
                    if k % 2 == 0 and k > 0:
                        split_hi(2 * U_DN + k // 2 + 1)

        @block.vector
        def _(dve):
            def tt(o, a, b, op):
                return dve.tensor_tensor(o, a, b, op)

            dve.wait_ge(const_ready, 1)
            dve.wait_ge(pos_loaded, 16)
            dve.tensor_copy(pos_f, pos_i[:, :])
            dve.drain()
            a3 = ang.rearrange("p (t i) -> p t i", t=TT_)
            tt(a3, over(pos_f, 2, 8), over(inv_freq, 1, TT_), ALU.mult)
            dve.drain()
            two_pi = 6.283185307179586
            c1 = 6.28125
            c2 = 0.0019350051879882812
            c3 = two_pi - c1 - c2
            magic = 12582912.0
            dve.tensor_scalar(turns, ang, 1.0 / two_pi, magic, ALU.mult, ALU.add)
            dve.drain()
            dve.tensor_scalar(turns, turns, magic, None, ALU.subtract)
            for c in (c1, c2, c3):
                dve.drain()
                dve.scalar_tensor_tensor(out=ang, in0=turns, scalar=-c, in1=ang, op0=ALU.mult, op1=ALU.add)
            dve.drain()
            dve.tensor_scalar(cosang, ang, two_pi / 4, None, ALU.add)
            dve.drain()
            dve.tensor_scalar(wrap, cosang, PI, -two_pi, ALU.is_gt, ALU.mult)
            dve.drain()
            tt(cosang, cosang, wrap, ALU.add)
            dve.drain()
            dve.tensor_scalar(cosang, cosang, PI, -PI, ALU.min, ALU.max)
            dve.tensor_scalar(ang, ang, PI, -PI, ALU.min, ALU.max)
            dve.drain().then_inc(rope_steps, 1)
            dve.wait_ge(rope_ready, 1)
            s3, k3 = ang.rearrange("p (t i) -> p t i", t=TT_), cosang.rearrange("p (t i) -> p t i", t=TT_)
            dve.tensor_scalar(rope_s[:, :, 0:8], s3, -1.0, None, ALU.mult)
            dve.tensor_copy(rope_s[:, :, 8:16], s3)
            dve.tensor_copy(rope_c[:, :, 0:8], k3)
            dve.tensor_copy(rope_c[:, :, 8:16], k3)
            dve.wait_ge(const_ready, 2)
            first, second = slice(0, CH), slice(CH, 2 * CH)
            dve.tensor_copy(ident64[second, :], ident64[first, :])
            dve.tensor_copy(upto[second, :], upto[first, :])
            dve.tensor_copy(sum_upto[second, second], sum_upto[first, first])
            dve.tensor_copy(after[second, second], after[first, first])
            dve.tensor_copy(level_mask[second, :, :], level_mask[first, :, :])
            dve.drain()

            with dve.Fori(0, depth) as l:

                def split_lo(p):
                    if p >= N_PIECES:
                        return
                    n = 4 * 288 if p // 2 == U_TAIL else PIECE
                    dve.wait_ge(*sig(l, "hi_done", p + 1))
                    tt(w_lo[:, p % 2, 0:n], raw[:, p % 2, 0:n], w_hi[:, p % 2, 0:n], ALU.subtract).then_inc(sems["split"], 1)

                def normalize(which, t):
                    dve.wait_ge(*sig(l, "rstd", 4 * which + t + 1))
                    dve.tensor_scalar(xo[:, t, :], x_res[:, t, :], rstd[:, t:t + 1], None,
                                      ALU.mult).then_inc(sems["normed"], 1)

                def h_rest(which, gain):
                    for kc in range(KC):
                        dve.wait_ge(*sig(l, "h_hi", 8 * which + kc + 1))
                        bank = turned_bank(which, kc)
                        if gain is None:
                            tt(h_lo[:, kc, :], bank[:, :], h_hi[:, kc, :], ALU.subtract).then_inc(sems["h_ready"], 1)
                        else:
                            dve.scalar_tensor_tensor(out=h_lo[:, kc, :], in0=bank[:, :], scalar=gain[:, kc:kc + 1],
                                                     in1=h_hi[:, kc, :], op0=ALU.mult,
                                                     op1=ALU.subtract).then_inc(sems["h_ready"], 1)

                for t in range(TT_):
                    normalize(0, t)
                dve.memset(conv_in[:, :, 0:4], 0.0)
                split_lo(0)
                split_lo(1)
                dve.wait_ge(*sig(l, "par_ready", 1))
                h_rest(0, gain_attn)
                for u in range(U_GV + 1):
                    split_lo(2 * u + 2)
                    for j in range(4):
                        dve.wait_ge(*sig(l, "proj_evac", 4 * u + j + 1))
                        if u > 0:
                            dve.wait_ge(*sig(l, "gsilu", 4 * (u - 1) + j + 1))
                        col = 4 * u + j
                        dve.tensor_scalar(conv_out[:, j, :], conv_in[:, j, 4:4 + T], gdn_taps[:, 3, col:col + 1], None,
                                          ALU.mult)
                        for s in (1, 2, 3):
                            dve.drain()
                            last = dve.scalar_tensor_tensor(
                                out=conv_out[:, j, :], in0=conv_in[:, j, 4 - s:4 - s + T],
                                scalar=gdn_taps[:, 3 - s, col:col + 1], in1=conv_out[:, j, :], op0=ALU.mult, op1=ALU.add)
                        last.then_inc(sems["gconv"], 1)
                    split_lo(2 * u + 3)
                split_lo(2 * U_TAIL + 2)
                split_lo(2 * U_TAIL + 3)
                dve.wait_ge(bc_loaded, (l * 7 + 7) * 16)
                dve.wait_ge(*sig(l, "proj_evac", 16))
                y3 = gy.rearrange("p (t h) -> p t h", t=TT_)
                tt(y3, pj[:, :, PJ_A:PJ_A + 4], over(bc_dt, 1, TT_), ALU.add)
                dve.drain()
                dve.tensor_scalar(gn, gy, -1.0, None, ALU.mult)
                dve.drain()
                tt(gn, gn, gy, ALU.min).then_inc(sems["ga_in"], 1)
                dve.wait_ge(*sig(l, "ga_exp", 1))
                dve.scalar_tensor_tensor(out=gdec, in0=gy, scalar=0.0, in1=gn, op0=ALU.max, op1=ALU.add)
                dve.tensor_scalar(bE, bE, 1.0, None, ALU.add)
                dve.tensor_scalar(gE, gE, 1.0, None, ALU.add)
                dve.drain()
                g3 = gdec.rearrange("p (t h) -> p t h", t=TT_)
                tt(g3, g3, over(aE, 1, TT_), ALU.mult)
                dve.reciprocal(beta, bE)
                dve.reciprocal(gate, gE)
                dve.drain()
                dve.tensor_scalar(gdec, gdec, -1.0, None, ALU.mult).then_inc(sems["ga_out"], 1)
                dve.drain()
                gate4 = gate.rearrange("p (t h b) -> p t h b", t=TT_, h=NH)

                def deltanet():
                    lanes = 2 * GH

                    def level(k):
                        tt(ltT[k % 2][:, :, :], akkT[:, :, :], over(level_mask[:, k, :], 1, lanes),
                           ALU.mult).then_inc(sems["lt_ready"], 1)

                    def lanes_of(bank):
                        return ps[bank][:, :].rearrange("p (k n) -> p k n", k=lanes)

                    def output_squares(r):
                        dve.wait_ge(*sig(l, "og_ready", 2 * r + 2))
                        dve.tensor_reduce(o_ss, og_sq, AX.X, ALU.add).then_inc(sems["oss"], 1)

                    def finish_tile(r):
                        dve.wait_ge(*sig(l, "orr", r + 1))
                        tt(og, og, over(o_rr, 2, GD), ALU.mult)
                        dve.drain()
                        tt(og, og, over(bc_go, 1, GH), ALU.mult)
                        dve.drain()
                        z = h4(xo[:, r, 512:1024])
                        tt(z, og, z, ALU.mult).then_inc(sems["o_written"], 1)

                    for b in range(2):
                        for r in (2 * b, 2 * b + 1):
                            rb = r % 2
                            be = beta[:, 4 * r:4 * r + 4]
                            dve.wait_ge(*sig(l, "raw_psum", 3 * r + 3))
                            tt(of_tile(2, r), h4(ps[7][:, :]), over(be, 2, GD), ALU.mult)
                            tt(g_upto[:, :, :], over(upto[:, :], 1, GH), over(gdec[:, 4 * r:4 * r + 4], 2, CH), ALU.mult)
                            dve.drain().then_inc(sems["vb_ready"], 1)
                            if r == 2:
                                output_squares(1)
                            yield
                            dve.wait_ge(*sig(l, "rr_ready", r + 1))
                            dve.wait_ge(*sig(l, "gcum_exp", 1))
                            e_cum, e_rest = ex[:, 4 * r:4 * r + 4], ex[:, 16 + 4 * r:20 + 4 * r]
                            s_q, s_qg, s_kb, s_kbg, s_kd = (g_sc[:, 4 * i:4 * i + 4] for i in range(5))
                            dve.tensor_scalar(s_q, g_rr[:, 0:4], float(GD) ** -0.5, None, ALU.mult)
                            tt(s_kb, g_rr[:, 4:8], be, ALU.mult)
                            tt(s_kd, g_rr[:, 4:8], e_rest, ALU.mult)
                            dve.drain()
                            tt(s_qg, s_q, e_cum, ALU.mult)
                            tt(s_kbg, s_kb, e_cum, ALU.mult)
                            dve.drain()
                            q_, k_ = raw_qk[:, 0, :, :], raw_qk[:, 1, :, :]
                            for o, src, sc in ((forms_sb[:, 0, :, :], k_, g_rr[:, 4:8]), (forms_sb[:, 1, :, :], k_, s_kb),
                                               (forms_sb[:, 2, :, :], q_, s_q), (forms_sb[:, 3, :, :], q_, s_qg),
                                               (of_tile(0, r), k_, s_kbg), (of_tile(1, r), k_, s_kd)):
                                tt(o, src, over(sc, 2, GD), ALU.mult)
                            dve.drain().then_inc(sems["forms"], 1)
                            if r == 2:
                                finish_tile(1)
                            yield
                            dve.wait_ge(*sig(l, "dt_exp", r + 1))
                            tt(decayT[:, :, :], decayT[:, :, :], over(upto[:, :], 1, GH), ALU.mult)
                            dve.drain()
                            yield
                            dve.wait_ge(*sig(l, "kk_psum", r + 1))
                            kk = ps[6][:, :].rearrange("p (f h n) -> p f h n", f=2, h=GH)
                            tt(akkT[:, GH * rb:GH * rb + GH, :], kk[:, 0, :, :], decayT[:, :, :], ALU.mult)
                            tt(aqkT[:, GH * rb:GH * rb + GH, :], kk[:, 1, :, :], decayT[:, :, :], ALU.mult)
                            dve.drain().then_inc(sems["a_ready"], 1)
                            if rb == 1:
                                level(0)
                                dve.drain()
                                tt(xiT[:, :, :], over(ident64[:, :], 1, lanes), lt_even[:, :, :],
                                   ALU.subtract).then_inc(sems["xiT_ready"], 1)
                                level(1)
                            yield
                        dve.wait_ge(*sig(l, "y_psum", 6 * b + 1))
                        tt(xi[:, :, :], over(ident64[:, :], 1, lanes), lanes_of(5), ALU.subtract).then_inc(sems["xi_ready"], 1)
                        dve.drain()
                        yield
                        for k in range(1, 6):
                            if k < 5:
                                dve.wait_ge(*sig(l, "y_psum", 6 * b + k))
                                level(k + 1)
                            yield
                            if k < 5:
                                dve.wait_ge(*sig(l, "xi_psum", 4 * b + k))
                                tt(xi[:, :, :], xi[:, :, :], lanes_of(6), ALU.subtract).then_inc(sems["xi_ready"], 1)
                            dve.wait_ge(*sig(l, "xiT_psum", 5 * b + k))
                            tt(xiT[:, :, :], xiT[:, :, :], lanes_of(7), ALU.subtract).then_inc(sems["xiT_ready"], 1)
                            dve.drain()
                            yield
                        if b == 0:
                            dve.memset(state, 0.0).then_inc(sems["s_ready"], 1)
                        yield
                        yield
                        for n in range(4 * b, 4 * b + 4):
                            r, c = n // 2, n % 2
                            rows = slice(CH * c, CH * c + CH)
                            dve.wait_ge(*sig(l, "ws_psum", n + 1))
                            tt(v_new[rows, :, :], u_sb[rows, r % 2, :, :], h4(ps[6 + c][rows, :]),
                               ALU.subtract).then_inc(sems["vn_ready"], 1)
                            if n % 4 == 2:
                                output_squares(r - 1)
                            yield
                            dve.wait_ge(*sig(l, "su_psum", n + 1))
                            dve.wait_ge(*sig(l, "sg_ready", n + 1))
                            tt(state, state_g, h4(ps[5][:, :]), ALU.add).then_inc(sems["s_ready"], 1)
                            if n % 4 == 2:
                                finish_tile(r - 1)
                            yield
                    output_squares(3)
                    yield
                    finish_tile(3)
                    yield

                dve.tensor_scalar(q_gain, bc_q, float(DH) ** -0.5, None, ALU.mult)

                def heads(ap, n):
                    return ap.rearrange("p (h d) -> p h d", h=n)

                def q_of(t, n=2):
                    return pj[:, t:t + n, 0:512].rearrange("p t (h d) -> p t h d", h=NH)

                def k_of(b, t, n=2):
                    return pj[:, t:t + n, 512 + 256 * b:640 + 256 * b].rearrange("p t (g d) -> p t g d", g=NG)

                def over2(ap):
                    return lambda n: over(over(ap, 1, n), 1, 2)

                def norms_and_rope():
                    for t in (0, 2):
                        q2 = xo[:, 0:2, 0:512].rearrange("p t (h d) -> p t h d", h=NH)
                        k2 = xo[:, 2, 0:512].rearrange("p (t h d) -> p t h d", t=2, h=4)
                        tt(q2, q_of(t), q_of(t), ALU.mult)
                        for b in range(2):
                            tt(k2[:, :, 2 * b:2 * b + 2, :], k_of(b + 1, t), k_of(b + 1, t), ALU.mult)
                        dve.drain()
                        ss = qk_ss[:, 12 * t:12 * t + 24].rearrange("p (t h) -> p t h", t=2)
                        dve.tensor_reduce(ss[:, :, 0:8], q2, AX.X, ALU.add)
                        dve.tensor_reduce(ss[:, :, 8:12], k2, AX.X, ALU.add)
                        dve.drain().then_inc(sems["qk_squares"], 1)
                        yield
                    for t in (0, 2):
                        dve.wait_ge(*sig(l, "qk_rstd", t // 2 + 1))
                        rs = qk_rs[:, 12 * t:12 * t + 24].rearrange("p (t h) -> p t h", t=2)
                        tt(q_of(t), q_of(t), over(rs[:, :, 0:8], 3, DH), ALU.mult)
                        for b in range(2):
                            tt(k_of(b + 1, t), k_of(b + 1, t), over(rs[:, :, 8 + 2 * b:10 + 2 * b], 3, DH), ALU.mult)
                        dve.drain()
                        yield
                        tt(q_of(t), q_of(t), over2(q_gain)(NH), ALU.mult)
                        for b in range(2):
                            tt(k_of(b + 1, t), k_of(b + 1, t), over2(bc_k[:, b + 1, :])(NG), ALU.mult)
                        dve.drain()
                        yield
                        parts, col = [], 0
                        for xx, n in ((q_of(t), NH), (k_of(0, t), NG), (k_of(1, t), NG), (k_of(2, t), NG)):
                            m1, m2 = (xo[:, i, col:col + 32 * n].rearrange("p (t h d) -> p t h d", t=2, h=n) for i in range(2))
                            parts.append((xx, m1, m2, n))
                            col += 32 * n
                        for xx, m1, m2, n in parts:
                            tt(m1, xx[:, :, :, 0:16], over(rope_c[:, t:t + 2, :], 2, n), ALU.mult)
                            tt(m2[:, :, :, 0:8], xx[:, :, :, 8:16], over(rope_s[:, t:t + 2, 0:8], 2, n), ALU.mult)
                            tt(m2[:, :, :, 8:16], xx[:, :, :, 0:8], over(rope_s[:, t:t + 2, 8:16], 2, n), ALU.mult)
                        dve.drain()
                        yield
                        for xx, m1, m2, n in parts:
                            tt(xx[:, :, :, 0:16], m1, m2, ALU.add)
                        dve.drain()
                        yield
                    dve.drain().then_inc(sems["q_ready"], 1)

                steps = deltanet()
                norms = norms_and_rope()
                for u in (U_KV, U_Q, U_Z):
                    for j in range(8):
                        if j == 3:
                            split_lo(2 * u + 2)
                        if j in UNIT_STEPS[u]:
                            next(steps)
                        if u == U_Z:
                            if j == 0:
                                dve.wait_ge(*sig(l, "proj_evac", 24))
                            next(norms)
                    if u < U_Z:
                        split_lo(2 * u + 3)
                for _ in norms:
                    pass
                split_lo(2 * U_Z + 3)



                def blocks(kv):
                    dve.wait_ge(*sig(l, "blkT_psum", kv + 1))
                    if kv == 0:
                        dve.memset(blk[:, :, :].rearrange("p m (g n) -> p m g n", g=NG)[:, :, :, 31], 0.0)
                        dve.drain()
                    else:
                        dve.wait_ge(*sig(l, "blk_hi", 1))
                    for g in range(NG):
                        for s in range(2):
                            rows = slice(64 * g, 64 * g + 64)
                            src = ps[kv][rows, :].rearrange("p (n m s) -> p s m n", m=8, s=2)
                            for half in range(2):
                                o = blk[64 * s:64 * s + 64, 8 * half:8 * half + 8, 32 * g:32 * g + 31]
                                pe_b = over(pe_kv[64 * s:64 * s + 64, kv, 8 * half:8 * half + 8], 2, 31)
                                tt(o, src[:, s, :, half:half + 31], pe_b, ALU.add)
                    dve.drain().then_inc(sems["blk_f32"], 1)
                    if kv == 1:
                        split_lo(2 * U_CV)
                    dve.wait_ge(*sig(l, "blk_hi", kv + 1))
                    tt(blk_lo[:, :, :], blk[:, :, :], blk_hi[:, :, :], ALU.subtract).then_inc(sems["blk_ready"], 1)

                blocks(0)
                dve.drain()
                next(steps)
                blocks(1)
                split_lo(2 * U_CV + 1)
                next(steps, None)
                next(steps, None)
                next(steps, None)
                dve.wait_ge(*sig(l, "cmp2_psum", 1))
                dve.tensor_copy(kc_rows[:, :], ps[1][0:64, 0:DH])
                dve.tensor_copy(vc_rows[:, :], ps[1][0:64, DH:2 * DH])
                dve.memset(vc_diag[:, :], 0.0)
                dve.memset(kcT[:, :, :], 0.0)
                dve.drain()
                tt(kc_sq[:, :], kc_rows[:, :], kc_rows[:, :], ALU.mult)
                dve.drain()
                dve.tensor_reduce(kc_ss, kc_sq[:, :], AX.X, ALU.add).then_inc(sems["kc_ss"], 1)
                for h in range(4):
                    g = h % NG
                    dve.tensor_copy(vc_diag[32 * h:32 * h + 32, DH * h:DH * h + DH], vc_rows[32 * g:32 * g + 32, :])
                dve.drain().then_inc(sems["vc_ready"], 1)
                next(steps, None)
                dve.wait_ge(*sig(l, "kc_rstd", 1))
                dve.scalar_tensor_tensor(out=kc_rows[:, :], in0=kc_rows[:, :], scalar=kc_rr, in1=bc_k[0:64, 0, :],
                                         op0=ALU.mult, op1=ALU.mult)
                dve.drain()
                for g in range(NG):
                    dve.tensor_copy(kc_two[:, DH * g:DH * g + DH], kc_rows[32 * g:32 * g + 32, :])
                dve.drain().then_inc(sems["kc_ready"], 1)
                next(steps, None)
                c_all = c_prob[:, :, :].rearrange("p t (h n) -> p t h n", h=NH)
                for i in range(2):
                    cp, tiles = c_all[:, 2 * i:2 * i + 2, :, :], slice(2 * i, 2 * i + 2)
                    cm = c_max[:, 16 * i:16 * i + 16].rearrange("p (t h) -> p t h", t=2)
                    dve.wait_ge(*sig(l, "cs_psum", i + 1))
                    tt(cp, ps[i][:, :].rearrange("p (t h n) -> p t h n", t=2, h=NH), over(cmp_add[:, tiles, :], 2, NH), ALU.add)
                    dve.drain()
                    dve.tensor_reduce(cm, cp, AX.X, ALU.max)
                    dve.drain()
                    tt(cp, cp, over(cm, 3, 32), ALU.subtract).then_inc(sems["cs_shift"], 1)
                for i in range(2):
                    cp, tiles = c_all[:, 2 * i:2 * i + 2, :, :], slice(2 * i, 2 * i + 2)
                    dve.wait_ge(*sig(l, "cs_exp", i + 1))
                    tt(cp, cp, over(cmp_mul[:, tiles, :], 2, NH), ALU.mult).then_inc(sems["cp_ready"], 1)
                next(steps, None)
                dve.wait_ge(*sig(l, "stack_hi", 1))
                for g in range(NG):
                    rows, other = slice(DH * g, DH * g + DH), slice(DH * (1 - g), DH * (1 - g) + DH)
                    tt(q_stack[other, 4 * g:4 * g + 4, :], qT[rows, :, :], q_stack[rows, 4 * g:4 * g + 4, :], ALU.subtract)
                dve.drain().then_inc(sems["q_stacked"], 1)
                dve.drain()
                dve.tensor_reduce(c_sum.rearrange("p (t h) -> p t h", t=TT_), c_all, AX.X, ALU.add)
                dve.drain()
                dve.tensor_scalar(c_sum, c_sum, 1e-30, None, ALU.max)
                dve.drain()
                dve.reciprocal(c_coef, c_sum)
                dve.drain()
                for t in range(TT_):
                    cc = c_coef[:, 8 * t:8 * t + 8].rearrange("p (n g) -> p n g", g=NG)
                    tt(cc, cc, gate4[:, t, :, 0].rearrange("p (g n) -> p n g", g=NG), ALU.mult)
                dve.drain()
                next(steps, None)
                for t in range(TT_):
                    cc = c_coef[:, 8 * t:8 * t + 8].rearrange("p (n g) -> p n g", g=NG)
                    dve.wait_ge(*sig(l, "co_psum", t + 1))
                    tt(xo[:, t, 0:512].rearrange("p (g n d) -> p n g d", g=NG, d=DH),
                       ps[(4, 0, 1, 2)[t]][:, :].rearrange("p (n g d) -> p n g d", g=NG, d=DH), over(cc, 3, DH),
                       ALU.mult).then_inc(sems["o_init"], 1)
                next(steps, None)

                def add_branch(k):
                    t, b, _ = item(NH * k)
                    dve.wait_ge(*sig(l, "p_ready", 8 * k + 8))
                    dve.reciprocal(coef, row_sum[:, 8 * k:8 * k + 8])
                    dve.drain()
                    tt(coef, coef, gate4[:, t, :, 1 + b], ALU.mult)
                    dve.drain()
                    dve.wait_ge(*sig(l, "pv_done", 8 * k + 8))
                    tt(heads(o_tmp[:, k % 2, :], NH), heads(ps[4][:, :], NH), over(coef, 2, DH),
                       ALU.mult).then_inc(sems["o_added"], 1)
                    dve.drain()
                    tt(xo[:, t, 0:512], xo[:, t, 0:512], o_tmp[:, k % 2, :], ALU.add)

                def norm_squares(t):
                    dve.drain()
                    tt(o_tmp[:, t % 2, :], xo[:, t, 0:512], xo[:, t, 0:512], ALU.mult)
                    dve.drain()
                    dve.tensor_reduce(no_ss[:, 8 * t:8 * t + 8], heads(o_tmp[:, t % 2, :], NH), AX.X,
                                      ALU.add).then_inc(sems["no_ss"], 1)
                    dve.drain()

                def norm_scale(t):
                    dve.wait_ge(*sig(l, "no_rstd", TILES.index(t) + 1))
                    o = heads(xo[:, t, 0:512], NH)
                    tt(o, o, over(no_rr[:, 8 * t:8 * t + 8], 2, DH), ALU.mult)
                    dve.drain()
                    tt(xo[:, t, 0:512], xo[:, t, 0:512], bc_no, ALU.mult).then_inc(sems["o_final"], 1)

                def row_max(i):
                    n = (item(i)[0] + 1) * P
                    dve.wait_ge(*sig(l, "s_psum", i + 1))
                    dve.tensor_reduce(neg_max[:, i:i + 1], ps[i % 2][:, 0:n], AX.X, ALU.max,
                                      negate=True).then_inc(sems["negmax"], 1)

                row_max(0)
                row_max(1)
                for i in range(N_ITEMS):
                    if i + 2 < N_ITEMS:
                        row_max(i + 2)
                    if item_step(i):
                        next(steps, None)
                    if i >= 8 and i % 8 == 0:
                        add_branch(i // 8 - 1)
                    if i >= 16 and i % 16 == 3:
                        norm_squares(item(i - 16)[0])
                    if i >= 16 and i % 16 == 5:
                        norm_scale(item(i - 16)[0])
                add_branch(7)
                norm_squares(TILES[-1])
                split_lo(2 * U_O0)
                norm_scale(TILES[-1])
                split_lo(2 * U_O0 + 1)
                dve.drain()
                dve.memset(conv_in[:, :, 0:4], 0.0)
                h_rest(1, None)
                for u in (U_O0, U_O0 + 1):
                    split_lo(2 * u + 2)
                    if u == U_O0:
                        split_lo(2 * u + 3)
                    c = (u - U_O0) * 512
                    for j in range(4):
                        dve.wait_ge(*task_done(l, u, j))
                        xs = x_res[:, j, c:c + 512]
                        tt(xs, xs, ps[4 * (u % 2) + j][:, :], ALU.add).then_inc(sems["x_added"], 1)
                        if u == U_O0 + 1 and j >= 1:
                            normalize(1, j - 1)
                normalize(1, 3)
                dve.sem_inc(sems["params_free"], 1)
                split_lo(2 * U_UP + 1)
                h_rest(2, gain_ffn)
                def hidden_lo(k):
                    dve.wait_ge(*sig(l, "g_hi_done", k + 1))
                    tt(g_lo[:, k % 2, :], g_mlp[:, k, :], g_hi[:, k % 2, :], ALU.subtract).then_inc(sems["g_split"], 1)

                for i in range(N_UP):
                    u = U_UP + i
                    split_lo(2 * u + 2)
                    if i == N_UP - 1:
                        hidden_lo(0)
                        hidden_lo(1)
                    for j in range(4):
                        col = 2 * i + j if j < 2 else FK + 2 * i + j - 2
                        dve.wait_ge(*sig(l, "ffn_copied", 4 * i + j + 1))
                        dve.tensor_scalar(conv_out[:, j, :], conv_in[:, j, 4:4 + T], ffn_tap2[:, col:col + 1],
                                          ffn_bias[:, col:col + 1], ALU.mult, ALU.add)
                        for s in (1, 2):
                            dve.drain()
                            dve.scalar_tensor_tensor(
                                out=conv_out[:, j, :], in0=conv_in[:, j, 4 - s:4 - s + T],
                                scalar=ffn_taps01[:, 2 - s, col:col + 1], in1=conv_out[:, j, :], op0=ALU.mult, op1=ALU.add)
                        dve.drain().then_inc(sems["ffn_conv"], 1)
                    split_lo(2 * u + 3)
                    for j in range(2):
                        dve.wait_ge(*sig(l, "silu_ready", 2 * i + j + 1))
                        tt(g_mlp[:, 2 * i + j, :], conv_out[:, j, :], conv_out[:, 2 + j, :],
                           ALU.mult).then_inc(sems["g_ready"], 1)
                    dve.drain()
                for k in range(2, FK):
                    hidden_lo(k)
                    if k % 2 == 0 and k > 0:
                        split_lo(2 * U_DN + k // 2 + 1)
                for i in range(8):
                    if i < 7:
                        dve.wait_ge(*sig(l, "down_done", i + 1))
                    else:
                        dve.wait_ge(*sig(l, "even_used", N_UNITS))
                    xs = x_res[:, i // 2, (i % 2) * 512:(i % 2) * 512 + 512]
                    tt(xs, xs, ps[i][:, :], ALU.add).then_inc(sems["x_added"], 1)

        @block.tensor
        def _(pe):
            def three(o, a, b, start, stop):
                pe.matmul(o, a[0], b[0], start=start, stop=False)
                pe.matmul(o, a[0], b[1], start=False, stop=False)
                return pe.matmul(o, a[1], b[0], start=False, stop=stop)

            pe.wait_ge(const_ready, 2)
            with pe.Fori(0, depth) as l:

                def turn_rows(which, ready, bank_free):
                    for t in range(TT_):
                        ready(t)
                        for kc in range(KC):
                            if t == 0:
                                bank_free(kc)
                            last = pe.transpose(turned_bank(which, kc)[:, t * P:(t + 1) * P],
                                                xo[:, t, kc * P:(kc + 1) * P], ident[:, :])
                            if t == TT_ - 1:
                                last.then_inc(sems["hT_psum"], 1)

                def dense(u, which, bank_free, after_task=lambda j: None):
                    up = U_UP <= u < U_DN
                    channels = u <= U_GV or up
                    width = 288 if u == U_TAIL else 512
                    for a in range(2):
                        pe.wait_ge(*sig(l, "split", 2 * u + a + 1))
                        hi = w_hi[:, a, 0:4 * width].rearrange("p (k n) -> p k n", k=4)
                        lo = w_lo[:, a, 0:4 * width].rearrange("p (k n) -> p k n", k=4)
                        for j in range(4):
                            if a == 0:
                                bank_free(j)
                            bank = ps[j if u <= U_Z else 4 * (u % 2) + j]
                            for k in range(4):
                                kc = 4 * a + k
                                if j == 0:
                                    pe.wait_ge(*sig(l, "h_ready", 8 * which + kc + 1))
                                h = (h_hi[:, kc, :], h_lo[:, kc, :])
                                st, sp_ = kc == 0, kc == KC - 1
                                if channels:
                                    w = (hi[:, k, P * j:P * j + P], lo[:, k, P * j:P * j + P])
                                    last = three(bank[:, :], w, h, st, sp_)
                                else:
                                    h = (h[0][:, P * j:P * j + P], h[1][:, P * j:P * j + P])
                                    last = three(bank[:, 0:width], h, (hi[:, k, :], lo[:, k, :]), st, sp_)
                            if j == 3:
                                last.then_inc(sems["odd_used" if a else "even_used"], 1)
                            elif a == 1:
                                last.then_inc(sems["dense_done"], 1)
                            after_task(4 * a + j)

                def wait(name, k):
                    pe.wait_ge(*sig(l, name, k))

                pe.wait_ge(par_loaded, (l * 7 + 7) * 16)
                wait("x_added", 1 - 8)
                for b, n in ((0, 108), (1, 88), (2, 76)):
                    last = pe.transpose(ps[0][:, b * P:b * P + n], par_rows[0:n, b, :], ident[0:n, 0:n])
                last.then_inc(sems["par_psum"], 1)
                turn_rows(0, lambda t: wait("normed", t + 1),
                          lambda kc: wait("par_ready", 1) if kc == 0 else wait("x_added", kc + 1 - 8))
                def decay_sums():
                    wait("ga_out", 1)
                    for i, m in enumerate((sum_upto[:, :], after[:, :], chunk_rows[:, 0, :], chunk_rows[:, 1, :])):
                        last = pe.matmul(ps[4][:, 16 * i:16 * i + 16], m, gdec, start=True, stop=True)
                    last.then_inc(sems["gcum_psum"], 1)

                def deltanet():
                    def lanes_mm(bank, lhs, rhs):
                        pe.sem_inc(pe_steps, 1)
                        for k in range(2 * GH):
                            for c in range(2):
                                rows = slice(CH * c, CH * c + CH)
                                r_ = rhs[rows, k, :] if rhs is not None else ident64[rows, :]
                                last = pe.matmul(ps[bank][rows, CH * k:CH * k + CH], lhs[rows, k, :], r_,
                                                 start=True, stop=True)
                        return last

                    wait("gsilu", 12)
                    for b in range(2):
                        for r in (2 * b, 2 * b + 1):
                            rb = r % 2
                            if r == 2:
                                wait("og_ready", 4)
                                wait("s_ready", 5)
                            elif rb == 1:
                                wait("formsT_ready", 4 * r)
                                wait("a_ready", r)
                            for f in range(3):
                                for h in range(GH):
                                    last = pe.transpose(ps[5 + f][:, P * h:P * h + P],
                                                        qkvT[:, GH * f + h, r * P:(r + 1) * P], ident[:, :])
                                last.then_inc(sems["raw_psum"], 1)
                            yield
                            wait("vb_ready", r + 1)
                            pe.matmul(ps[7][:, 0:GH * CH], after[:, :], g_upto[:, :, :].rearrange("p h n -> p (h n)"),
                                      start=True, stop=True).then_inc(sems["decay_psum"], 1)
                            yield
                            wait("forms", r + 1)
                            for f in range(3):
                                if f == 2:
                                    wait("dt_exp", r + 1)
                                for h in range(GH):
                                    last = pe.transpose(ps[5 + f][:, P * h:P * h + P], forms_sb[:, f, h, :], ident[:, :])
                                last.then_inc(sems["formsT_psum"], 1)
                            yield
                            wait("formsT_ready", 4 * r + 1)
                            for h in range(GH):
                                last = pe.transpose(ps[5][:, P * h:P * h + P], forms_sb[:, 3, h, :], ident[:, :])
                            last.then_inc(sems["formsT_psum"], 1)
                            wait("formsT_ready", 4 * r + 3)
                            pe.sem_inc(pe_steps, 1)
                            for f, other in ((0, 1), (1, 2)):
                                for h in range(GH):
                                    for c in range(2):
                                        rows = slice(CH * c, CH * c + CH)
                                        last = pe.matmul(ps[6][rows, 256 * f + CH * h:256 * f + CH * h + CH],
                                                         formsT[:, 0, h, rows], formsT[:, other, h, rows], start=True, stop=True)
                            last.then_inc(sems["kk_psum"], 1)
                            yield
                        wait("lt_ready", 6 * b + 1)
                        wait("formsT_ready", 8 * b + 8)
                        lanes_mm(5, lt_even, None).then_inc(sems["y_psum"], 1)
                        yield
                        for k in range(1, 6):
                            wait("lt_ready", 6 * b + k + 1)
                            wait("xi_ready", 5 * b + k)
                            lanes_mm(5, ltT[k % 2], xi).then_inc(sems["y_psum"], 1)
                            yield
                            wait("y_ready", 5 * b + k)
                            wait("xiT_ready", 6 * b + k)
                            if k < 5:
                                lanes_mm(6, xiT, yy).then_inc(sems["xi_psum"], 1)
                            lanes_mm(7, yy, xiT).then_inc(sems["xiT_psum"], 1)
                            yield
                        wait("xiT_ready", 6 * b + 6)
                        pe.sem_inc(pe_steps, 1)
                        for rb in range(2):
                            r = 2 * b + rb
                            if rb == 1:
                                wait("uw_ready", 2 * b + 1)
                                pe.sem_inc(pe_steps, 1)
                            for h in range(GH):
                                for c in range(2):
                                    rows = slice(CH * c, CH * c + CH)
                                    last = pe.matmul(ps[5][rows, P * h:P * h + P], xiT[rows, GH * rb + h, :],
                                                     of_tile(2, r)[rows, h, :], start=True, stop=True)
                            if rb == 0:
                                for r2 in range(2):
                                    for h in range(GH):
                                        for c in range(2):
                                            rows = slice(CH * c, CH * c + CH)
                                            col = 256 * r2 + CH * h
                                            last = pe.matmul(ps[6 + c][:, col:col + CH], of_tile(0, 2 * b + r2)[rows, h, :],
                                                             xiT[rows, GH * r2 + h, :], start=True, stop=True)
                            last.then_inc(sems["uw_psum"], 1)
                            yield
                        for n in range(4 * b, 4 * b + 4):
                            r, c = n // 2, n % 2
                            rb = r % 2
                            rows, other = slice(CH * c, CH * c + CH), slice(CH * (1 - c), CH * (1 - c) + CH)
                            bank = ps[6 + c]
                            wait("uw_ready", 2 * b + 2)
                            wait("s_ready", n + 1)
                            if n % 4 >= 2:
                                wait("og_ready", n - 1)
                            for h in range(GH):
                                last = pe.matmul(bank[:, P * h:P * h + P], wq[:, rb, h, P * c:P * c + P], state[:, h, :],
                                                 start=h == 0, stop=False, skip_group_check=True)
                            last.then_inc(sems["ws_psum"], 1)
                            yield
                            wait("vn_ready", n + 1)
                            for h in range(GH):
                                last = pe.matmul(ps[5][:, P * h:P * h + P], of_tile(1, r)[rows, h, :], v_new[rows, h, :],
                                                 start=True, stop=True)
                            last.then_inc(sems["su_psum"], 1)
                            for h in range(GH):
                                last = pe.matmul(bank[other, P * h:P * h + P], aqkT[rows, GH * rb + h, :], v_new[rows, h, :],
                                                 start=False, stop=h == GH - 1, skip_group_check=True)
                            last.then_inc(sems["oc_psum"], 1)
                            yield
                    yield
                    yield

                steps = deltanet()

                def task_step(u, j):
                    if u == U_KV and j == 2:
                        decay_sums()
                    if j in UNIT_STEPS.get(u, ()):
                        next(steps)

                for u in range(U_Z + 1):
                    dense(u, 0, lambda j: wait("proj_evac", 4 * (u - 1) + j + 1) if u else wait("h_ready", j + 1),
                          lambda j: task_step(u, j))

                wait("proj_evac", 28)
                wait("q_ready", 1)
                wait("gcum_exp", 1)
                for i, (bank, col) in enumerate(((0, 512), (1, 640), (2, 0), (3, P), (4, 2 * P), (2, 3 * P), (3, 768), (4, 1024))):
                    if i >= 5:
                        wait("qkT_ready", i - 4)
                    for t in range(TT_):
                        last = pe.transpose(ps[bank][:, t * P:(t + 1) * P], pj[:, t, col:col + P], ident[:, :])
                    last.then_inc(sems["blkT_psum" if i < 2 else "qkT_psum"], 1)
                next(steps)
                for kv in range(2):
                    u = U_CK + kv
                    wait("blk_ready", kv + 1)
                    wait("qkT_ready", 5 + kv)
                    for a in range(2):
                        wait("split", 2 * u + a + 1)
                        pe.sem_inc(pe_steps, 1)
                        hi = w_hi[:, a, :].rearrange("p (m n) -> p m n", m=8)
                        lo = w_lo[:, a, :].rearrange("p (m n) -> p m n", m=8)
                        for m in range(8):
                            last = three(ps[3 + kv][0:64, 0:HID], (blk_hi[:, 8 * a + m, :], blk_lo[:, 8 * a + m, :]),
                                         (hi[:, m, :], lo[:, m, :]), a == 0 and m == 0, a == 1 and m == 7)
                        last.then_inc(sems["odd_used" if a else "even_used"], 1)
                    next(steps, None)
                wait("hid_silu", 2)
                wait("blk_f32", 1)
                pe.sem_inc(pe_steps, 1)
                for kv in range(2):
                    for s in range(2):
                        c = 64 * (2 * kv + s)
                        last = pe.transpose(ps[0][:, c:c + 64], hid_rows[:, kv, P * s:P * s + P], ident[0:64, 0:64])
                last.then_inc(sems["hid_psum"], 1)
                next(steps, None)
                pe.wait_ge(bc_loaded, (l * 7 + 7) * 16)
                wait("hid_ready", 1)
                wait("blk_f32", 2)
                pe.sem_inc(pe_steps, 1)
                for kv in range(2):
                    for s in range(2):
                        last = pe.matmul(ps[1][0:64, DH * kv:DH * kv + DH], hid[:, kv, s, :], cmp_w2_sb[:, kv, s, :],
                                         start=s == 0, stop=s == 1)
                last.then_inc(sems["cmp2_psum"], 1)
                next(steps, None)
                wait("kc_ready", 1)
                pe.sem_inc(pe_steps, 1)
                pe.transpose(ps[2][:, 0:32], kc_two[:, :], ident[0:32, 0:32]).then_inc(sems["kcT_psum"], 1)
                next(steps, None)

                wait("kcT_ready", 1)
                wait("vc_ready", 1)

                for t in range(TT_):
                    if t == 0:
                        wait("hid_ready", 1)
                    for n in range(NH // NG):
                        col = 256 * (t % 2) + 64 * n
                        last = pe.matmul(ps[t // 2][:, col:col + 64], qT[:, n, t * P:(t + 1) * P],
                                         kcT[:, :, :].rearrange("p g n -> p (g n)"), start=True, stop=True)
                    if t % 2 == 1:
                        last.then_inc(sems["cs_psum"], 1)
                next(steps, None)
                for i in range(2):
                    wait("cp_ready", i + 1)
                    for t in (2 * i, 2 * i + 1):
                        for g in range(NG):
                            col = 256 * (t % 2) + P * g
                            last = pe.transpose(ps[2 + i][:, col:col + P], c_prob[:, t, P * g:P * g + P], ident[:, :])
                    last.then_inc(sems["cpT_psum"], 1)
                next(steps, None)
                for t in range(TT_):
                    wait("cpT_ready", t // 2 + 1)
                    for g in range(NG):
                        last = pe.matmul(ps[(4, 0, 1, 2)[t]][:, 256 * g:256 * g + 256], c_probT[:, t, P * g:P * g + P],
                                         vc_diag[:, :], start=True, stop=True)
                    last.then_inc(sems["co_psum"], 1)
                next(steps, None)

                def scores(i):
                    t, b, h = item(i)
                    if i >= 2:
                        wait("p_ready", i - 1)
                    else:
                        wait("o_init", 2 + i)
                    n = (t + 1) * P
                    for part in range(2):
                        pe.matmul(ps[i % 2][:, :], q_stack[:, h, t * P:(t + 1) * P], k_stack[:, part, b, h // 4, :],
                                  start=part == 0, stop=False)
                    pe.matmul(ps[i % 2][:, t * P:n], ident_bf[:, :], causal_bf[:, :],
                              start=False, stop=True).then_inc(sems["s_psum"], 1)

                def turn(i):
                    t = item(i)[0]
                    wait("p_ready", i + 1)
                    if i >= 2:
                        wait("pT_ready", i - 1)
                    elif i == 0:
                        wait("o_init", 4)
                    for j in range(t + 1):
                        last = pe.transpose(ps[2 + i % 2][:, j * P:(j + 1) * P], prob[:, i % 2, j * P:(j + 1) * P], ident[:, :])
                    last.then_inc(sems["pT_psum"], 1)

                def weigh(i):
                    t, b, h = item(i)
                    k = i // 8
                    wait("pT_ready", i + 1)
                    if i > 0 and i % 8 == 0:
                        wait("o_added", k)
                    col = 512 + 256 * (b + 1) + 128 + DH * (h // 4)
                    for j in range(t + 1):
                        last = pe.matmul(ps[4][:, DH * h:DH * h + DH], probT[:, i % 2, j * P:(j + 1) * P],
                                         pj[:, j, col:col + DH], start=j == 0, stop=j == t)
                    last.then_inc(sems["pv_done"], 1)

                wait("q_stacked", 1)
                wait("k_stacked", 1)
                scores(0)
                scores(1)
                for i in range(N_ITEMS):
                    turn(i)
                    if i + 2 < N_ITEMS:
                        scores(i + 2)
                    if item_step(i):
                        next(steps, None)
                    if i >= 1:
                        weigh(i - 1)
                weigh(N_ITEMS - 1)

                def mixed(t):
                    wait("o_written", t + 1)
                    wait("o_final", TILES.index(t) + 1)

                def mixer_bank_free(kc):
                    if kc == 0:
                        wait("o_added", NH)
                    elif kc < 4:
                        wait("og_ready", 8)
                        wait("s_ready", 9)

                turn_rows(1, mixed, mixer_bank_free)
                for u in (U_O0, U_O0 + 1):
                    dense(u, 1, (lambda j: wait("h_ready", 8 + j + 1)) if u == U_O0 else (lambda j: None))
                turn_rows(2, lambda t: wait("normed", 4 + t + 1), lambda kc: wait("x_added", kc + 1))
                for i in range(N_UP):
                    u = U_UP + i
                    dense(u, 2, (lambda j: wait("ffn_copied", 4 * (i - 2) + j + 1)) if i >= 2 else
                          (lambda j: wait("h_ready", 16 + j + 1)) if i == 0 else (lambda j: None))
                for k in range(FK):
                    p = 2 * U_DN + k // 2
                    a = p % 2
                    if k % 2 == 0:
                        wait("split", p + 1)
                    wait("g_split", k + 1)
                    cols = slice((k % 2) * 1024, (k % 2) * 1024 + 1024)
                    hi, lo = w_hi[:, a, cols], w_lo[:, a, cols]
                    for i in range(8):
                        if k == 0:
                            wait("ffn_copied", 40 + max(0, i - 3))
                        j, c = i // 2, slice((i % 2) * 512, (i % 2) * 512 + 512)
                        g = (g_hi[:, k % 2, P * j:P * j + P], g_lo[:, k % 2, P * j:P * j + P])
                        last = three(ps[i][:, :], g, (hi[:, c], lo[:, c]), k == 0, k == FK - 1)
                        if k == FK - 1 and i < 7:
                            last.then_inc(sems["down_done"], 1)
                    last.then_inc(sems["g_used" if k % 2 == 0 else "odd_used" if a else "even_used"], 1)


def kernel(**inputs):
    import numpy as np
    import concourse.bacc as bacc
    from concourse.bass_utils import run_bass_kernel_spmd

    names = ["x", "positions", "attn_norm", "w_in", "nsa_q_norm", "nsa_k_norm", "cmp_pe", "cmp_w1", "cmp_w2",
             "nsa_out_norm", "gdn_conv_w", "gdn_a_log", "gdn_dt_bias", "gdn_out_norm", "w_out", "ffn_norm", "w_up",
             "ffn_conv_w", "ffn_conv_b", "w_down"]
    nc = bacc.Bacc("TRN2", target_bir_lowering=False, num_devices=1)
    arrays = {n: np.ascontiguousarray(inputs[n]) for n in names}
    aps = [nc.dram_tensor(f"in_{n}", arrays[n].shape, mybir.dt.from_np(arrays[n].dtype), kind="ExternalInput").ap()
           for n in names]
    out = nc.dram_tensor("out", arrays["x"].shape, F32, kind="ExternalOutput").ap()
    trunk(nc, arrays["w_in"].shape[0], *aps, out)
    r = run_bass_kernel_spmd(nc, [{f"in_{n}": arrays[n] for n in names}], core_ids=[0])
    return r.results[0]["out"]
```
